# Optimizing a Trainium2 kernel written in Bass

```python
import math
import jax, jax.numpy as jnp
from jax import lax
import numpy as np

D_MODEL = 1024
BATCH = 1
SEQ = 256
DEPTH = 1

CONV_DIM = 1024
CONV_WIDTH = 3
DIFF_HEADS = 8
DIFF_HEAD_DIM = 64
DIFF_V_DIM = 2 * DIFF_HEAD_DIM
Q_BLOCK = 128
N_BUCKETS = 32
MAX_DISTANCE = 128
MEM_LEN = 256
CROSS_HEADS = 4
CROSS_HEAD_DIM = D_MODEL // CROSS_HEADS
PEER_HEADS = 8
N_KEYS = 128
N_EXPERTS = N_KEYS * N_KEYS
PEER_TOPK = 16
PEER_DK = 256
PEER_DK_HALF = PEER_DK // 2
PEER_CHUNK = 128

IN_SPLITS = [CONV_DIM, CONV_DIM, CONV_DIM,
             DIFF_HEADS * 2 * DIFF_HEAD_DIM,
             DIFF_HEADS * 2 * DIFF_HEAD_DIM,
             DIFF_HEADS * DIFF_V_DIM,
             D_MODEL, D_MODEL]
IN_COLS = sum(IN_SPLITS)


def rmsnorm(x, g, eps=1e-6):
    x32 = x.astype(jnp.float32)
    y = x32 * lax.rsqrt(jnp.mean(x32 * x32, axis=-1, keepdims=True) + eps)
    return (y * g.astype(jnp.float32)).astype(x.dtype)

def t5_bucket(dist):
    n = jnp.maximum(dist, 0)
    max_exact = N_BUCKETS // 2
    nf = jnp.maximum(n, 1).astype(jnp.float32)
    large = max_exact + (jnp.log(nf / max_exact) / math.log(MAX_DISTANCE / max_exact)
                         * (N_BUCKETS - max_exact)).astype(jnp.int32)
    large = jnp.minimum(large, N_BUCKETS - 1)
    return jnp.where(n < max_exact, n, large)

def short_conv_mixer(b_gate, c_gate, xc, conv_w, w_out):
    u = c_gate * xc
    rhs = conv_w.reshape(CONV_WIDTH, 1, CONV_DIM).astype(u.dtype)
    conv = lax.conv_general_dilated(u, rhs, window_strides=(1,), padding=[(CONV_WIDTH - 1, 0)],
                                    dimension_numbers=('NWC', 'WIO', 'NWC'),
                                    feature_group_count=CONV_DIM)
    return (b_gate * conv) @ w_out

def diff_attention(q, k, v, rel_bias, lam, lam_init, subln_g):
    b, s = q.shape[0], q.shape[1]
    nb = s // Q_BLOCK
    scale = DIFF_HEAD_DIM ** -0.5
    qb = q.reshape(b, nb, Q_BLOCK, DIFF_HEADS, 2, DIFF_HEAD_DIM).swapaxes(0, 1)
    kpos = jnp.arange(s, dtype=jnp.int32)

    def block(args):
        qi, blk = args
        qpos = blk * Q_BLOCK + jnp.arange(Q_BLOCK, dtype=jnp.int32)
        rel = qpos[:, None] - kpos[None, :]
        bias = jnp.transpose(rel_bias[t5_bucket(rel)], (2, 0, 1)).astype(jnp.float32)
        logits = jnp.einsum('bqhcd,bkhcd->bhcqk', qi, k).astype(jnp.float32) * scale
        logits = logits + bias[None, :, None]
        logits = jnp.where(rel[None, None, None] >= 0, logits, -1e30)
        p = jax.nn.softmax(logits, axis=-1)
        a = p[:, :, 0] - lam * p[:, :, 1]
        return jnp.einsum('bhqk,bkhe->bqhe', a.astype(v.dtype), v)

    out = lax.map(block, (qb, jnp.arange(nb, dtype=jnp.int32)))
    out = out.swapaxes(0, 1).reshape(b, s, DIFF_HEADS, DIFF_V_DIM)
    out = rmsnorm(out, subln_g, eps=1e-5) * (1.0 - lam_init)
    return out.reshape(b, s, DIFF_HEADS * DIFF_V_DIM)

def cross_attention(h, m, w_cq, w_ckv, w_co):
    b, s, _ = h.shape
    q = (h @ w_cq).reshape(b, s, CROSS_HEADS, CROSS_HEAD_DIM)
    kv = (m @ w_ckv).reshape(b, m.shape[1], 2, CROSS_HEADS, CROSS_HEAD_DIM)
    k, v = kv[:, :, 0], kv[:, :, 1]
    logits = jnp.einsum('bshd,bmhd->bhsm', q, k).astype(jnp.float32) * (CROSS_HEAD_DIM ** -0.5)
    p = jax.nn.softmax(logits, axis=-1).astype(v.dtype)
    o = jnp.einsum('bhsm,bmhd->bshd', p, v).reshape(b, s, CROSS_HEADS * CROSS_HEAD_DIM)
    return o @ w_co

def peer_ffn(h, w_pq, sub_keys, peer_u, peer_v):
    b, s, d = h.shape
    hf = h.reshape(b * s // PEER_CHUNK, PEER_CHUNK, d)

    def chunk(hc):
        q = (hc @ w_pq).reshape(PEER_CHUNK, PEER_HEADS, 2, PEER_DK_HALF)
        sc = jnp.einsum('thcd,chnd->thcn', q, sub_keys).astype(jnp.float32)
        vals, idx = lax.top_k(sc, PEER_TOPK)
        cand = vals[:, :, 0, :, None] + vals[:, :, 1, None, :]
        cand_idx = idx[:, :, 0, :, None] * N_KEYS + idx[:, :, 1, None, :]
        top_s, top_c = lax.top_k(cand.reshape(PEER_CHUNK, PEER_HEADS, PEER_TOPK * PEER_TOPK), PEER_TOPK)
        experts = jnp.take_along_axis(
            cand_idx.reshape(PEER_CHUNK, PEER_HEADS, PEER_TOPK * PEER_TOPK), top_c, axis=-1)
        g = jax.nn.softmax(top_s, axis=-1)
        ue = peer_u[experts]
        ve = peer_v[experts]
        act = jax.nn.gelu(jnp.einsum('td,thkd->thk', hc, ue).astype(jnp.float32), approximate=False)
        return jnp.einsum('thk,thkd->td', (g * act).astype(ve.dtype), ve)

    return lax.map(chunk, hf).reshape(b, s, d)

def first_inputs(seed: int = 0) -> dict:
    key = jax.random.key(seed)
    ks = jax.random.split(key, 32)
    f32 = jnp.float32
    D = D_MODEL

    def nrm(k, shape, scale):
        return jax.random.normal(k, shape, f32) * scale

    def gain(k, shape):
        return 1.0 + 0.02 * jax.random.normal(k, shape, f32)

    return {
        "x": nrm(ks[0], (BATCH, SEQ, D), 1.0),
        "mem": nrm(ks[1], (BATCH, MEM_LEN, D), 1.0),
        "norm_mix_g": gain(ks[2], (DEPTH, D)),
        "w_in": nrm(ks[3], (DEPTH, D, IN_COLS), D ** -0.5),
        "conv_w": nrm(ks[4], (DEPTH, CONV_WIDTH, CONV_DIM), CONV_WIDTH ** -0.5),
        "w_conv_out": nrm(ks[5], (DEPTH, CONV_DIM, D), CONV_DIM ** -0.5),
        "lambda_q1": nrm(ks[6], (DEPTH, DIFF_HEAD_DIM), 0.1),
        "lambda_k1": nrm(ks[7], (DEPTH, DIFF_HEAD_DIM), 0.1),
        "lambda_q2": nrm(ks[8], (DEPTH, DIFF_HEAD_DIM), 0.1),
        "lambda_k2": nrm(ks[9], (DEPTH, DIFF_HEAD_DIM), 0.1),
        "subln_g": gain(ks[10], (DEPTH, DIFF_V_DIM)),
        "w_attn_out": nrm(ks[11], (DEPTH, DIFF_HEADS * DIFF_V_DIM, D), (DIFF_HEADS * DIFF_V_DIM) ** -0.5),
        "w_mix_out": nrm(ks[12], (DEPTH, D, D), D ** -0.5),
        "rel_bias": nrm(ks[13], (N_BUCKETS, DIFF_HEADS), 0.5),
        "norm_cross_g": gain(ks[14], (DEPTH, D)),
        "norm_mem_g": gain(ks[15], (DEPTH, D)),
        "w_cq": nrm(ks[16], (DEPTH, D, CROSS_HEADS * CROSS_HEAD_DIM), D ** -0.5),
        "w_ckv": nrm(ks[17], (DEPTH, D, 2 * CROSS_HEADS * CROSS_HEAD_DIM), D ** -0.5),
        "w_co": nrm(ks[18], (DEPTH, CROSS_HEADS * CROSS_HEAD_DIM, D), (CROSS_HEADS * CROSS_HEAD_DIM) ** -0.5),
        "norm_ffn_g": gain(ks[19], (DEPTH, D)),
        "w_pq": nrm(ks[20], (DEPTH, D, PEER_HEADS * PEER_DK), D ** -0.5),
        "sub_keys": nrm(ks[21], (DEPTH, 2, PEER_HEADS, N_KEYS, PEER_DK_HALF), PEER_DK_HALF ** -0.5),
        "peer_u": nrm(ks[22], (DEPTH, N_EXPERTS, D), D ** -0.5),
        "peer_v": nrm(ks[23], (DEPTH, N_EXPERTS, D), D ** -0.5),
        "final_g": gain(ks[24], (D,)),
    }

def first_block(x, mem, norm_mix_g, w_in, conv_w, w_conv_out, lambda_q1, lambda_k1, lambda_q2, lambda_k2,
              subln_g, w_attn_out, w_mix_out, rel_bias, norm_cross_g, norm_mem_g, w_cq, w_ckv, w_co,
              norm_ffn_g, w_pq, sub_keys, peer_u, peer_v, final_g):
    b, s, _ = x.shape
    split_points = list(np.cumsum(IN_SPLITS)[:-1])
    for l in range(DEPTH):
        h = rmsnorm(x, norm_mix_g[l])
        proj = h @ w_in[l]
        cb, cc, cx, q, k, v, gc, ga = jnp.split(proj, split_points, axis=-1)
        y_conv = short_conv_mixer(cb, cc, cx, conv_w[l], w_conv_out[l])
        lam_init = 0.8 - 0.6 * math.exp(-0.3 * l)
        lam = (jnp.exp(jnp.sum(lambda_q1[l] * lambda_k1[l]).astype(jnp.float32))
               - jnp.exp(jnp.sum(lambda_q2[l] * lambda_k2[l]).astype(jnp.float32)) + lam_init)
        q = q.reshape(b, s, DIFF_HEADS, 2, DIFF_HEAD_DIM)
        k = k.reshape(b, s, DIFF_HEADS, 2, DIFF_HEAD_DIM)
        v = v.reshape(b, s, DIFF_HEADS, DIFF_V_DIM)
        y_attn = diff_attention(q, k, v, rel_bias, lam, lam_init, subln_g[l]) @ w_attn_out[l]
        merged = jax.nn.sigmoid(gc) * y_conv + jax.nn.sigmoid(ga) * y_attn
        x = x + merged @ w_mix_out[l]
        hc = rmsnorm(x, norm_cross_g[l])
        m = rmsnorm(mem, norm_mem_g[l])
        x = x + cross_attention(hc, m, w_cq[l], w_ckv[l], w_co[l])
        hf = rmsnorm(x, norm_ffn_g[l])
        x = x + peer_ffn(hf, w_pq[l], sub_keys[l], peer_u[l], peer_v[l])
    return rmsnorm(x, final_g)


DEPTH_2 = 2

N_A = DEPTH_2 // 2
N_B = DEPTH_2 - N_A
HEAD_DIM = 64
MIX_WIDTH = D_MODEL
MEM_HEADS = 4
MEM_WIDTH = MEM_HEADS * HEAD_DIM
MAIN_WIDTH = MIX_WIDTH - MEM_WIDTH
POOL_WINDOWS = (2, 4, 8, 16)
POOL_GROUPS = len(POOL_WINDOWS)
POOL_GROUP_DIM = MAIN_WIDTH // POOL_GROUPS
SWA_Q_HEADS = MAIN_WIDTH // HEAD_DIM
SWA_KV_HEADS = 4
SWA_GROUP = SWA_Q_HEADS // SWA_KV_HEADS
KV_WIDTH = 2 * SWA_KV_HEADS * HEAD_DIM
MEM_KV_WIDTH = 2 * MEM_WIDTH
WINDOW = 128
BLOCK = 128
D_FF = 4 * D_MODEL
EPS = 1e-6


def rmsnorm_2(x, g):
    xf = x.astype(jnp.float32)
    y = xf * lax.rsqrt(jnp.mean(xf * xf, axis=-1, keepdims=True) + EPS)
    return (y * g.astype(jnp.float32)).astype(x.dtype)

def alibi_slopes(n):
    return jnp.exp2(-8.0 * jnp.arange(1, n + 1, dtype=jnp.float32) / n)

def pool_mixer(u, pool_w, pool_scale):
    B, S, _ = u.shape
    uf = u.astype(jnp.float32).reshape(B, S, POOL_GROUPS, POOL_GROUP_DIM)
    csum = jnp.concatenate([jnp.zeros((B, 1, POOL_GROUPS, POOL_GROUP_DIM), jnp.float32),
                            jnp.cumsum(uf, axis=1)], axis=1)
    win = jnp.array(POOL_WINDOWS, jnp.int32)
    t = jnp.arange(S, dtype=jnp.int32)[:, None]
    lo = jnp.maximum(t + 1 - win[None, :], 0)
    cnt = jnp.minimum(t + 1, win[None, :]).astype(jnp.float32)
    window_sum = csum[:, 1:] - csum[:, lo, jnp.arange(POOL_GROUPS)[None, :]]
    d = (window_sum / cnt[None, :, :, None] - uf).astype(u.dtype)
    mixed = jnp.einsum('bsgc,gcd->bsgd', d, pool_w)
    return mixed.reshape(B, S, MAIN_WIDTH) * pool_scale

def swa_sink_attention(q, k, v, sinks):
    B, S = q.shape[0], q.shape[1]
    nb = S // BLOCK
    qb = q.reshape(B, nb, BLOCK, SWA_KV_HEADS, SWA_GROUP, HEAD_DIM)

    def with_prev(a):
        ab = a.reshape(B, nb, BLOCK, SWA_KV_HEADS, HEAD_DIM)
        prev = jnp.pad(ab[:, :-1], ((0, 0), (1, 0), (0, 0), (0, 0), (0, 0)))
        return jnp.concatenate([prev, ab], axis=2)

    kb, vb = with_prev(k), with_prev(v)
    s = jnp.einsum('bnqkgd,bnpkd->bnkgqp', qb, kb).astype(jnp.float32) * (HEAD_DIM ** -0.5)
    blk = jnp.arange(nb, dtype=jnp.int32)[:, None] * BLOCK
    qpos = blk + jnp.arange(BLOCK, dtype=jnp.int32)[None, :]
    kpos = blk - BLOCK + jnp.arange(2 * BLOCK, dtype=jnp.int32)[None, :]
    dist = qpos[:, :, None] - kpos[:, None, :]
    valid = (dist >= 0) & (dist < WINDOW) & (kpos[:, None, :] >= 0)
    slopes = alibi_slopes(SWA_Q_HEADS).reshape(SWA_KV_HEADS, SWA_GROUP)
    s = s - slopes[None, None, :, :, None, None] * dist.astype(jnp.float32)[None, :, None, None]
    s = jnp.where(valid[None, :, None, None], s, jnp.finfo(jnp.float32).min)
    sink = sinks.astype(jnp.float32).reshape(SWA_KV_HEADS, SWA_GROUP)[None, None, :, :, None, None]
    m = jnp.maximum(jnp.max(s, axis=-1, keepdims=True), sink)
    e = jnp.exp(s - m)
    p = e / (jnp.sum(e, axis=-1, keepdims=True) + jnp.exp(sink - m))
    o = jnp.einsum('bnkgqp,bnpkd->bnqkgd', p.astype(vb.dtype), vb)
    return o.reshape(B, S, SWA_Q_HEADS * HEAD_DIM)

def memory_attention(q, mk, mv):
    s = jnp.einsum('bshd,bmhd->bhsm', q, mk).astype(jnp.float32) * (HEAD_DIM ** -0.5)
    p = jax.nn.softmax(s, axis=-1)
    o = jnp.einsum('bhsm,bmhd->bshd', p.astype(mv.dtype), mv)
    return o.reshape(q.shape[0], q.shape[1], MEM_WIDTH)

def sq_relu_mlp(x, w_up, w_down):
    h = jax.nn.relu(x @ w_up)
    return (h * h) @ w_down

def second_inputs(seed: int = 0) -> dict:
    key = jax.random.key(seed)
    ks = jax.random.split(key, 20)
    f32 = jnp.float32

    def nrm(k, shape, scale):
        return jax.random.normal(k, shape, f32) * scale

    def gain(k, shape):
        return 1.0 + 0.02 * jax.random.normal(k, shape, f32)

    return {
        "x": nrm(ks[0], (BATCH, SEQ, D_MODEL), 1.0),
        "mem": nrm(ks[1], (BATCH, MEM_LEN, D_MODEL), 1.0),
        "norm_mix": gain(ks[2], (DEPTH_2, D_MODEL)),
        "w_in": nrm(ks[3], (DEPTH_2, D_MODEL, MIX_WIDTH), D_MODEL ** -0.5),
        "pool_w": nrm(ks[4], (N_A, POOL_GROUPS, POOL_GROUP_DIM, POOL_GROUP_DIM), POOL_GROUP_DIM ** -0.5),
        "pool_scale": gain(ks[5], (N_A, MAIN_WIDTH)),
        "kv_norm": gain(ks[6], (D_MODEL,)),
        "w_kv": nrm(ks[7], (D_MODEL, KV_WIDTH), D_MODEL ** -0.5),
        "k_norm": gain(ks[8], (HEAD_DIM,)),
        "q_norm": gain(ks[9], (N_B, HEAD_DIM)),
        "sinks": nrm(ks[10], (N_B, SWA_Q_HEADS), 0.5),
        "mem_norm": gain(ks[11], (DEPTH_2, D_MODEL)),
        "w_mem_kv": nrm(ks[12], (DEPTH_2, D_MODEL, MEM_KV_WIDTH), D_MODEL ** -0.5),
        "mem_q_norm": gain(ks[13], (DEPTH_2, HEAD_DIM)),
        "mem_k_norm": gain(ks[14], (DEPTH_2, HEAD_DIM)),
        "w_out": nrm(ks[15], (DEPTH_2, MIX_WIDTH, D_MODEL), MIX_WIDTH ** -0.5),
        "norm_mlp": gain(ks[16], (DEPTH_2, D_MODEL)),
        "w_up": nrm(ks[17], (DEPTH_2, D_MODEL, D_FF), D_MODEL ** -0.5),
        "w_down": nrm(ks[18], (DEPTH_2, D_FF, D_MODEL), D_FF ** -0.5),
    }

def second_block(x, mem, norm_mix, w_in, pool_w, pool_scale, kv_norm, w_kv, k_norm, q_norm, sinks,
              mem_norm, w_mem_kv, mem_q_norm, mem_k_norm, w_out, norm_mlp, w_up, w_down):
    B, S, _ = x.shape
    h = x
    k_shared = None
    v_shared = None
    for l in range(DEPTH_2):
        if l == N_A:
            kv = rmsnorm_2(h, kv_norm) @ w_kv
            k_shared = rmsnorm_2(kv[..., :KV_WIDTH // 2].reshape(B, S, SWA_KV_HEADS, HEAD_DIM), k_norm)
            v_shared = kv[..., KV_WIDTH // 2:].reshape(B, S, SWA_KV_HEADS, HEAD_DIM)

        proj = rmsnorm_2(h, norm_mix[l]) @ w_in[l]
        main, mq = proj[..., :MAIN_WIDTH], proj[..., MAIN_WIDTH:]
        if l < N_A:
            main_out = pool_mixer(main, pool_w[l], pool_scale[l])
        else:
            j = l - N_A
            q = rmsnorm_2(main.reshape(B, S, SWA_Q_HEADS, HEAD_DIM), q_norm[j])
            main_out = swa_sink_attention(q, k_shared, v_shared, sinks[j])

        mkv = rmsnorm_2(mem, mem_norm[l]) @ w_mem_kv[l]
        mk = rmsnorm_2(mkv[..., :MEM_WIDTH].reshape(B, MEM_LEN, MEM_HEADS, HEAD_DIM), mem_k_norm[l])
        mv = mkv[..., MEM_WIDTH:].reshape(B, MEM_LEN, MEM_HEADS, HEAD_DIM)
        mqh = rmsnorm_2(mq.reshape(B, S, MEM_HEADS, HEAD_DIM), mem_q_norm[l])
        mem_out = memory_attention(mqh, mk, mv)

        h = h + jnp.concatenate([main_out, mem_out], axis=-1) @ w_out[l]
        h = h + sq_relu_mlp(rmsnorm_2(h, norm_mlp[l]), w_up[l], w_down[l])
    return h


def setup_inputs(seed=0):
    out = dict(first_inputs(seed))
    for name, value in second_inputs(seed + 1).items():
        if name != "x":
            out[name + "_2"] = value
    return out


def reference(
    x, mem, norm_mix_g, w_in, conv_w, w_conv_out, lambda_q1, lambda_k1, lambda_q2, lambda_k2,
    subln_g, w_attn_out, w_mix_out, rel_bias, norm_cross_g, norm_mem_g, w_cq, w_ckv, w_co,
    norm_ffn_g, w_pq, sub_keys, peer_u, peer_v, final_g, mem_2, norm_mix_2, w_in_2, pool_w_2,
    pool_scale_2, kv_norm_2, w_kv_2, k_norm_2, q_norm_2, sinks_2, mem_norm_2, w_mem_kv_2,
    mem_q_norm_2, mem_k_norm_2, w_out_2, norm_mlp_2, w_up_2, w_down_2,
):
    x = first_block(
        x, mem, norm_mix_g, w_in, conv_w, w_conv_out, lambda_q1, lambda_k1, lambda_q2,
        lambda_k2, subln_g, w_attn_out, w_mix_out, rel_bias, norm_cross_g, norm_mem_g, w_cq,
        w_ckv, w_co, norm_ffn_g, w_pq, sub_keys, peer_u, peer_v, final_g,
    )
    return second_block(
        x, mem_2, norm_mix_2, w_in_2, pool_w_2, pool_scale_2, kv_norm_2, w_kv_2, k_norm_2,
        q_norm_2, sinks_2, mem_norm_2, w_mem_kv_2, mem_q_norm_2, mem_k_norm_2, w_out_2,
        norm_mlp_2, w_up_2, w_down_2,
    )


_drawn_inputs = setup_inputs


def setup_inputs(seed=0):
    import zlib

    import numpy as np

    out = dict(_drawn_inputs(seed))
    spreads = {}
    factors = {'lambda_q1': 5.273,
     'lambda_k2': 8.0,
     'subln_g': 6.29,
     'norm_cross_g': 8.0,
     'norm_mem_g': 8.0,
     'norm_ffn_g': 8.0,
     'w_pq': 3.941,
     'sub_keys': 3.964,
     'peer_u': 4.354,
     'peer_v': 3.938,
     'norm_mix_2': 4.254,
     'pool_scale_2': 4.228,
     'kv_norm_2': 8.0,
     'k_norm_2': 8.0,
     'q_norm_2': 23.104,
     'mem_norm_2': 8.0,
     'mem_q_norm_2': 8.0,
     'mem_k_norm_2': 8.0,
     'sinks_2': 64.0,
     'norm_mlp_2': 5.459}
    for name, (base, spread) in spreads.items():
        noise = np.random.default_rng([zlib.crc32(name.encode()), seed]).standard_normal(out[name].shape)
        drawn = base * np.exp(spread * noise) if base else spread * noise
        out[name] = __import__('jax').numpy.asarray(drawn.astype(out[name].dtype))
    for name, factor in factors.items():
        out[name] = (out[name] * factor).astype(out[name].dtype)
    return out
```

```python
import math
from contextlib import ExitStack

import numpy as np

import concourse.bass as bass
from concourse import mybir

F32 = mybir.dt.float32
I32 = mybir.dt.int32
U32 = mybir.dt.uint32
ALU = mybir.AluOpType
ACT = mybir.ActivationFunctionType
AX = mybir.AxisListType

P = 128
D = 1024
S = 256
KC = D // P
TB = S // P
CW = 512
HEADS = 8
HD = 64
CROSS_HEADS = 4
BUCKETS = 32
MAX_DISTANCE = 128
PH = 8
TOPK = 16
NKEYS = 128
NEXP = NKEYS * NKEYS
PAIRS = PH * TOPK
SWA_HEADS = 12
SWA_TILES = SWA_HEADS * HD // P
MEM_HEADS = 4
POOL_WINDOWS = (2, 4, 8, 16)
POOL_GROUP = SWA_HEADS * HD // len(POOL_WINDOWS)
FF_TILES = 4 * D // P
LAM_INIT = 0.8 - 0.6 * math.exp(0.0)
MASKED = -1e30
SLOTS = 4
GSLOTS = 8
SWA_ORDER = [h for j in range(SWA_TILES) for h in (6 * (j // 3) + j % 3, 6 * (j // 3) + 3 + j % 3)]
POOL_BLOCKS = [(0, 0), (1, 0), (0, 1), (1, 1), (2, 1), (1, 2), (2, 2)]

VEC = {}
for _name, _n in [("mix", 8), ("cross", 8), ("mem", 8), ("ffn", 8), ("mixa", 8), ("mixb", 8), ("mlpa", 8),
                  ("mlpb", 8), ("kv", 8), ("mem2a", 8), ("mem2b", 8), ("conv", 24), ("subln", 1),
                  ("pool", 6), ("kn", 1), ("qn", 1), ("mqna", 1), ("mqnb", 1), ("mkna", 1), ("mknb", 1)]:
    VEC[_name] = (sum(n for _, n in VEC.values()), _n)
NVEC = sum(n for _, n in VEC.values())
NBC = 4 * HD + SWA_HEADS

CHUNKS = (["q", "q", "k", "k", "v", "v", "cx", "cx", "cc", "cc", "cb", "cb", "gc", "gc", "ga", "ga"]
          + ["ck", "ck", "cv", "cv", "mkva", "mkvb", "cout", "cout", "aout", "aout", "mixo", "mixo"]
          + ["cq", "cq", "co", "co", "pq", "pq", "pq", "pq"]
          + ["ina", "ina", "outa", "outa"] + ["upa"] * 8 + ["downa"] * 8
          + ["kvb", "inb", "inb", "outb", "outb"] + ["upb"] * 8 + ["downb"] * 8)
NCHUNK = len(CHUNKS)


def plan():
    lin, last, misc = {}, {}, {}
    half = 0
    seen = {}
    for c in CHUNKS:
        i = seen.get(c, 0)
        seen[c] = i + 1
        for j in range(2):
            half += 1
            key = (c, 2 * (i // 4) + j) if c.startswith("down") else (c, 2 * i + j)
            lin.setdefault(key, len(lin))
            last[key] = half

    def m(*name):
        misc[name] = len(misc)

    def norm(n):
        for tb in range(TB):
            for h in range(2):
                m("xT", n, tb, h)

    def attention(kind, items, group, lag):
        for i in range(min(lag, items)):
            for g in range(group):
                m("S", kind, i * group + g)
        for i in range(items):
            if i + lag < items:
                for g in range(group):
                    m("S", kind, (i + lag) * group + g)
            m("T", kind, i)
            m("O", kind, i)

    m("bias")
    norm("mix")
    attention("diff", HEADS, 2, 1)
    norm("mem")
    for j in range(4):
        m("sub", j)
    norm("mem2")
    for l in "ab":
        m("mkr", l)
    norm("cross")
    attention("cross", CROSS_HEADS, 1, 2)
    norm("ffn")
    for tb in range(TB):
        for j in range(4):
            m("sc", tb, j)
    norm("mixa")
    m("mqr", "a")
    for g in range(2):
        for j in range(3):
            m("pool", g, j)
    attention("mema", MEM_HEADS, 1, 2)
    norm("mlpa")
    norm("mixb")
    m("kr")
    for j in range(4):
        m("qr", j)
    attention("swa", SWA_HEADS, 1, 2)
    attention("memb", MEM_HEADS, 1, 2)
    norm("mlpb")
    return lin, last, misc


def build(nc, x_in, mem_in, mem2_in, wstream, experts, vecs_in, bc_in, final_g, rel_in, keys_in, pool_in,
          consts_in, onehot_in, cnt_in, scratch, out):
    LIN, LAST, MISC = plan()
    ctx = ExitStack()
    with ctx:
        def sb(name, shape, dt=F32):
            return ctx.enter_context(nc.sbuf_tensor(name, shape, dt))

        sems = {}

        def sem(name):
            sems[name] = ctx.enter_context(nc.semaphore(name))
            return sems[name]

        wring = sb("wring", [P, SLOTS, KC, CW])
        x = sb("x", [P, TB, D])
        xn = sb("xn", [P, TB, D])
        act_t = sb("act_t", [P, KC, S])
        act2_t = sb("act2_t", [P, KC, S])
        memk = sb("memk", [P, 2, 2, S])
        memv = sb("memv", [P, 2, TB, S])
        vecs = sb("vecs", [P, NVEC])
        bc = sb("bc", [P, NBC])
        consts = sb("consts", [P, 3 * P + TOPK])
        stat = sb("stat", [P, 60])
        arena = sb("arena", [P, 25600])

        ident = consts[:, 0:P]
        mean128 = consts[:, P:2 * P]
        mean64 = consts[:, 2 * P:3 * P]
        iota16 = consts[:, 3 * P:3 * P + TOPK]

        def part(at, *shape):
            n = int(np.prod(shape))
            v = arena[:, at:at + n]
            if len(shape) == 2:
                v = v.rearrange("p (a b) -> p a b", a=shape[0])
            if len(shape) == 3:
                v = v.rearrange("p (a b c) -> p a b c", a=shape[0], b=shape[1])
            if len(shape) == 4:
                v = v.rearrange("p (a b c d) -> p a b c d", a=shape[0], b=shape[1], c=shape[2])
            return v

        prob = part(22528, 4, TB, S)
        prob_t = part(24576, 2, 2, S)
        q_half = part(0, 2, HEADS, S)
        k_diff = part(4096, HEADS, S)
        v_diff = part(6144, TB, D)
        u_conv = part(8192, KC, S)
        conv = part(10240, KC, S)
        gate_c = part(12288, KC, S)
        gate_a = part(14336, KC, S)
        bias = part(16384, HEADS, TB, S)
        o_diff = part(20480, KC, S)
        rel_sb = part(20480, 512)[0:BUCKETS + 1, 0:8]
        onehot = part(20992, 512)[0:BUCKETS + 1, :]
        bias_row = part(21504, 512)[0:8, :]
        k_cross = part(0, KC, S)
        v_cross = part(2048, TB, D)
        q_cross = part(4096, KC, S)
        o_cross = part(6144, KC, S)
        sq = part(16384, KC, S)
        junk = part(18432, KC, S)
        merged = part(10240, KC, S)
        q_peer = part(0, 2 * PH, S)
        keys = part(4096, 2 * PH, NKEYS)
        rows = part(0, GSLOTS, 2 * D)
        score = part(16384, TB, 2 * PH, NKEYS)
        u_pool = part(0, SWA_TILES, S)
        win = part(2048, 2, SWA_TILES, S)
        cnt = part(5120, SWA_TILES, S)
        pool_w = part(6656, len(POOL_BLOCKS) * 2 - 0, P)
        mq_half = part(8448, 2, 2, S)
        cat_t = part(9472, KC, S)
        sq2 = part(11520, KC, S)
        raw2 = part(13568, KC, S)
        q_swa = part(0, 2, KC, S)
        k_swa = part(4096, 2, S)
        v_swa = part(4608, TB, S)
        alibi = part(5120, TB, S)
        hidden = part(0, FF_TILES, S)
        gfin = part(16384, D)

        half_score = part(20480, 2, NKEYS)
        half_vals = part(20736, 2, TOPK)
        half_idx = part(20768, 2, TOPK).bitcast(U32)
        half_idxf = part(20800, 2, TOPK)
        cand = part(20832, TOPK, TOPK)
        top_vals = part(21088, TOPK)
        top_pos = part(21104, TOPK).bitcast(U32)
        top_half = part(21120, 2, TOPK).bitcast(U32)
        top_halff = part(21152, 2, TOPK)
        pick = part(21184, TOPK, TOPK)
        found = part(21440, 2, TOPK)
        top_less = part(21472, TOPK)
        top_e = part(21488, TOPK)
        hsum = part(21504, 1)
        hinv = part(21505, 1)
        diag = xn[:, 0, :].rearrange("p (s n) -> p s n", s=GSLOTS)
        expert = xn[:, 1, 0:256].rearrange("p (t n) -> p t n", t=TB).bitcast(I32)
        weight = xn[:, 1, 256:512].rearrange("p (t n) -> p t n", t=TB)
        zeros = xn[:, 1, 640:768]
        stage = xn[:, 1, 768:784].rearrange("p (t n) -> p t n", t=2).bitcast(I32)
        dots = xn[:, 1, 784:792]
        gact = xn[:, 1, 792:800]
        wact = xn[:, 1, 800:808]
        nmax = sb("nmax", [P, 4, 2])
        ssum = sb("ssum", [P, 4, 2])
        rsum = sb("rsum", [P, 4, 2])
        esink = sb("esink", [P, 4, 2])
        small = sb("small", [P, 16])

        bank_pairs = [ctx.enter_context(nc.psum_tensor(f"banks{i}", [P, 2, 512], F32)) for i in range(4)]
        banks = [bank_pairs[i // 2][:, i % 2, :] for i in range(8)]

        chunk_in = [sem(f"chunk_in{i}") for i in range(SLOTS)]
        half_done = sem("half_done")
        lin_free = [sem(f"lin_free{i}") for i in range(4)]
        misc_full = sem("misc_full")
        misc_free = [sem(f"misc_free{i}") for i in range(4)]
        x_in_s = sem("x_in_s")
        mem_in_s = sem("mem_in_s")
        mem2_in_s = sem("mem2_in_s")
        const_in = sem("const_in")
        row_in = sem("row_in")
        bias_out = sem("bias_out")
        bias_in = sem("bias_in")
        keys_in_s = sem("keys_in_s")
        gfin_in = sem("gfin_in")
        pool_in_s = sem("pool_in_s")
        alibi_in = sem("alibi_in")
        out_s = sem("out_s")
        bias_row_s = sem("bias_row_s")
        dve_chain = sem("dve_chain")
        act_chain = sem("act_chain")
        pool_chain = sem("pool_chain")
        squares = sem("squares")
        mean_sq = sem("mean_sq")
        rstd_s = sem("rstd_s")
        xn_ready = sem("xn_ready")
        max_ready = sem("max_ready")
        exp_ready = sem("exp_ready")
        p_ready = sem("p_ready")
        zero_ready = sem("zero_ready")
        lam_sums = sem("lam_sums")
        lam_exps = sem("lam_exps")
        gate_exp = sem("gate_exp")
        sub_sq = sem("sub_sq")
        sub_root = sem("sub_root")
        head_sq = sem("head_sq")
        head_ms = sem("head_ms")
        head_root = sem("head_root")
        ready = sem("ready")
        top_chain = sem("top_chain")
        top_passed = sem("top_passed")
        top_exp_in = sem("top_exp_in")
        top_exp = sem("top_exp")
        experts_ready = sem("experts_ready")
        gathered = [sem(f"gathered{i}") for i in range(GSLOTS)]
        staged = sem("staged")
        issued = sem("issued")
        hidden_ready = sem("hidden_ready")
        peer_zero = sem("peer_zero")
        hf_ready = sem("hf_ready")
        dot_ready = sem("dot_ready")
        gelu_ready = sem("gelu_ready")
        wact_ready = sem("wact_ready")
        diag_ready = sem("diag_ready")
        row_free = sem("row_free")
        acc_ready = sem("acc_ready")
        acc_used = sem("acc_used")

        count = {}

        def chain(eng, ins, s):
            count[id(s)] = count.get(id(s), 0) + 1
            ins.then_inc(s, 1)
            eng.wait_ge(s, count[id(s)])

        token_rows = bank_pairs[1], bank_pairs[2]
        row_sums = bank_pairs[0], bank_pairs[3]

        def lin_bank(key):
            return banks[LIN[key] % 4]

        def misc_bank(key):
            return banks[4 + MISC[key] % 4]

        def wait_lin(eng, key):
            eng.wait_ge(half_done, LAST[key])

        def wait_misc(eng, key):
            eng.wait_ge(misc_full, MISC[key] + 1)

        def empty_lin(ins, key):
            ins.then_inc(lin_free[LIN[key] % 4], 1)

        def empty_misc(ins, key):
            ins.then_inc(misc_free[MISC[key] % 4], 1)

        def lin_emptied(eng, key):
            eng.wait_ge(lin_free[LIN[key] % 4], LIN[key] // 4 + 1)

        def misc_emptied(eng, key):
            eng.wait_ge(misc_free[MISC[key] % 4], MISC[key] // 4 + 1)

        def gain(name):
            a, n = VEC[name]
            return vecs[:, a:a + n]

        NORMS = ["mix", "mem", "mem2", "cross", "ffn", "final", "mixa", "mlpa", "mixb", "mlpb"]

        def stats(n):
            a = 6 * NORMS.index(n)
            return stat[:, a:a + 2], stat[:, a + 2:a + 4], stat[:, a + 4:a + 6]

        UNIT0, ITEM0 = {}, {}
        n_units = n_items = 0
        for kind, items, group in (("diff", HEADS, 2), ("cross", CROSS_HEADS, 1), ("mema", MEM_HEADS, 1),
                                   ("swa", SWA_HEADS, 1), ("memb", MEM_HEADS, 1)):
            UNIT0[kind], ITEM0[kind] = n_units, n_items
            n_units += items * group
            n_items += items

        POINTS = ["zeros", "o_diff", "kmem_a", "kmem_b", "merged", "h", "d_pool", "mq", "k_swa", "q_swa"]

        def at_point(ins, name):
            assert POINTS[count.setdefault("point", 0)] == name, name
            count["point"] += 1
            ins.then_inc(ready, 1)

        def point(eng, name):
            eng.wait_ge(ready, POINTS.index(name) + 1)

        block = ctx.enter_context(nc.Block())

        @block.sync
        def _(sp):
            def chunk(c, slot):
                sp.dma_start(wring[:, slot, :, :], wstream[c].rearrange("p (a b) -> p a b", a=KC))\
                  .then_inc(chunk_in[slot], 16)

            sp.dma_start(x[:, :, :], x_in.rearrange("(t p) d -> p t d", p=P)).then_inc(x_in_s, 16)
            for c in range(SLOTS):
                chunk(c, c)
            misc_emptied(sp, ("bias",))
            head = P * (2 * S + 1)
            sp.dma_start(bass.AP(scratch.tensor, 0, [[head, HEADS], [2 * S + 1, P], [1, 2 * S]]),
                         bias_row.unsqueeze(1).broadcast_to([HEADS, P, 2 * S])).then_inc(bias_out, 16)
            sp.wait_ge(bias_out, 16)
            for qb in range(TB):
                sp.dma_start(bias[:, :, qb, :], bass.AP(scratch.tensor, S - 1 - P * qb,
                                                        [[2 * S, P], [head, HEADS], [1, S]])).then_inc(bias_in, 16)
            with sp.Fori(1, NCHUNK // SLOTS) as i:
                for slot in range(SLOTS):
                    sp.wait_ge(half_done, i * (2 * SLOTS) + 2 * (slot + 1 - SLOTS))
                    sp.dma_start(wring[:, slot, :, :],
                                 wstream[bass.ds(i * SLOTS + slot, 1)].rearrange("o p (a b) -> p (o a) b", a=KC))\
                      .then_inc(chunk_in[slot], 16)
            for c in range(NCHUNK - NCHUNK % SLOTS, NCHUNK):
                sp.wait_ge(half_done, 2 * (c + 1 - SLOTS))
                chunk(c, c % SLOTS)
            for tb in range(TB):
                for n in range(2):
                    lin_emptied(sp, ("downb", 2 * n + tb))
            sp.dma_start(out.rearrange("(t p) d -> p t d", p=P), x[:, :, :]).then_inc(out_s, 16)
            sp.wait_ge(out_s, 16)

        @block.gpsimd
        def _(pool):
            pool.memset(small[:, 14:16], -0.5).then_inc(pool_chain, 1)
            pool.wait_ge(pool_chain, 1)

            def rstd(n):
                _, ms, rs = stats(n)
                pool.wait_ge(mean_sq, NORMS.index(n) + 1)
                pool.tensor_tensor(rs, ms, small[:, 14:16], ALU.pow).then_inc(rstd_s, 1)

            for n in ("mix", "mem", "mem2", "cross", "ffn"):
                rstd(n)
            wait_misc(pool, ("sc", TB - 1, 3))
            for tb in range(TB):
                with pool.Fori(0, PH) as h:
                    pool.wait_ge(experts_ready, h + (tb * PH + 1))
                    for half in range(2):
                        turn = h * 2 + (half + tb * (PAIRS // GSLOTS))
                        pool.tensor_copy(stage[:, half, :],
                                         expert[:, tb, bass.ds(h * TOPK + half * GSLOTS, GSLOTS)])\
                            .then_inc(staged, 1)
                        pool.wait_ge(staged, turn + 1)
                        pool.sem_inc(issued, 1)
                        for s in range(GSLOTS):
                            pool.wait_ge(row_free, turn * GSLOTS + (s + 1))
                            pool.sem_inc(issued, 1)
                            pool.indirect_dma_start(
                                rows[:, s, :], None, experts,
                                bass.IndirectOffsetOnAxis(ap=stage[:, half, s:s + 1], axis=0))\
                                .then_inc(gathered[s], 16)
            for n in ("final", "mixa", "mlpa", "mixb", "mlpb"):
                rstd(n)

        @block.scalar
        def _(act):
            act.dma_start(consts[:, :], consts_in[:, 0:3 * P + TOPK]).then_inc(const_in, 16)
            act.dma_start(vecs[:, :], vecs_in).then_inc(const_in, 16)
            act.dma_start(bc[:, :], bass.AP(bc_in.tensor, 0, [[0, P], [1, NBC]])).then_inc(const_in, 16)
            act.dma_start(rel_sb, rel_in).then_inc(row_in, 16)
            act.dma_start(onehot, onehot_in).then_inc(row_in, 16)

            def sum_squares(n, src):
                ss = stats(n)[0]
                for tb in range(TB):
                    act.activation(xn[:, tb, :], src[:, tb, :], ACT.Square, accum_out=ss[:, tb:tb + 1])\
                       .then_inc(squares, 1)

            def x_updated(weight):
                for j in range(4):
                    lin_emptied(act, (weight, j))

            def xn_free(n):
                wait_misc(act, ("xT", n, 1, 1))

            def exps(kind, u):
                g = UNIT0[kind] + u
                r = g % 4
                act.wait_ge(max_ready, g + 1)
                in_psum = kind in ("cross", "mema", "memb")
                src = misc_bank(("S", kind, u)).rearrange("p (a b) -> p a b", a=TB) if in_psum \
                    else prob[:, r]
                if kind == "swa":
                    h = SWA_ORDER[u]
                    sink = bc[:, 4 * HD + h:4 * HD + h + 1]
                    chain(act, act.activation(esink[:, r, :], nmax[:, r, :], ACT.Exp, bias=sink), act_chain)
                for qb in range(TB):
                    e = act.activation(prob[:, r, qb, :], src[:, qb, :], ACT.Exp,
                                       bias=nmax[:, r, qb:qb + 1], accum_out=ssum[:, r, qb:qb + 1])
                    if in_psum and qb == TB - 1:
                        empty_misc(e, ("S", kind, u))
                    else:
                        e.then_inc(exp_ready, 1)

            def turned(kind, i):
                wait_misc(act, ("T", kind, i))
                if i >= 2:
                    wait_misc(act, ("O", kind, i - 2))
                e = act.activation(prob_t[:, (ITEM0[kind] + i) % 2, :, :],
                                   misc_bank(("T", kind, i)).rearrange("p (a b) -> p a b", a=2), ACT.Copy)
                empty_misc(e, ("T", kind, i))

            def free_prob(kind, i, group):
                j = i - 4 // group
                if j >= 0:
                    wait_misc(act, ("T", kind, j))

            def attention(kind, items, group, lag, fill=()):
                for i in range(min(lag, items)):
                    for g in range(group):
                        exps(kind, i * group + g)
                for i in range(items):
                    if i + lag < items:
                        for g in range(group):
                            free_prob(kind, i + lag, group)
                            exps(kind, (i + lag) * group + g)
                    if i < len(fill) and fill[i]:
                        fill[i]()
                    turned(kind, i)

            def copy_lin(key, dst, scale=None):
                wait_lin(act, key)
                src = lin_bank(key)
                if len(dst.shape) == 3:
                    src = src.rearrange("p (a b) -> p a b", a=2)
                e = act.activation(dst, src, ACT.Copy, scale=scale) if scale is not None \
                    else act.activation(dst, src, ACT.Copy)
                empty_lin(e, key)

            act.wait_ge(x_in_s, 16)
            sum_squares("mix", x)
            point(act, "zeros")
            for j in range(4):
                wait_lin(act, ("q", j))
                src = lin_bank(("q", j)).rearrange("p (a b) -> p a b", a=2)
                chain(act, act.activation(q_half[0:HD, 0, 2 * j:2 * j + 2, :], src[0:HD], ACT.Copy,
                                          scale=HD ** -0.5), act_chain)
                e = act.activation(q_half[HD:P, 1, 2 * j:2 * j + 2, :], src[HD:P], ACT.Copy, scale=HD ** -0.5)
                empty_lin(e, ("q", j))
            for j in range(4):
                copy_lin(("k", j), k_diff[:, 2 * j:2 * j + 2, :])
            for j in range(4):
                copy_lin(("v", j), v_diff[:, j % 2, (j // 2) * CW:(j // 2 + 1) * CW])
            for j in range(4):
                copy_lin(("cx", j), u_conv[:, 2 * j:2 * j + 2, :])
            xn_free("mix")
            act.dma_start(xn[:, :, :], mem_in.rearrange("(t p) d -> p t d", p=P)).then_inc(mem_in_s, 16)
            act.wait_ge(lam_sums, 2)
            act.activation(small[:, 2:4], small[:, 0:2], ACT.Exp).then_inc(lam_exps, 1)

            def gate(name, dst, i):
                def f():
                    for j in (2 * i, 2 * i + 1):
                        wait_lin(act, (name, j))
                        e = act.activation(dst[:, 2 * j:2 * j + 2, :],
                                           lin_bank((name, j)).rearrange("p (a b) -> p a b", a=2),
                                           ACT.Exp, scale=-1.0)
                        empty_lin(e, (name, j))
                return f

            attention("diff", HEADS, 2, 1, [None] * 4 + [gate("gc", gate_c, 0), gate("gc", gate_c, 1),
                                                         gate("ga", gate_a, 0), gate("ga", gate_a, 1)])
            def memory_squares(n):
                ss = stats(n)[0]
                for tb in range(TB):
                    act.activation(junk[:, 4 * tb:4 * tb + 4, :], xn[:, tb, :].rearrange("p (a b) -> p a b", a=4),
                                   ACT.Square, accum_out=ss[:, tb:tb + 1]).then_inc(squares, 1)

            act.wait_ge(mem_in_s, 16)
            memory_squares("mem")
            misc_emptied(act, ("O", "diff", HEADS - 1))
            act.activation(sq[:, :, :], o_diff[:, :, :], ACT.Square).then_inc(sub_sq, 1)
            for j in range(4):
                wait_misc(act, ("sub", j))
                e = act.activation(sq[:, 2 * j:2 * j + 2, :],
                                   misc_bank(("sub", j)).rearrange("p (a b) -> p a b", a=2), ACT.Sqrt,
                                   bias=small[:, 8:9])
                empty_misc(e, ("sub", j))
            xn_free("mem")
            act.dma_start(xn[:, :, :], mem2_in.rearrange("(t p) d -> p t d", p=P)).then_inc(mem2_in_s, 16)
            for j in range(4):
                copy_lin(("ck", j), k_cross[:, 2 * j:2 * j + 2, :])
            act.wait_ge(mem2_in_s, 16)
            act.wait_ge(squares, 4)
            memory_squares("mem2")
            for j in range(4):
                copy_lin(("cv", j), v_cross[:, j % 2, (j // 2) * CW:(j // 2 + 1) * CW])
            for l in range(2):
                copy_lin(("mkv" + "ab"[l], 0), memk[:, l, :, :])
                copy_lin(("mkv" + "ab"[l], 1), memv[:, l, :, :])
            act.wait_ge(squares, 6)
            for l in range(2):
                key = ("mkr", "ab"[l])
                lin_emptied(act, ("mkv" + "ab"[l], 0))
                act.activation(junk[:, 2 * l:2 * l + 2, :], memk[:, l, :, :], ACT.Square).then_inc(head_sq, 1)
                wait_misc(act, key)
                e = act.activation(junk[:, 4 + 2 * l:6 + 2 * l, :],
                                   misc_bank(key).rearrange("p (a b) -> p a b", a=2), ACT.Sqrt, bias=small[:, 9:10])
                empty_misc(e, key)
            x_updated("mixo")
            xn_free("mem2")
            sum_squares("cross", x)
            for j in range(4):
                copy_lin(("cq", j), q_cross[:, 2 * j:2 * j + 2, :], scale=(D // CROSS_HEADS) ** -0.5)
            attention("cross", CROSS_HEADS, 1, 2)
            x_updated("co")
            xn_free("cross")
            sum_squares("ffn", x)
            wait_misc(act, ("O", "cross", CROSS_HEADS - 1))
            act.dma_start(keys[:, :, :], keys_in.rearrange("p (a b) -> p a b", a=2 * PH)).then_inc(keys_in_s, 16)
            for j in range(8):
                copy_lin(("pq", j), q_peer[:, 2 * j:2 * j + 2, :])
            for tb in range(TB):
                for j in range(4):
                    wait_misc(act, ("sc", tb, j))
                    e = act.activation(score[:, tb, 4 * j:4 * j + 4, :],
                                       misc_bank(("sc", tb, j)).rearrange("p (a b) -> p a b", a=4), ACT.Copy)
                    empty_misc(e, ("sc", tb, j))
            act.sem_inc(gelu_ready, 1)

            def top_exps(tb, h):
                act.wait_ge(top_exp_in, h + (tb * PH + 1))
                act.activation(top_e, top_less, ACT.Exp, accum_out=hsum).then_inc(top_exp, 1)

            def weigh_rows(tb, h):
                for j in range(0, TOPK, 2):
                    s = j % GSLOTS
                    done = h * TOPK + (tb * PAIRS + j)
                    act.wait_ge(dot_ready, done + 2)
                    act.activation(gact[:, s:s + 2], dots[:, s:s + 2], ACT.Gelu).then_inc(gelu_ready, 1)
                    act.wait_ge(gelu_ready, h * (TOPK // 2) + (tb * (PAIRS // 2) + j // 2 + 2))
                    act.wait_ge(row_free, done + 2)
                    for k in range(2):
                        at = h * TOPK + (j + k)
                        act.activation(wact[:, s + k:s + k + 1], gact[:, s + k:s + k + 1], ACT.Copy,
                                       scale=weight[:, tb, at:at + 1] if isinstance(h, int) else
                                       weight[:, tb, bass.ds(at, 1)]).then_inc(wact_ready, 1)
                    act.wait_ge(wact_ready, done + 2)
                    for k in range(2):
                        act.activation(diag[:, s + k, :], ident, ACT.Copy, scale=wact[:, s + k:s + k + 1])\
                           .then_inc(diag_ready, 1)

            top_exps(0, 0)
            for tb in range(TB):
                with act.Fori(0, PH - 1) as h:
                    top_exps(tb, h + 1)
                    weigh_rows(tb, h)
                if tb < TB - 1:
                    top_exps(tb + 1, 0)
                weigh_rows(tb, PH - 1)
            act.wait_ge(acc_used, 4)
            sum_squares("final", x)
            act.dma_start(gfin, bass.AP(final_g.tensor, 0, [[0, P], [1, D]])).then_inc(gfin_in, 16)
            act.dma_start(pool_w, pool_in.rearrange("p (a b) -> p a b", b=P)).then_inc(pool_in_s, 16)
            act.dma_start(cnt[:, :, :], cnt_in.rearrange("p (a b) -> p a b", a=SWA_TILES)).then_inc(pool_in_s, 16)
            point(act, "h")
            sum_squares("mixa", x)

            def head_roots(keys_):
                for j, key in enumerate(keys_):
                    wait_misc(act, key)
                    e = act.activation(sq2[:, 2 * j:2 * j + 2, :],
                                       misc_bank(key).rearrange("p (a b) -> p a b", a=2),
                                       ACT.Sqrt, bias=small[:, 9:10])
                    empty_misc(e, key)

            def mlp(l):
                wt = "up" + l
                for j in range(16):
                    wait_lin(act, (wt, j))
                    h = hidden[:, 2 * j:2 * j + 2, :]
                    empty_lin(act.activation(h, lin_bank((wt, j)).rearrange("p (a b) -> p a b", a=2), ACT.Relu),
                              (wt, j))
                    lin_emptied(act, (wt, j))
                    act.activation(h, h, ACT.Square).then_inc(hidden_ready, 1)

            for j in range(3):
                copy_lin(("ina", j), u_pool[:, 2 * j:2 * j + 2, :])
            copy_lin(("ina", 3), raw2[:, 6:8, :])
            lin_emptied(act, ("ina", 3))
            act.activation(sq2[:, 6:8, :], raw2[:, 6:8, :], ACT.Square).then_inc(head_sq, 1)
            wait_misc(act, ("mqr", "a"))
            e = act.activation(sq2[:, 0:2, :], misc_bank(("mqr", "a")).rearrange("p (a b) -> p a b", a=2),
                               ACT.Sqrt, bias=small[:, 9:10])
            empty_misc(e, ("mqr", "a"))
            attention("mema", MEM_HEADS, 1, 2)
            x_updated("outa")
            xn_free("mixa")
            sum_squares("mlpa", x)
            mlp("a")
            x_updated("downa")
            xn_free("mlpa")
            sum_squares("mixb", x)
            act.dma_start(alibi[:, :, :], consts_in[:, 3 * P + TOPK:].rearrange("p (a b) -> p a b", a=TB))\
               .then_inc(alibi_in, 16)
            copy_lin(("kvb", 0), k_swa[:, :, :])
            copy_lin(("kvb", 1), v_swa[:, :, :])
            lin_emptied(act, ("kvb", 0))
            act.activation(sq2[:, 6:8, :], k_swa[:, :, :], ACT.Square).then_inc(head_sq, 1)
            wait_misc(act, ("kr",))
            e = act.activation(sq2[:, 0:2, :], misc_bank(("kr",)).rearrange("p (a b) -> p a b", a=2),
                               ACT.Sqrt, bias=small[:, 9:10])
            empty_misc(e, ("kr",))
            for j in range(4):
                copy_lin(("inb", j), raw2[:, 2 * j:2 * j + 2, :])
            lin_emptied(act, ("inb", 3))
            point(act, "k_swa")
            act.activation(sq2[:, :, :], raw2[:, :, :], ACT.Square).then_inc(head_sq, 1)
            head_roots([("qr", j) for j in range(4)])
            attention("swa", SWA_HEADS, 1, 2)
            attention("memb", MEM_HEADS, 1, 2)
            x_updated("outb")
            xn_free("mixb")
            sum_squares("mlpb", x)
            mlp("b")

        @block.tensor
        def _(pe):
            state = {"chunk": 0, "misc": 0}

            def fill_misc(key):
                assert MISC[key] == state["misc"], key
                state["misc"] += 1
                j = MISC[key]
                if j >= 4:
                    pe.wait_ge(misc_free[j % 4], j // 4)
                return misc_bank(key)

            def lin_bank_free(key):
                j = LIN[key]
                if j >= 4:
                    pe.wait_ge(lin_free[j % 4], j // 4)

            def next_chunk():
                c = state["chunk"]
                state["chunk"] += 1
                pe.wait_ge(chunk_in[c % SLOTS], 16 * (c // SLOTS + 1))
                return c

            def features(src):
                c = next_chunk()
                w = wring[:, c % SLOTS, :, :]
                i = CHUNKS[:c].count(CHUNKS[c])
                for j in range(2):
                    key = (CHUNKS[c], 2 * i + j)
                    lin_bank_free(key)
                    for n in range(2):
                        for kc in range(KC):
                            at = (2 * j + n) * P
                            mm = pe.matmul(lin_bank(key)[:, n * S:(n + 1) * S], w[:, kc, at:at + P],
                                           src[:, kc, :], start=(kc == 0), stop=(kc == KC - 1))
                    mm.then_inc(half_done, 1)

            def tokens(src, k0=0, start=True, stop=True):
                c = next_chunk()
                w = wring[:, c % SLOTS, :, :]
                i = CHUNKS[:c].count(CHUNKS[c])
                for tb in range(TB):
                    key = (CHUNKS[c], 2 * (i // 4 if CHUNKS[c].startswith("down") else i) + tb)
                    if start:
                        lin_bank_free(key)
                    for kc in range(KC):
                        mm = pe.matmul(lin_bank(key), src[:, k0 + kc, tb * P:(tb + 1) * P], w[:, kc, :],
                                       start=(start and kc == 0), stop=(stop and kc == KC - 1))
                    mm.then_inc(half_done, 1)

            def keys_values(src):
                c = next_chunk()
                w = wring[:, c % SLOTS, :, :]
                name = CHUNKS[c]
                lin_bank_free((name, 0))
                for n in range(2):
                    for kc in range(KC):
                        mm = pe.matmul(lin_bank((name, 0))[:, n * S:(n + 1) * S], w[:, kc, n * P:(n + 1) * P],
                                       src[:, kc, :], start=(kc == 0), stop=(kc == KC - 1))
                mm.then_inc(half_done, 1)
                lin_bank_free((name, 1))
                for tb in range(TB):
                    for kc in range(KC):
                        mm = pe.matmul(lin_bank((name, 1))[:, tb * S:(tb + 1) * S],
                                       src[:, kc, tb * P:(tb + 1) * P], w[:, kc, 2 * P:CW],
                                       start=(kc == 0), stop=(kc == KC - 1))
                mm.then_inc(half_done, 1)

            def norm(n):
                pe.wait_ge(xn_ready, 2 * [m for m in NORMS if m != "final"].index(n) + 1)
                for tb in range(TB):
                    if tb:
                        pe.wait_ge(xn_ready, 2 * [m for m in NORMS if m != "final"].index(n) + 2)
                    for h in range(2):
                        b = fill_misc(("xT", n, tb, h))
                        for f in range(4):
                            at = (4 * h + f) * P
                            mm = pe.transpose(b[:, f * P:(f + 1) * P], xn[:, tb, at:at + P], ident)
                        mm.then_inc(misc_full, 1)

            def normed(n):
                for tb in range(TB):
                    for h in range(2):
                        misc_emptied(pe, ("xT", n, tb, h))

            def attention(kind, items, group, lag, scores, values, fill=()):
                def s(u):
                    b = fill_misc(("S", kind, u))
                    for qb in range(TB):
                        pairs = scores(u, qb)
                        for n, (l, r) in enumerate(pairs):
                            mm = pe.matmul(b[:, qb * S:(qb + 1) * S], l, r, start=(n == 0),
                                           stop=(n == len(pairs) - 1))
                    mm.then_inc(misc_full, 1)

                for i in range(min(lag, items)):
                    for g in range(group):
                        s(i * group + g)
                for i in range(items):
                    if i + lag < items:
                        for g in range(group):
                            s((i + lag) * group + g)
                    if i < len(fill) and fill[i]:
                        fill[i]()
                    r = (UNIT0[kind] + i * group) % 4
                    pe.wait_ge(p_ready, ITEM0[kind] + i + 1)
                    b = fill_misc(("T", kind, i))
                    for kb in range(2):
                        for qb in range(TB):
                            mm = pe.transpose(b[:, kb * S + qb * P:kb * S + (qb + 1) * P],
                                              prob[:, r, qb, kb * P:(kb + 1) * P], ident)
                    mm.then_inc(misc_full, 1)
                    misc_emptied(pe, ("T", kind, i))
                    for e, part_ in enumerate(values(i)):
                        if e == 0:
                            b = fill_misc(("O", kind, i))
                        for kb in range(2):
                            mm = pe.matmul(b[:, e * S:(e + 1) * S], part_(kb),
                                           prob_t[:, (ITEM0[kind] + i) % 2, kb, :], start=(kb == 0), stop=(kb == 1))
                    mm.then_inc(misc_full, 1)

            pe.wait_ge(const_in, 48)
            pe.wait_ge(row_in, 32)
            b = fill_misc(("bias",))
            pe.matmul(b[0:8, :], rel_sb, onehot, start=True, stop=True).then_inc(misc_full, 1)
            norm("mix")
            normed("mix")
            for _ in range(4):
                features(act_t)
            for _ in range(2):
                tokens(act_t)
            for _ in range(2):
                features(act_t)
            for j in range(4):
                lin_emptied(pe, ("q", j))
                lin_emptied(pe, ("k", j))
                lin_emptied(pe, ("v", j))
            attention("diff", HEADS, 2, 1,
                      lambda u, qb: [(q_half[:, u % 2, u // 2, qb * P:(qb + 1) * P], k_diff[:, u // 2, :])],
                      lambda h: [lambda kb: v_diff[:, kb, h * P:(h + 1) * P]],
                      [lambda: features(act_t)] * 8)
            norm("mem")
            pe.wait_ge(sub_sq, 1)
            for j in range(4):
                b = fill_misc(("sub", j))
                pe.matmul(b, mean128, sq[:, 2 * j:2 * j + 2, :], start=True, stop=True).then_inc(misc_full, 1)
            normed("mem")
            for _ in range(2):
                features(act2_t)
            for _ in range(2):
                tokens(act2_t)
            norm("mem2")
            normed("mem2")
            keys_values(act_t)
            keys_values(act2_t)
            for l in range(2):
                pe.wait_ge(head_sq, l + 1)
                b = fill_misc(("mkr", "ab"[l]))
                pe.matmul(b, mean64, junk[:, 2 * l:2 * l + 2, :], start=True, stop=True).then_inc(misc_full, 1)
            for j in range(4):
                lin_emptied(pe, ("cb", j))
            for _ in range(2):
                features(u_conv)
            point(pe, "o_diff")
            for _ in range(2):
                features(o_diff)
            point(pe, "merged")
            for _ in range(2):
                tokens(merged)
            norm("cross")
            normed("cross")
            for _ in range(2):
                features(act_t)
            for j in range(4):
                lin_emptied(pe, ("ck", j))
                lin_emptied(pe, ("cv", j))
                lin_emptied(pe, ("cq", j))
            attention("cross", CROSS_HEADS, 1, 2,
                      lambda h, qb: [(q_cross[:, 2 * h + e, qb * P:(qb + 1) * P], k_cross[:, 2 * h + e, :])
                                     for e in range(2)],
                      lambda h: [lambda kb, e=e: v_cross[:, kb, (2 * h + e) * P:(2 * h + e + 1) * P]
                                 for e in range(2)])
            for h in range(CROSS_HEADS):
                misc_emptied(pe, ("O", "cross", h))
            for _ in range(2):
                tokens(o_cross)
            norm("ffn")
            normed("ffn")
            for _ in range(4):
                features(act_t)
            for j in range(8):
                lin_emptied(pe, ("pq", j))
            pe.wait_ge(keys_in_s, 16)
            for tb in range(TB):
                for j in range(4):
                    b = fill_misc(("sc", tb, j))
                    for n in range(4):
                        mm = pe.matmul(b[:, n * P:(n + 1) * P], q_peer[:, 4 * j + n, tb * P:(tb + 1) * P],
                                       keys[:, 4 * j + n, :], start=True, stop=True)
                    mm.then_inc(misc_full, 1)
            for j in range(4):
                misc_emptied(pe, ("sc", TB - 1, j))
            pe.wait_ge(peer_zero, 1)
            pe.sem_inc(row_free, GSLOTS)
            for tb in range(TB):
                for kc in range(KC):
                    mm = pe.transpose(token_rows[tb][:, kc // 4, kc % 4 * P:(kc % 4 + 1) * P],
                                      act_t[:, kc, tb * P:(tb + 1) * P], ident)
                mm.then_inc(hf_ready, 1)
            for tb in range(TB):
                sums = row_sums[tb]
                for n in range(2):
                    pe.matmul(sums[:, n, :], zeros, act_t[:, 0:2, :], start=True, stop=False,
                              skip_group_check=True)
                with pe.Fori(0, PAIRS // GSLOTS) as i:
                    for s in range(GSLOTS):
                        pe.wait_ge(diag_ready, i * GSLOTS + (tb * PAIRS + s + 1))
                        for n in range(2):
                            mm = pe.matmul(sums[:, n, :], diag[:, s, :], rows[:, s, D + n * CW:D + (n + 1) * CW],
                                           start=False, stop=False, skip_group_check=True)
                        mm.then_inc(row_free, 1)
                for n in range(2):
                    mm = pe.matmul(sums[:, n, :], zeros, act_t[:, 0:2, :], start=False, stop=True,
                                   skip_group_check=True)
                mm.then_inc(acc_ready, 1)

            def mlp(l):
                norm("mlp" + l)
                normed("mlp" + l)
                for _ in range(8):
                    features(act_t)
                for n in range(2):
                    for kg in range(4):
                        if n == 0:
                            pe.wait_ge(hidden_ready, 16 * "ab".index(l) + 4 * (kg + 1))
                        tokens(hidden, k0=8 * kg, start=(kg == 0), stop=(kg == 3))

            norm("mixa")
            normed("mixa")
            for i in range(2):
                if i == 0:
                    pe.wait_ge(acc_used, 4)
                features(act_t)
            pe.wait_ge(head_sq, 3)
            b = fill_misc(("mqr", "a"))
            pe.matmul(b, mean64, sq2[:, 6:8, :], start=True, stop=True).then_inc(misc_full, 1)
            point(pe, "d_pool")
            pe.wait_ge(pool_in_s, 32)
            for g in range(2):
                for j in range(3):
                    b = fill_misc(("pool", g, j))
                    ins_ = [(n, a) for n, (a, o) in enumerate(POOL_BLOCKS) if o == j]
                    for n, (at, a) in enumerate(ins_):
                        mm = pe.matmul(b[:, 0:S], pool_w[:, 7 * g + at, :], win[:, 0, 3 * g + a, :],
                                       start=(n == 0), stop=(n == len(ins_) - 1))
                    mm.then_inc(misc_full, 1)
            point(pe, "mq")
            point(pe, "kmem_b")
            attention("mema", MEM_HEADS, 1, 2,
                      lambda h, qb: [(mq_half[:, h % 2, h // 2, qb * P:(qb + 1) * P], memk[:, 0, h // 2, :])],
                      lambda h: [lambda kb: memv[:, 0, kb, (h // 2) * P:(h // 2 + 1) * P]])
            for h in range(MEM_HEADS):
                misc_emptied(pe, ("O", "mema", h))
            for g in range(2):
                for j in range(3):
                    misc_emptied(pe, ("pool", g, j))
            for _ in range(2):
                tokens(cat_t)
            mlp("a")
            norm("mixb")
            normed("mixb")
            keys_values(act2_t)
            pe.wait_ge(head_sq, 4)
            b = fill_misc(("kr",))
            pe.matmul(b, mean64, sq2[:, 6:8, :], start=True, stop=True).then_inc(misc_full, 1)
            for _ in range(2):
                features(act_t)
            pe.wait_ge(head_sq, 5)
            for j in range(4):
                b = fill_misc(("qr", j))
                pe.matmul(b, mean64, sq2[:, 2 * j:2 * j + 2, :], start=True, stop=True).then_inc(misc_full, 1)
            point(pe, "q_swa")
            lin_emptied(pe, ("kvb", 1))
            attention("swa", SWA_HEADS, 1, 2,
                      lambda u, qb: [(q_swa[:, u % 2, u // 2, qb * P:(qb + 1) * P], k_swa[:, u // 6, :])],
                      lambda u: [lambda kb: v_swa[:, kb, (u // 6) * P:(u // 6 + 1) * P]])
            attention("memb", MEM_HEADS, 1, 2,
                      lambda h, qb: [(q_swa[:, h % 2, SWA_TILES + h // 2, qb * P:(qb + 1) * P],
                                      memk[:, 1, h // 2, :])],
                      lambda h: [lambda kb: memv[:, 1, kb, (h // 2) * P:(h // 2 + 1) * P]])
            for u in range(SWA_HEADS):
                misc_emptied(pe, ("O", "swa", u))
            for h in range(MEM_HEADS):
                misc_emptied(pe, ("O", "memb", h))
            for _ in range(2):
                tokens(cat_t)
            mlp("b")
            assert state["misc"] == len(MISC) and state["chunk"] == NCHUNK

        @block.vector
        def _(dve):
            def do(ins):
                chain(dve, ins, dve_chain)

            def rows2(ap):
                return ap.rearrange("p (a b) -> p a b", a=2)

            def scale_rows(n, src, dst):
                ss, ms, rs = stats(n)
                dve.wait_ge(squares, 2 * NORMS.index(n) + 2)
                dve.tensor_scalar(ms, ss, 1.0 / D, 1e-6, ALU.mult, ALU.add).then_inc(mean_sq, 1)
                dve.wait_ge(rstd_s, NORMS.index(n) + 1)
                for tb in range(TB):
                    ins = dve.tensor_scalar(dst[:, tb, :], src[:, tb, :], rs[:, tb:tb + 1], None, ALU.mult)
                    if n == "final":
                        do(ins)
                    else:
                        ins.then_inc(xn_ready, 1)

            def take_norm(n, dsts):
                for tb in range(TB):
                    for h in range(2):
                        key = ("xT", n, tb, h)
                        wait_misc(dve, key)
                        for k, (g, dst) in enumerate(dsts):
                            ins = dve.tensor_tensor(
                                dst[:, 4 * h:4 * h + 4, tb * P:(tb + 1) * P],
                                misc_bank(key).rearrange("p (a b) -> p a b", a=4),
                                gain(g)[:, 4 * h:4 * h + 4].unsqueeze(2).broadcast_to([P, 4, P]), ALU.mult)
                            if k < len(dsts) - 1:
                                do(ins)
                            else:
                                empty_misc(ins, key)

            def add_x(weight):
                for j in range(4):
                    wait_lin(dve, (weight, j))
                    tb, n = j % 2, j // 2
                    xs = x[:, tb, n * CW:(n + 1) * CW]
                    empty_lin(dve.tensor_tensor(xs, lin_bank((weight, j)), xs, ALU.add), (weight, j))

            def maxima(kind, u, bias_ap=None, slope=None, sink=None):
                g = UNIT0[kind] + u
                r = g % 4
                key = ("S", kind, u)
                wait_misc(dve, key)
                b = rows2(misc_bank(key))
                src = b
                if bias_ap is not None:
                    if slope is None:
                        ins = dve.tensor_tensor(prob[:, r], b, bias_ap, ALU.add)
                    else:
                        ins = dve.scalar_tensor_tensor(prob[:, r], bias_ap, slope, b, ALU.mult, ALU.add)
                    empty_misc(ins, key)
                    misc_emptied(dve, key)
                    src = prob[:, r]
                if sink is None:
                    dve.tensor_reduce(nmax[:, r, :], src, AX.X, ALU.max, negate=True).then_inc(max_ready, 1)
                else:
                    do(dve.tensor_reduce(nmax[:, r, :], src, AX.X, ALU.max))
                    dve.tensor_scalar(nmax[:, r, :], nmax[:, r, :], sink, -1.0, ALU.max, ALU.mult)\
                       .then_inc(max_ready, 1)

            def exps_done(kind, u):
                in_psum = kind in ("cross", "mema", "memb")
                n = 0
                for k in ("diff", "cross", "mema", "swa", "memb"):
                    per = 1 if k in ("cross", "mema", "memb") else 2
                    if k == kind:
                        n += per * (u + 1)
                        break
                    n += per * {"diff": 2 * HEADS, "cross": CROSS_HEADS, "mema": MEM_HEADS, "swa": SWA_HEADS}[k]
                dve.wait_ge(exp_ready, n)
                if in_psum:
                    misc_emptied(dve, ("S", kind, u))

            def normalise(kind, i):
                if kind == "diff":
                    ra, rb = (UNIT0[kind] + 2 * i) % 4, (UNIT0[kind] + 2 * i + 1) % 4
                    exps_done(kind, 2 * i + 1)
                    do(dve.reciprocal(rsum[:, ra:rb + 1, :], ssum[:, ra:rb + 1, :]))
                    do(dve.tensor_scalar(rsum[:, rb, :], rsum[:, rb, :], small[:, 6:7], None, ALU.mult))
                    for qb in range(TB):
                        do(dve.tensor_scalar(prob[:, rb, qb, :], prob[:, rb, qb, :], rsum[:, rb, qb:qb + 1],
                                             None, ALU.mult))
                    for qb in range(TB):
                        ins = dve.scalar_tensor_tensor(prob[:, ra, qb, :], prob[:, ra, qb, :],
                                                       rsum[:, ra, qb:qb + 1], prob[:, rb, qb, :],
                                                       ALU.mult, ALU.add)
                        do(ins) if qb == 0 else ins.then_inc(p_ready, 1)
                    return
                r = (UNIT0[kind] + i) % 4
                exps_done(kind, i)
                if kind == "swa":
                    do(dve.tensor_tensor(ssum[:, r, :], ssum[:, r, :], esink[:, r, :], ALU.add))
                do(dve.reciprocal(rsum[:, r, :], ssum[:, r, :]))
                for qb in range(TB):
                    ins = dve.tensor_scalar(prob[:, r, qb, :], prob[:, r, qb, :], rsum[:, r, qb:qb + 1], None,
                                            ALU.mult)
                    do(ins) if qb == 0 else ins.then_inc(p_ready, 1)

            def attention(kind, items, group, lag, extra, dst, fill=()):
                for i in range(min(lag, items)):
                    for g in range(group):
                        maxima(kind, i * group + g, **extra(i * group + g))
                for i in range(items):
                    if i + lag < items:
                        for g in range(group):
                            u = (i + lag) * group + g
                            j = i + lag - 4 // group
                            if j >= 0:
                                wait_misc(dve, ("T", kind, j))
                            maxima(kind, u, **extra(u))
                    normalise(kind, i)
                    if i < len(fill) and fill[i]:
                        fill[i]()
                    key = ("O", kind, i)
                    wait_misc(dve, key)
                    lo, hi, d, w = dst(i)
                    src = misc_bank(key)[lo:hi, 0:w]
                    if w == 2 * S:
                        src = rows2(src)
                    empty_misc(dve.tensor_copy(d, src), key)

            do(dve.memset(q_half[HD:P, 0, :, :], 0.0))
            do(dve.memset(q_half[0:HD, 1, :, :], 0.0))
            do(dve.memset(small[:, 8:9], 1e-5))
            at_point(dve.memset(small[:, 9:10], 1e-6), "zeros")
            dve.wait_ge(const_in, 48)
            for j in range(2):
                at = 2 * j * HD
                do(dve.tensor_tensor(bc[:, at:at + HD], bc[:, at:at + HD], bc[:, at + HD:at + 2 * HD], ALU.mult))
                dve.tensor_reduce(small[:, j:j + 1], bc[:, at:at + HD], AX.X, ALU.add).then_inc(lam_sums, 1)
            dve.wait_ge(x_in_s, 16)
            scale_rows("mix", x, xn)
            wait_misc(dve, ("bias",))
            empty_misc(dve.tensor_copy(bias_row, misc_bank(("bias",))[0:8, :]), ("bias",))
            take_norm("mix", [("mix", act_t)])
            dve.wait_ge(lam_exps, 1)
            do(dve.tensor_tensor(small[:, 5:6], small[:, 3:4], small[:, 2:3], ALU.subtract))
            do(dve.tensor_scalar(small[:, 6:7], small[:, 5:6], -LAM_INIT, None, ALU.add))
            dve.wait_ge(bias_in, 32)

            def take_cc(i):
                def f():
                    for j in (2 * i, 2 * i + 1):
                        key = ("cc", j)
                        wait_lin(dve, key)
                        us = u_conv[:, 2 * j:2 * j + 2, :]
                        lin_emptied(dve, ("cx", j))
                        empty_lin(dve.tensor_tensor(us, rows2(lin_bank(key)), us, ALU.mult), key)
                        lin_emptied(dve, key)
                        for t in (2 * j, 2 * j + 1):
                            a = VEC["conv"][0]
                            do(dve.tensor_scalar(conv[:, t, :], u_conv[:, t, :], vecs[:, a + 16 + t:a + 17 + t],
                                                 None, ALU.mult))
                            for back in (1, 2):
                                w = vecs[:, a + 8 * (2 - back) + t:a + 8 * (2 - back) + t + 1]
                                do(dve.scalar_tensor_tensor(conv[:, t, back:S], u_conv[:, t, 0:S - back], w,
                                                            conv[:, t, back:S], ALU.mult, ALU.add))
                return f

            def take_cb(i):
                def f():
                    for j in (2 * i, 2 * i + 1):
                        key = ("cb", j)
                        wait_lin(dve, key)
                        cs = conv[:, 2 * j:2 * j + 2, :]
                        empty_lin(dve.tensor_tensor(u_conv[:, 2 * j:2 * j + 2, :], rows2(lin_bank(key)), cs,
                                                    ALU.mult), key)
                return f

            def sigmoid(name, dst, i):
                def f():
                    for j in (2 * i, 2 * i + 1):
                        lin_emptied(dve, (name, j))
                    d = dst[:, 4 * i:4 * i + 4, :]
                    do(dve.tensor_scalar(d, d, 1.0, None, ALU.add))
                    do(dve.reciprocal(d, d))
                return f

            attention("diff", HEADS, 2, 1, lambda u: dict(bias_ap=bias[:, u // 2]),
                      lambda h: (0, P, o_diff[:, h, :], S),
                      [take_cc(0), take_cc(1), take_cb(0), take_cb(1), sigmoid("gc", gate_c, 0),
                       sigmoid("gc", gate_c, 1), sigmoid("ga", gate_a, 0), sigmoid("ga", gate_a, 1)])
            for j in range(4):
                lin_emptied(dve, ("cb", j))
            do(dve.tensor_scalar(small[:, 7:8], gain("subln"), 1.0 - LAM_INIT, None, ALU.mult))
            dve.wait_ge(mem_in_s, 16)
            scale_rows("mem", xn, xn)
            take_norm("mem", [("mem", act2_t)])
            for j in range(4):
                misc_emptied(dve, ("sub", j))
            do(dve.reciprocal(sq[:, :, :], sq[:, :, :]))
            at_point(dve.scalar_tensor_tensor(o_diff[:, :, :], o_diff[:, :, :], small[:, 7:8], sq[:, :, :],
                                              ALU.mult, ALU.mult), "o_diff")
            dve.wait_ge(mem2_in_s, 16)
            scale_rows("mem2", xn, xn)
            take_norm("mem2", [("mem2a", act_t), ("mem2b", act2_t)])
            for l in range(2):
                misc_emptied(dve, ("mkr", "ab"[l]))
                r = junk[:, 4 + 2 * l:6 + 2 * l, :]
                do(dve.reciprocal(r, r))
                at_point(dve.scalar_tensor_tensor(memk[:, l, :, :], memk[:, l, :, :], gain("mkn" + "ab"[l]), r,
                                                  ALU.mult, ALU.mult), "kmem_" + "ab"[l])
            for j in range(4):
                key = ("cout", j)
                wait_lin(dve, key)
                empty_lin(dve.tensor_tensor(merged[:, 2 * j:2 * j + 2, :], rows2(lin_bank(key)),
                                            gate_c[:, 2 * j:2 * j + 2, :], ALU.mult), key)
            for j in range(4):
                key = ("aout", j)
                wait_lin(dve, key)
                g = gate_a[:, 2 * j:2 * j + 2, :]
                empty_lin(dve.tensor_tensor(g, rows2(lin_bank(key)), g, ALU.mult), key)
            for j in range(4):
                lin_emptied(dve, ("aout", j))
                lin_emptied(dve, ("cout", j))
            at_point(dve.tensor_tensor(merged[:, :, :], merged[:, :, :], gate_a[:, :, :], ALU.add), "merged")
            add_x("mixo")
            scale_rows("cross", x, xn)
            take_norm("cross", [("cross", act_t)])
            attention("cross", CROSS_HEADS, 1, 2, lambda u: {},
                      lambda h: (0, P, o_cross[:, 2 * h:2 * h + 2, :], 2 * S))
            add_x("co")
            scale_rows("ffn", x, xn)
            take_norm("ffn", [("ffn", act_t)])
            dve.memset(zeros, 0.0).then_inc(peer_zero, 1)
            STEPS = 22

            def top_experts(tb, h):
                turn = h + tb * PH
                steps = [0]

                def step(ins):
                    steps[0] += 1
                    ins.then_inc(top_chain, 1)
                    dve.wait_ge(top_chain, turn * STEPS + steps[0])
                    dve.sem_inc(top_passed, 1)

                def at(ap, size):
                    return ap[:, tb, h * size:(h + 1) * size] if isinstance(h, int) \
                        else ap[:, tb, bass.ds(h * size, size)]

                src = score[:, tb, 2 * h:2 * h + 2, :] if isinstance(h, int) \
                    else score[:, tb, bass.ds(h * 2, 2), :]
                step(dve.tensor_copy(half_score, src))
                for r in range(2):
                    k0 = 8 * r
                    dve.max(half_vals[:, 0, k0:k0 + 8], half_score[:, 0, :])
                    step(dve.max(half_vals[:, 1, k0:k0 + 8], half_score[:, 1, :]))
                    dve.max_index(half_idx[:, 0, k0:k0 + 8], half_vals[:, 0, k0:k0 + 8], half_score[:, 0, :])
                    step(dve.max_index(half_idx[:, 1, k0:k0 + 8], half_vals[:, 1, k0:k0 + 8], half_score[:, 1, :]))
                    if r == 0:
                        dve.match_replace(half_score[:, 0, :], half_vals[:, 0, 0:8], half_score[:, 0, :], -3e38)
                        step(dve.match_replace(half_score[:, 1, :], half_vals[:, 1, 0:8], half_score[:, 1, :],
                                               -3e38))
                dve.tensor_copy(half_idxf, half_idx)
                step(dve.tensor_tensor(cand, half_vals[:, 0, :].unsqueeze(2).broadcast_to([P, TOPK, TOPK]),
                                       half_vals[:, 1, :].unsqueeze(1).broadcast_to([P, TOPK, TOPK]), ALU.add))
                flat = cand.rearrange("p a b -> p (a b)")
                for r in range(2):
                    k0 = 8 * r
                    step(dve.max(top_vals[:, k0:k0 + 8], flat))
                    step(dve.max_index(top_pos[:, k0:k0 + 8], top_vals[:, k0:k0 + 8], flat))
                    if r == 0:
                        step(dve.match_replace(flat, top_vals[:, 0:8], flat, -3e38))
                dve.tensor_scalar(top_less, top_vals, top_vals[:, 0:1], None, ALU.subtract).then_inc(top_exp_in, 1)
                dve.tensor_scalar(top_half[:, 0, :], top_pos, 4, None, ALU.logical_shift_right)
                step(dve.tensor_scalar(top_half[:, 1, :], top_pos, TOPK - 1, None, ALU.bitwise_and))
                step(dve.tensor_copy(top_halff, top_half))
                for c in range(2):
                    step(dve.tensor_tensor(pick, iota16.unsqueeze(1).broadcast_to([P, TOPK, TOPK]),
                                           top_halff[:, c, :].unsqueeze(2).broadcast_to([P, TOPK, TOPK]),
                                           ALU.is_equal))
                    step(dve.tensor_tensor(pick, pick,
                                           half_idxf[:, c, :].unsqueeze(1).broadcast_to([P, TOPK, TOPK]),
                                           ALU.mult))
                    step(dve.tensor_reduce(found[:, c, :], pick, AX.X, ALU.add))
                dve.scalar_tensor_tensor(at(expert, TOPK), found[:, 0, :], float(NKEYS), found[:, 1, :],
                                         ALU.mult, ALU.add).then_inc(experts_ready, 1)
                dve.wait_ge(top_exp, turn + 1)
                step(dve.reciprocal(hinv, hsum))
                step(dve.tensor_scalar(at(weight, TOPK), top_e, hinv, None, ALU.mult))
                assert steps[0] == STEPS, steps

            def dot_rows(tb, h):
                for j in range(TOPK):
                    s = j % GSLOTS
                    if s == 0:
                        dve.wait_ge(gelu_ready, h * (TOPK // 2) + (tb * (PAIRS // 2) + j // 2 + 1))
                    dve.wait_ge(gathered[s], h * 32 + (tb * (PAIRS // GSLOTS) + j // GSLOTS + 1) * 16)
                    u = rows[:, s, 0:D].rearrange("p (a b) -> p a b", a=2)
                    dve.tensor_tensor_reduce(u, u, token_rows[tb][:, :, :], 1.0, 0.0,
                                             ALU.mult, ALU.add, dots[:, s:s + 1]).then_inc(dot_ready, 1)

            for j in range(4):
                misc_emptied(dve, ("sc", 0, j))
            top_experts(0, 0)
            for tb in range(TB):
                dve.wait_ge(hf_ready, tb + 1)
                with dve.Fori(0, PH - 1) as h:
                    top_experts(tb, h + 1)
                    dot_rows(tb, h)
                if tb < TB - 1:
                    for j in range(4):
                        misc_emptied(dve, ("sc", tb + 1, j))
                    top_experts(tb + 1, 0)
                dot_rows(tb, PH - 1)
                dve.wait_ge(acc_ready, tb + 1)
                for n in range(2):
                    xs = x[:, tb, n * CW:(n + 1) * CW]
                    dve.tensor_tensor(xs, row_sums[tb][:, n, :], xs, ALU.add).then_inc(acc_used, 1)
            dve.wait_ge(acc_used, 4)
            scale_rows("final", x, xn)
            dve.wait_ge(gfin_in, 16)
            for tb in range(TB):
                ins = dve.tensor_tensor(x[:, tb, :], xn[:, tb, :], gfin, ALU.mult)
                do(ins) if tb == 0 else at_point(ins, "h")
            point(dve, "h")
            scale_rows("mixa", x, xn)
            take_norm("mixa", [("mixa", act_t)])

            do(dve.memset(mq_half[HD:P, 0, :, :], 0.0))
            do(dve.memset(mq_half[0:HD, 1, :, :], 0.0))
            for j in range(3):
                lin_emptied(dve, ("ina", j))

            def window(dst, src, t0, back):
                n = SWA_TILES
                do(dve.tensor_copy(dst[:, t0:n, 0:back], src[:, t0:n, 0:back]))
                do(dve.tensor_tensor(dst[:, t0:n, back:S], src[:, t0:n, back:S], src[:, t0:n, 0:S - back],
                                     ALU.add))

            w0, w1 = win[:, 0], win[:, 1]
            window(w0, u_pool, 0, 1)
            window(w1, w0, 1, 2)
            window(w0, w1, 3, 4)
            window(w1, w0, 4, 8)
            dve.wait_ge(pool_in_s, 32)
            for src, lo, hi, t in ((w0, 0, P, 0), (w0, 0, HD, 1), (w1, HD, P, 1), (w1, 0, P, 2), (w0, 0, P, 3),
                                   (w0, 0, HD, 4), (w1, HD, P, 4), (w1, 0, P, 5)):
                do(dve.tensor_tensor(w0[lo:hi, t, :], src[lo:hi, t, :], cnt[lo:hi, t, :], ALU.mult))
            at_point(dve.tensor_tensor(w0, w0, u_pool[:, :, :], ALU.subtract), "d_pool")
            misc_emptied(dve, ("mqr", "a"))
            r = sq2[:, 0:2, :]
            do(dve.reciprocal(r, r))
            do(dve.tensor_scalar(small[:, 10:11], gain("mqna"), HD ** -0.5, None, ALU.mult))
            do(dve.scalar_tensor_tensor(mq_half[0:HD, 0, :, :], raw2[0:HD, 6:8, :], small[0:HD, 10:11], r[0:HD],
                                        ALU.mult, ALU.mult))
            at_point(dve.scalar_tensor_tensor(mq_half[HD:P, 1, :, :], raw2[HD:P, 6:8, :], small[HD:P, 10:11],
                                              r[HD:P], ALU.mult, ALU.mult), "mq")
            for g in range(2):
                for j in range(3):
                    key = ("pool", g, j)
                    wait_misc(dve, key)
                    t = 3 * g + j
                    empty_misc(dve.tensor_scalar(cat_t[:, t, :], misc_bank(key)[:, 0:S],
                                                 gain("pool")[:, t:t + 1], None, ALU.mult), key)

            def half_tile(t0):
                def f(h):
                    lo = HD * (h % 2)
                    return lo, lo + HD, cat_t[lo:lo + HD, t0 + h // 2, :], S
                return f

            attention("mema", MEM_HEADS, 1, 2, lambda u: {}, half_tile(SWA_TILES))
            add_x("outa")

            def mlp(l):
                scale_rows("mlp" + l, x, xn)
                take_norm("mlp" + l, [("mlp" + l, act_t)])
                add_x("down" + l)

            mlp("a")
            scale_rows("mixb", x, xn)
            take_norm("mixb", [("kv", act2_t), ("mixb", act_t)])
            do(dve.memset(q_swa[HD:P, 0, :, :], 0.0))
            do(dve.memset(q_swa[0:HD, 1, :, :], 0.0))
            misc_emptied(dve, ("kr",))
            do(dve.reciprocal(r, r))
            at_point(dve.scalar_tensor_tensor(k_swa[:, :, :], k_swa[:, :, :], gain("kn"), r, ALU.mult, ALU.mult),
                     "k_swa")
            do(dve.tensor_scalar(small[:, 10:11], gain("qn"), HD ** -0.5, None, ALU.mult))
            do(dve.tensor_scalar(small[:, 11:12], gain("mqnb"), HD ** -0.5, None, ALU.mult))
            for j in range(4):
                misc_emptied(dve, ("qr", j))
            do(dve.reciprocal(sq2[:, :, :], sq2[:, :, :]))
            for a, b, g in ((0, SWA_TILES, 10), (SWA_TILES, KC, 11)):
                for c in range(2):
                    lo, hi = c * HD, (c + 1) * HD
                    ins = dve.scalar_tensor_tensor(q_swa[lo:hi, c, a:b, :], raw2[lo:hi, a:b, :],
                                                   small[lo:hi, g:g + 1], sq2[lo:hi, a:b, :], ALU.mult, ALU.mult)
                    at_point(ins, "q_swa") if (a and c) else do(ins)
            dve.wait_ge(alibi_in, 16)

            def swa_extra(u):
                h = SWA_ORDER[u]
                slope = float(np.float32(2.0) ** np.float32(-8.0 * (h + 1) / SWA_HEADS))
                return dict(bias_ap=alibi[:, :, :], slope=slope, sink=bc[:, 4 * HD + h:4 * HD + h + 1])

            attention("swa", SWA_HEADS, 1, 2, swa_extra, half_tile(0))
            attention("memb", MEM_HEADS, 1, 2, lambda u: {}, half_tile(SWA_TILES))
            add_x("outb")
            mlp("b")


def chunked(w):
    k, n = w.shape
    c = w.reshape(k // D, KC, P, n // CW, CW).transpose(3, 0, 2, 1, 4)
    return [c[j, g].reshape(P, KC * CW) for j in range(n // CW) for g in range(k // D)]


def tiles(v):
    return v.reshape(-1, P).T


def layout(i):
    w_in = np.split(i["w_in"][0], 8, axis=1)
    cb, cc, cx, q, k, v, gc, ga = w_in
    ckv = i["w_ckv"][0]
    heads = np.concatenate([np.arange(h * HD, (h + 1) * HD) for h in SWA_ORDER])
    order = np.concatenate([heads, np.arange(SWA_HEADS * HD, D)])
    parts = {"q": q, "k": k, "v": v, "cx": cx, "cc": cc, "cb": cb, "gc": gc, "ga": ga,
             "ck": ckv[:, :D], "cv": ckv[:, D:], "cout": i["w_conv_out"][0], "aout": i["w_attn_out"][0],
             "mixo": i["w_mix_out"][0], "cq": i["w_cq"][0], "co": i["w_co"][0], "pq": i["w_pq"][0],
             "mkva": i["w_mem_kv_2"][0], "mkvb": i["w_mem_kv_2"][1], "kvb": i["w_kv_2"],
             "ina": i["w_in_2"][0], "inb": i["w_in_2"][1][:, order],
             "outa": i["w_out_2"][0], "outb": i["w_out_2"][1][order],
             "upa": i["w_up_2"][0], "upb": i["w_up_2"][1], "downa": i["w_down_2"][0], "downb": i["w_down_2"][1]}
    made = {name: chunked(w) for name, w in parts.items()}
    taken = {}
    stream = np.empty((NCHUNK, P, KC * CW), np.float32)
    for n, c in enumerate(CHUNKS):
        stream[n] = made[c][taken.get(c, 0)]
        taken[c] = taken.get(c, 0) + 1

    def twice(g):
        return np.concatenate([g, g]).reshape(P, 1)

    columns = {"mix": tiles(i["norm_mix_g"][0]), "cross": tiles(i["norm_cross_g"][0]),
               "mem": tiles(i["norm_mem_g"][0]), "ffn": tiles(i["norm_ffn_g"][0]),
               "mixa": tiles(i["norm_mix_2"][0]), "mixb": tiles(i["norm_mix_2"][1]),
               "mlpa": tiles(i["norm_mlp_2"][0]), "mlpb": tiles(i["norm_mlp_2"][1]), "kv": tiles(i["kv_norm_2"]),
               "mem2a": tiles(i["mem_norm_2"][0]), "mem2b": tiles(i["mem_norm_2"][1]),
               "conv": tiles(i["conv_w"][0]), "subln": i["subln_g"][0].reshape(P, 1),
               "pool": tiles(i["pool_scale_2"][0]), "kn": twice(i["k_norm_2"]), "qn": twice(i["q_norm_2"][0]),
               "mqna": twice(i["mem_q_norm_2"][0]), "mqnb": twice(i["mem_q_norm_2"][1]),
               "mkna": twice(i["mem_k_norm_2"][0]), "mknb": twice(i["mem_k_norm_2"][1])}
    vecs = np.concatenate([columns[n] for n in VEC], axis=1)
    bc = np.concatenate([i["lambda_q1"][0], i["lambda_k1"][0], i["lambda_q2"][0], i["lambda_k2"][0],
                         i["sinks_2"][0]]).reshape(1, NBC)
    n = np.arange(S)
    big = np.maximum(n, 1).astype(np.float32)
    exact = BUCKETS // 2
    large = exact + (np.log(big / exact) / math.log(MAX_DISTANCE / exact) * (BUCKETS - exact)).astype(np.int32)
    bucket = np.where(n < exact, n, np.minimum(large, BUCKETS - 1))
    onehot = np.zeros((BUCKETS + 1, 2 * S), np.float32)
    onehot[bucket[::-1], n] = 1.0
    onehot[BUCKETS, S:] = 1.0
    rel = np.concatenate([i["rel_bias"], np.full((1, HEADS), MASKED, np.float32)])
    pos = np.arange(P)
    dist = P * np.arange(TB)[None, :, None] + pos[:, None, None] - n[None, None, :]
    alibi = np.where((dist >= 0) & (dist < P), -dist, -1e36).astype(np.float32)
    same = (pos[:, None] // HD == pos[None, :] // HD)
    consts = np.concatenate([np.eye(P), np.full((P, P), 1.0 / P), same / HD,
                             np.tile(np.arange(TOPK), (P, 1)), alibi.reshape(P, -1)], axis=1).astype(np.float32)
    window = np.repeat(np.array(POOL_WINDOWS), POOL_GROUP)
    cnt = 1.0 / np.minimum(n[None, :] + 1, window[:, None])
    cnt = cnt.reshape(SWA_TILES, P, S).transpose(1, 0, 2).reshape(P, -1).astype(np.float32)
    pool_w = np.zeros((2, 2 * POOL_GROUP, 2 * POOL_GROUP), np.float32)
    for g in range(len(POOL_WINDOWS)):
        a = g % 2 * POOL_GROUP
        pool_w[g // 2, a:a + POOL_GROUP, a:a + POOL_GROUP] = i["pool_w_2"][0, g]
    pool_w = np.concatenate([pool_w[g, a * P:(a + 1) * P, o * P:(o + 1) * P]
                             for g in range(2) for a, o in POOL_BLOCKS], axis=1)
    keys = i["sub_keys"][0].transpose(3, 1, 0, 2).reshape(P, -1)
    return dict(x_in=i["x"][0], mem_in=i["mem"][0], mem2_in=i["mem_2"][0], wstream=stream,
                experts=np.concatenate([i["peer_u"][0], i["peer_v"][0]], axis=1), vecs_in=vecs, bc_in=bc,
                final_g=i["final_g"].reshape(1, D), rel_in=rel, keys_in=keys, pool_in=pool_w,
                consts_in=consts, onehot_in=onehot, cnt_in=cnt)


def kernel(**inputs):
    import concourse.bacc as bacc
    from concourse.bass_utils import run_bass_kernel_spmd

    nc = bacc.Bacc("TRN2", target_bir_lowering=False, num_devices=1)
    arrays, args = {}, {}
    for name, a in layout({k: np.asarray(v) for k, v in inputs.items()}).items():
        arrays[name] = np.ascontiguousarray(a)
        args[name] = nc.dram_tensor(name, a.shape, F32, kind="ExternalInput").ap()
    args["scratch"] = nc.dram_tensor("scratch", (HEADS, P * (2 * S + 1)), F32, kind="Internal").ap()
    args["out"] = nc.dram_tensor("out_dram", (S, D), F32, kind="ExternalOutput").ap()
    build(nc, **args)
    r = run_bass_kernel_spmd(nc, [arrays], core_ids=[0])
    return r.results[0]["out_dram"].reshape(1, S, D)
```

```python
import math
from contextlib import ExitStack

import numpy as np

import concourse.bass as bass
from concourse import mybir

F32 = mybir.dt.float32
F32R = mybir.dt.float32r
I32 = mybir.dt.int32
U32 = mybir.dt.uint32
ALU = mybir.AluOpType
ACT = mybir.ActivationFunctionType
AX = mybir.AxisListType

P = 128
D = 1024
S = 256
KC = D // P
TB = S // P
CW = 512
HEADS = 8
HD = 64
CROSS_HEADS = 4
BUCKETS = 32
MAX_DISTANCE = 128
PH = 8
TOPK = 16
NKEYS = 128
NEXP = NKEYS * NKEYS
PAIRS = PH * TOPK
SWA_HEADS = 12
SWA_TILES = SWA_HEADS * HD // P
MEM_HEADS = 4
POOL_WINDOWS = (2, 4, 8, 16)
POOL_GROUP = SWA_HEADS * HD // len(POOL_WINDOWS)
FF_TILES = 4 * D // P
LAM_INIT = 0.8 - 0.6 * math.exp(0.0)
MASKED = -1e30
HW = CW // 2
RAW = 3
HI = 3
LO = 2
GSLOTS = 8
SWA_ORDER = [h for j in range(SWA_TILES) for h in (6 * (j // 3) + j % 3, 6 * (j // 3) + 3 + j % 3)]
POOL_BLOCKS = [(0, 0), (1, 0), (0, 1), (1, 1), (2, 1), (1, 2), (2, 2)]

VEC = {}
for _name, _n in [("mix", 8), ("cross", 8), ("mem", 8), ("ffn", 8), ("mixa", 8), ("mixb", 8), ("mlpa", 8),
                  ("mlpb", 8), ("kv", 8), ("mem2a", 8), ("mem2b", 8), ("conv", 24), ("subln", 1),
                  ("pool", 6), ("kn", 1), ("qn", 1), ("mqna", 1), ("mqnb", 1), ("mkna", 1), ("mknb", 1)]:
    VEC[_name] = (sum(n for _, n in VEC.values()), _n)
NVEC = sum(n for _, n in VEC.values())
NBC = 4 * HD + SWA_HEADS

CHUNKS = (["q", "q", "k", "k", "v", "v", "cx", "cx", "cc", "cc", "cb", "cb", "gc", "gc", "ga", "ga"]
          + ["ck", "ck", "cv", "cv", "mkva", "mkvb", "cout", "cout", "aout", "aout", "mixo", "mixo"]
          + ["cq", "cq", "co", "co", "pq", "pq", "pq", "pq"]
          + ["ina", "ina", "outa", "outa"] + ["upa"] * 8 + ["downa"] * 8
          + ["kvb", "inb", "inb", "outb", "outb"] + ["upb"] * 8 + ["downb"] * 8)
NCHUNK = len(CHUNKS)
NHALF = 2 * NCHUNK
SPLITS = ["u", "o", "merged"] + [f"hidden{l}{g}" for l in "ab" for g in range(4)]


def plan():
    lin, last, misc = {}, {}, {}
    half = 0
    seen = {}
    for c in CHUNKS:
        i = seen.get(c, 0)
        seen[c] = i + 1
        for j in range(2):
            half += 1
            key = (c, 2 * (i % 2) + j) if c.startswith("down") else (c, 2 * i + j)
            lin.setdefault(key, len(lin))
            last[key] = half

    def m(*name):
        misc[name] = len(misc)

    def norm(n):
        for tb in range(TB):
            for h in range(2):
                m("xT", n, tb, h)

    def attention(kind, items, group, lag):
        for i in range(min(lag, items)):
            for g in range(group):
                m("S", kind, i * group + g)
        for i in range(items):
            if i + lag < items:
                for g in range(group):
                    m("S", kind, (i + lag) * group + g)
            if i:
                m("O", kind, i - 1)
            m("T", kind, i)
        m("O", kind, items - 1)

    m("bias")
    norm("mix")
    attention("diff", HEADS, 2, 1)
    norm("mem")
    for j in range(4):
        m("sub", j)
    norm("mem2")
    for l in "ab":
        m("mkr", l)
    norm("cross")
    attention("cross", CROSS_HEADS, 1, 2)
    norm("ffn")
    for tb in range(TB):
        for j in range(4):
            m("sc", tb, j)
    norm("mixa")
    m("mqr", "a")
    for g in range(2):
        for j in range(3):
            m("pool", g, j)
    attention("mema", MEM_HEADS, 1, 2)
    norm("mlpa")
    norm("mixb")
    m("kr")
    for j in range(4):
        m("qr", j)
    attention("swa", SWA_HEADS, 1, 2)
    attention("memb", MEM_HEADS, 1, 2)
    norm("mlpb")
    return lin, last, misc


def build(nc, x_in, mem_in, mem2_in, wstream, experts, vecs_in, bc_in, final_g, rel_in, keys_in, pool_in,
          consts_in, onehot_in, cnt_in, scratch, out):
    LIN, LAST, MISC = plan()
    ctx = ExitStack()
    with ctx:
        def sb(name, shape, dt=F32):
            return ctx.enter_context(nc.sbuf_tensor(name, shape, dt))

        sems = {}

        def sem(name):
            sems[name] = ctx.enter_context(nc.semaphore(name))
            return sems[name]

        raw = sb("raw", [P, RAW, KC, HW])
        w_hi = sb("w_hi", [P, HI, KC, HW], F32R)
        w_lo = sb("w_lo", [P, LO, KC, HW], F32R)
        x = sb("x", [P, TB, D])
        xn = sb("xn", [P, TB, D])
        op_hi = sb("op_hi", [P, 2, KC, S], F32R)
        op_lo = sb("op_lo", [P, 2, KC, S], F32R)
        memk = sb("memk", [P, 2, 2, S])
        memv = sb("memv", [P, 2, TB, S])
        vecs = sb("vecs", [P, NVEC])
        bc = sb("bc", [P, NBC])
        consts = sb("consts", [P, 3 * P + TOPK])
        stat = sb("stat", [P, 60])
        arena = sb("arena", [P, 21508])

        ident = consts[:, 0:P]
        mean128 = consts[:, P:2 * P]
        mean64 = consts[:, 2 * P:3 * P]
        iota16 = consts[:, 3 * P:3 * P + TOPK]

        def part(at, *shape):
            n = int(np.prod(shape))
            v = arena[:, at:at + n]
            if len(shape) == 2:
                v = v.rearrange("p (a b) -> p a b", a=shape[0])
            if len(shape) == 3:
                v = v.rearrange("p (a b c) -> p a b c", a=shape[0], b=shape[1])
            if len(shape) == 4:
                v = v.rearrange("p (a b c d) -> p a b c d", a=shape[0], b=shape[1], c=shape[2])
            return v

        prob = part(18432, 4, TB, S)
        prob_t = part(20480, 2, 2, S)
        q_half = part(0, 2, HEADS, S)
        k_diff = part(4096, HEADS, S)
        v_diff = part(6144, TB, D)
        u_conv = part(8192, KC, S)
        conv = part(10240, KC, S)
        gate_c = part(12288, KC, S)
        gate_a = part(10240, KC, S)
        bias = part(14336, HEADS, TB, S)
        o_diff = part(0, KC, S)
        rel_sb = part(12288, 512)[0:BUCKETS + 1, 0:8]
        onehot = part(12800, 512)[0:BUCKETS + 1, :]
        bias_row = part(13312, 512)[0:8, :]
        k_cross = part(2048, KC, S)
        v_cross = part(4096, TB, D)
        q_cross = part(6144, KC, S)
        sq = part(14336, KC, S)
        junk = part(16384, KC, S)
        q_peer = part(0, 2 * PH, S)
        keys = part(4096, 2 * PH, NKEYS)
        rows = part(0, GSLOTS, 2 * D)
        score = part(16384, TB, 2 * PH, NKEYS)
        u_pool = part(0, SWA_TILES, S)
        win = part(2048, 2, SWA_TILES, S)
        cnt = part(5120, SWA_TILES, S)
        pool_w = part(6656, len(POOL_BLOCKS) * 2 - 0, P)
        mq_half = part(8448, 2, 2, S)
        sq2 = part(11520, KC, S)
        raw2 = part(13568, KC, S)
        q_swa = part(0, 2, KC, S)
        k_swa = part(4096, 2, S)
        v_swa = part(4608, TB, S)
        alibi = part(5120, TB, S)
        hidden = part(0, FF_TILES, S)
        gfin = part(16384, D)

        half_score = part(20480, 2, NKEYS)
        half_vals = part(20736, 2, TOPK)
        half_idx = part(20768, 2, TOPK).bitcast(U32)
        half_idxf = part(20800, 2, TOPK)
        cand = part(20832, TOPK, TOPK)
        top_vals = part(21088, TOPK)
        top_pos = part(21104, TOPK).bitcast(U32)
        top_half = part(21120, 2, TOPK).bitcast(U32)
        top_halff = part(21152, 2, TOPK)
        pick = part(21184, TOPK, TOPK)
        found = part(21440, 2, TOPK)
        top_less = part(21472, TOPK)
        top_e = part(21488, TOPK)
        hsum = part(21504, 1)
        hinv = part(21505, 1)
        diag = xn[:, 0, :].rearrange("p (s n) -> p s n", s=GSLOTS)
        expert = xn[:, 1, 0:256].rearrange("p (t n) -> p t n", t=TB).bitcast(I32)
        weight = xn[:, 1, 256:512].rearrange("p (t n) -> p t n", t=TB)
        zeros = xn[:, 1, 640:768]
        stage = xn[:, 1, 768:784].rearrange("p (t n) -> p t n", t=2).bitcast(I32)
        dots = xn[:, 1, 784:792]
        gact = xn[:, 1, 792:800]
        wact = xn[:, 1, 800:808]
        nmax = sb("nmax", [P, 4, 2])
        ssum = sb("ssum", [P, 4, 2])
        rsum = sb("rsum", [P, 4, 2])
        esink = sb("esink", [P, 4, 2])
        small = sb("small", [P, 16])

        bank_pairs = [ctx.enter_context(nc.psum_tensor(f"banks{i}", [P, 2, 512], F32)) for i in range(4)]
        banks = [bank_pairs[i // 2][:, i % 2, :] for i in range(8)]

        raw_in = [sem(f"raw_in{i}") for i in range(RAW)]
        hi_ready = sem("hi_ready")
        lo_ready = sem("lo_ready")
        norm_hi = sem("norm_hi")
        split_hi = sem("split_hi")
        split_lo = sem("split_lo")
        half_done = sem("half_done")
        lin_free = [sem(f"lin_free{i}") for i in range(4)]
        misc_full = sem("misc_full")
        misc_free = [sem(f"misc_free{i}") for i in range(4)]
        x_in_s = sem("x_in_s")
        mem_in_s = sem("mem_in_s")
        mem2_in_s = sem("mem2_in_s")
        const_in = sem("const_in")
        row_in = sem("row_in")
        bias_out = sem("bias_out")
        bias_in = sem("bias_in")
        keys_in_s = sem("keys_in_s")
        gfin_in = sem("gfin_in")
        pool_in_s = sem("pool_in_s")
        alibi_in = sem("alibi_in")
        out_s = sem("out_s")
        bias_row_s = sem("bias_row_s")
        dve_chain = sem("dve_chain")
        act_chain = sem("act_chain")
        pool_chain = sem("pool_chain")
        squares = sem("squares")
        mean_sq = sem("mean_sq")
        rstd_s = sem("rstd_s")
        xn_ready = sem("xn_ready")
        max_ready = sem("max_ready")
        exp_ready = sem("exp_ready")
        p_ready = sem("p_ready")
        zero_ready = sem("zero_ready")
        lam_sums = sem("lam_sums")
        lam_exps = sem("lam_exps")
        gate_exp = sem("gate_exp")
        sub_sq = sem("sub_sq")
        sub_root = sem("sub_root")
        head_sq = sem("head_sq")
        head_ms = sem("head_ms")
        head_root = sem("head_root")
        ready = sem("ready")
        top_chain = sem("top_chain")
        top_passed = sem("top_passed")
        top_exp_in = sem("top_exp_in")
        top_exp = sem("top_exp")
        experts_ready = sem("experts_ready")
        gathered = [sem(f"gathered{i}") for i in range(GSLOTS)]
        staged = sem("staged")
        issued = sem("issued")
        hidden_ready = sem("hidden_ready")
        peer_zero = sem("peer_zero")
        hf_ready = sem("hf_ready")
        dot_ready = sem("dot_ready")
        gelu_ready = sem("gelu_ready")
        wact_ready = sem("wact_ready")
        diag_ready = sem("diag_ready")
        row_free = sem("row_free")
        acc_ready = sem("acc_ready")
        acc_used = sem("acc_used")

        count = {}

        def chain(eng, ins, s):
            count[id(s)] = count.get(id(s), 0) + 1
            ins.then_inc(s, 1)
            eng.wait_ge(s, count[id(s)])

        token_rows = bank_pairs[1], bank_pairs[2]
        row_sums = bank_pairs[0], bank_pairs[3]

        def lin_bank(key):
            return banks[LIN[key] % 4]

        def misc_bank(key):
            return banks[4 + MISC[key] % 4]

        def wait_lin(eng, key):
            eng.wait_ge(half_done, LAST[key])

        def wait_misc(eng, key):
            eng.wait_ge(misc_full, MISC[key] + 1)

        def empty_lin(ins, key):
            ins.then_inc(lin_free[LIN[key] % 4], 1)

        def empty_misc(ins, key):
            ins.then_inc(misc_free[MISC[key] % 4], 1)

        def lin_emptied(eng, key):
            eng.wait_ge(lin_free[LIN[key] % 4], LIN[key] // 4 + 1)

        def misc_emptied(eng, key):
            eng.wait_ge(misc_free[MISC[key] % 4], MISC[key] // 4 + 1)

        def gain(name):
            a, n = VEC[name]
            return vecs[:, a:a + n]

        NORMS = ["mix", "mem", "mem2", "cross", "ffn", "final", "mixa", "mlpa", "mixb", "mlpb"]

        def stats(n):
            a = 6 * NORMS.index(n)
            return stat[:, a:a + 2], stat[:, a + 2:a + 4], stat[:, a + 4:a + 6]

        def norm_tiles(n):
            done = [m for m in NORMS[:NORMS.index(n) + 1] if m != "final"]
            return sum(8 if m in ("mem2", "mixb") else 4 for m in done)

        UNIT0, ITEM0 = {}, {}
        n_units = n_items = 0
        for kind, items, group in (("diff", HEADS, 2), ("cross", CROSS_HEADS, 1), ("mema", MEM_HEADS, 1),
                                   ("swa", SWA_HEADS, 1), ("memb", MEM_HEADS, 1)):
            UNIT0[kind], ITEM0[kind] = n_units, n_items
            n_units += items * group
            n_items += items

        POINTS = ["zeros", "kmem_a", "kmem_b", "h", "d_pool", "mq", "k_swa", "q_swa"]

        def at_point(ins, name):
            assert POINTS[count.setdefault("point", 0)] == name, name
            count["point"] += 1
            ins.then_inc(ready, 1)

        def point(eng, name):
            eng.wait_ge(ready, POINTS.index(name) + 1)

        block = ctx.enter_context(nc.Block())

        @block.sync
        def _(sp):
            def load(n, slot):
                sp.dma_start(raw[:, slot, :, :], wstream[n].rearrange("p (a b) -> p a b", a=KC))\
                  .then_inc(raw_in[slot], 16)

            sp.dma_start(x[:, :, :], x_in.rearrange("(t p) d -> p t d", p=P)).then_inc(x_in_s, 16)
            for n in range(RAW):
                load(n, n)
            misc_emptied(sp, ("bias",))
            head = P * (2 * S + 1)
            sp.dma_start(bass.AP(scratch.tensor, 0, [[head, HEADS], [2 * S + 1, P], [1, 2 * S]]),
                         bias_row.unsqueeze(1).broadcast_to([HEADS, P, 2 * S])).then_inc(bias_out, 16)
            sp.wait_ge(bias_out, 16)
            for qb in range(TB):
                sp.dma_start(bias[:, :, qb, :], bass.AP(scratch.tensor, S - 1 - P * qb,
                                                        [[2 * S, P], [head, HEADS], [1, S]])).then_inc(bias_in, 16)
            with sp.Fori(1, NHALF // RAW) as i:
                for slot in range(RAW):
                    sp.wait_ge(lo_ready, i * RAW + (slot + 1 - RAW))
                    sp.dma_start(raw[:, slot, :, :],
                                 wstream[bass.ds(i * RAW + slot, 1)].rearrange("o p (a b) -> p (o a) b", a=KC))\
                      .then_inc(raw_in[slot], 16)
            for n in range(NHALF - NHALF % RAW, NHALF):
                sp.wait_ge(lo_ready, n + 1 - RAW)
                load(n, n % RAW)
            for j in range(4):
                lin_emptied(sp, ("downb", j))
            sp.dma_start(out.rearrange("(t p) d -> p t d", p=P), x[:, :, :]).then_inc(out_s, 16)
            sp.wait_ge(out_s, 16)

        @block.gpsimd
        def _(pool):
            pool.memset(small[:, 14:16], -0.5).then_inc(pool_chain, 1)
            pool.wait_ge(pool_chain, 1)

            def rstd(n):
                _, ms, rs = stats(n)
                pool.wait_ge(mean_sq, NORMS.index(n) + 1)
                pool.tensor_tensor(rs, ms, small[:, 14:16], ALU.pow).then_inc(rstd_s, 1)

            halves = [0]

            def low_parts(upto):
                for n in range(halves[0], upto):
                    pool.wait_ge(hi_ready, n + 1)
                    if n >= LO:
                        pool.wait_ge(half_done, n - LO + 1)
                    pool.tensor_tensor(w_lo[:, n % LO, :, :], raw[:, n % RAW, :, :],
                                       w_hi[:, n % HI, :, :].bitcast(F32), ALU.subtract).then_inc(lo_ready, 1)
                halves[0] = upto

            for n, upto in (("mix", 2), ("mem", 34), ("mem2", 38), ("cross", 58), ("ffn", 66)):
                low_parts(upto)
                rstd(n)
            low_parts(74)
            wait_misc(pool, ("sc", TB - 1, 3))
            for tb in range(TB):
                with pool.Fori(0, PH) as h:
                    pool.wait_ge(experts_ready, h + (tb * PH + 1))
                    for half in range(2):
                        turn = h * 2 + (half + tb * (PAIRS // GSLOTS))
                        pool.tensor_copy(stage[:, half, :],
                                         expert[:, tb, bass.ds(h * TOPK + half * GSLOTS, GSLOTS)])\
                            .then_inc(staged, 1)
                        pool.wait_ge(staged, turn + 1)
                        pool.sem_inc(issued, 1)
                        for s in range(GSLOTS):
                            pool.wait_ge(row_free, turn * GSLOTS + (s + 1))
                            pool.sem_inc(issued, 1)
                            pool.indirect_dma_start(
                                rows[:, s, :], None, experts,
                                bass.IndirectOffsetOnAxis(ap=stage[:, half, s:s + 1], axis=0))\
                                .then_inc(gathered[s], 16)
            for n, upto in (("final", 74), ("mixa", 74), ("mlpa", 82), ("mixb", 114), ("mlpb", 124)):
                low_parts(upto)
                rstd(n)
            low_parts(NHALF)

        @block.scalar
        def _(act):
            act.dma_start(consts[:, :], consts_in[:, 0:3 * P + TOPK]).then_inc(const_in, 16)
            act.dma_start(vecs[:, :], vecs_in).then_inc(const_in, 16)
            act.dma_start(bc[:, :], bass.AP(bc_in.tensor, 0, [[0, P], [1, NBC]])).then_inc(const_in, 16)
            act.dma_start(rel_sb, rel_in).then_inc(row_in, 16)
            act.dma_start(onehot, onehot_in).then_inc(row_in, 16)

            halves = [0]

            def high_parts(upto):
                for n in range(halves[0], min(upto, NHALF)):
                    act.wait_ge(raw_in[n % RAW], 16 * (n // RAW + 1))
                    if n >= HI:
                        act.wait_ge(half_done, n - HI + 1)
                    act.activation(w_hi[:, n % HI, :, :], raw[:, n % RAW, :, :], ACT.Copy).then_inc(hi_ready, 1)
                halves[0] = max(halves[0], upto)

            def product(key):
                high_parts(LAST[key] + 2)
                wait_lin(act, key)

            def sum_squares(n, src):
                ss = stats(n)[0]
                for tb in range(TB):
                    act.activation(xn[:, tb, :], src[:, tb, :], ACT.Square, accum_out=ss[:, tb:tb + 1])\
                       .then_inc(squares, 1)

            def x_updated(weight):
                high_parts(LAST[(weight, 3)] + 2)
                for j in range(4):
                    lin_emptied(act, (weight, j))
                high_parts(LAST[(weight, 3)] + HI)

            def xn_free(n):
                wait_misc(act, ("xT", n, 1, 1))

            def exps(kind, u):
                g = UNIT0[kind] + u
                r = g % 4
                act.wait_ge(max_ready, g + 1)
                in_psum = kind in ("cross", "mema", "memb")
                src = misc_bank(("S", kind, u)).rearrange("p (a b) -> p a b", a=TB) if in_psum \
                    else prob[:, r]
                if kind == "swa":
                    h = SWA_ORDER[u]
                    sink = bc[:, 4 * HD + h:4 * HD + h + 1]
                    chain(act, act.activation(esink[:, r, :], nmax[:, r, :], ACT.Exp, bias=sink), act_chain)
                for qb in range(TB):
                    e = act.activation(prob[:, r, qb, :], src[:, qb, :], ACT.Exp,
                                       bias=nmax[:, r, qb:qb + 1], accum_out=ssum[:, r, qb:qb + 1])
                    if in_psum and qb == TB - 1:
                        empty_misc(e, ("S", kind, u))
                    else:
                        e.then_inc(exp_ready, 1)

            def turned(kind, i):
                wait_misc(act, ("T", kind, i))
                if i >= 2:
                    wait_misc(act, ("O", kind, i - 2))
                e = act.activation(prob_t[:, (ITEM0[kind] + i) % 2, :, :],
                                   misc_bank(("T", kind, i)).rearrange("p (a b) -> p a b", a=2), ACT.Copy)
                empty_misc(e, ("T", kind, i))

            def free_prob(kind, i, group):
                j = i - 4 // group
                if j >= 0:
                    wait_misc(act, ("T", kind, j))

            def attention(kind, items, group, lag, fill=()):
                start = halves[0]
                for i in range(min(lag, items)):
                    for g in range(group):
                        exps(kind, i * group + g)
                for i in range(items):
                    if i + lag < items:
                        for g in range(group):
                            free_prob(kind, i + lag, group)
                            exps(kind, (i + lag) * group + g)
                    if i < len(fill):
                        high_parts(start + 2 * (i + 1))
                        if fill[i]:
                            fill[i]()
                    turned(kind, i)

            def copy_lin(key, dst, scale=None):
                product(key)
                src = lin_bank(key)
                if len(dst.shape) == 3:
                    src = src.rearrange("p (a b) -> p a b", a=2)
                e = act.activation(dst, src, ACT.Copy, scale=scale) if scale is not None \
                    else act.activation(dst, src, ACT.Copy)
                empty_lin(e, key)

            act.wait_ge(x_in_s, 16)
            sum_squares("mix", x)
            high_parts(HI)
            point(act, "zeros")
            for j in range(4):
                product(("q", j))
                src = lin_bank(("q", j)).rearrange("p (a b) -> p a b", a=2)
                chain(act, act.activation(q_half[0:HD, 0, 2 * j:2 * j + 2, :], src[0:HD], ACT.Copy,
                                          scale=HD ** -0.5), act_chain)
                e = act.activation(q_half[HD:P, 1, 2 * j:2 * j + 2, :], src[HD:P], ACT.Copy, scale=HD ** -0.5)
                empty_lin(e, ("q", j))
            for j in range(4):
                copy_lin(("k", j), k_diff[:, 2 * j:2 * j + 2, :])
            for j in range(4):
                copy_lin(("v", j), v_diff[:, :, j * HW:(j + 1) * HW])
            for j in range(4):
                copy_lin(("cx", j), u_conv[:, 2 * j:2 * j + 2, :])
            xn_free("mix")
            act.dma_start(xn[:, :, :], mem_in.rearrange("(t p) d -> p t d", p=P)).then_inc(mem_in_s, 16)
            act.wait_ge(lam_sums, 2)
            act.activation(small[:, 2:4], small[:, 0:2], ACT.Exp).then_inc(lam_exps, 1)

            def gate(name, dst, i):
                def f():
                    for j in (2 * i, 2 * i + 1):
                        product((name, j))
                        e = act.activation(dst[:, 2 * j:2 * j + 2, :],
                                           lin_bank((name, j)).rearrange("p (a b) -> p a b", a=2),
                                           ACT.Exp, scale=-1.0)
                        empty_lin(e, (name, j))
                return f

            attention("diff", HEADS, 2, 1, [None] * 4 + [gate("gc", gate_c, 0), gate("gc", gate_c, 1),
                                                         gate("ga", gate_a, 0), gate("ga", gate_a, 1)])
            def memory_squares(n):
                ss = stats(n)[0]
                for tb in range(TB):
                    act.activation(junk[:, 4 * tb:4 * tb + 4, :], xn[:, tb, :].rearrange("p (a b) -> p a b", a=4),
                                   ACT.Square, accum_out=ss[:, tb:tb + 1]).then_inc(squares, 1)

            act.wait_ge(mem_in_s, 16)
            memory_squares("mem")
            misc_emptied(act, ("O", "diff", HEADS - 1))
            act.activation(sq[:, :, :], o_diff[:, :, :], ACT.Square).then_inc(sub_sq, 1)
            for j in range(4):
                wait_misc(act, ("sub", j))
                e = act.activation(sq[:, 2 * j:2 * j + 2, :],
                                   misc_bank(("sub", j)).rearrange("p (a b) -> p a b", a=2), ACT.Sqrt,
                                   bias=small[:, 8:9])
                empty_misc(e, ("sub", j))
            xn_free("mem")
            act.dma_start(xn[:, :, :], mem2_in.rearrange("(t p) d -> p t d", p=P)).then_inc(mem2_in_s, 16)
            for j in range(4):
                copy_lin(("ck", j), k_cross[:, 2 * j:2 * j + 2, :])
            act.wait_ge(mem2_in_s, 16)
            act.wait_ge(squares, 4)
            memory_squares("mem2")
            for j in range(4):
                copy_lin(("cv", j), v_cross[:, :, j * HW:(j + 1) * HW])
            for l in range(2):
                copy_lin(("mkv" + "ab"[l], 0), memk[:, l, :, :])
                copy_lin(("mkv" + "ab"[l], 1), memv[:, l, :, :])
            act.wait_ge(squares, 6)
            for l in range(2):
                key = ("mkr", "ab"[l])
                lin_emptied(act, ("mkv" + "ab"[l], 0))
                act.activation(junk[:, 2 * l:2 * l + 2, :], memk[:, l, :, :], ACT.Square).then_inc(head_sq, 1)
                wait_misc(act, key)
                e = act.activation(junk[:, 4 + 2 * l:6 + 2 * l, :],
                                   misc_bank(key).rearrange("p (a b) -> p a b", a=2), ACT.Sqrt, bias=small[:, 9:10])
                empty_misc(e, key)
            x_updated("mixo")
            xn_free("mem2")
            sum_squares("cross", x)
            for j in range(4):
                copy_lin(("cq", j), q_cross[:, 2 * j:2 * j + 2, :], scale=(D // CROSS_HEADS) ** -0.5)
            attention("cross", CROSS_HEADS, 1, 2)
            x_updated("co")
            xn_free("cross")
            sum_squares("ffn", x)
            wait_misc(act, ("O", "cross", CROSS_HEADS - 1))
            act.dma_start(keys[:, :, :], keys_in.rearrange("p (a b) -> p a b", a=2 * PH)).then_inc(keys_in_s, 16)
            for j in range(8):
                copy_lin(("pq", j), q_peer[:, 2 * j:2 * j + 2, :])
            for tb in range(TB):
                for j in range(4):
                    wait_misc(act, ("sc", tb, j))
                    e = act.activation(score[:, tb, 4 * j:4 * j + 4, :],
                                       misc_bank(("sc", tb, j)).rearrange("p (a b) -> p a b", a=4), ACT.Copy)
                    empty_misc(e, ("sc", tb, j))
            act.sem_inc(gelu_ready, 1)

            def top_exps(tb, h):
                act.wait_ge(top_exp_in, h + (tb * PH + 1))
                act.activation(top_e, top_less, ACT.Exp, accum_out=hsum).then_inc(top_exp, 1)

            def weigh_rows(tb, h):
                for j in range(0, TOPK, 2):
                    s = j % GSLOTS
                    done = h * TOPK + (tb * PAIRS + j)
                    act.wait_ge(dot_ready, done + 2)
                    act.activation(gact[:, s:s + 2], dots[:, s:s + 2], ACT.Gelu).then_inc(gelu_ready, 1)
                    act.wait_ge(gelu_ready, h * (TOPK // 2) + (tb * (PAIRS // 2) + j // 2 + 2))
                    act.wait_ge(row_free, done + 2)
                    for k in range(2):
                        at = h * TOPK + (j + k)
                        act.activation(wact[:, s + k:s + k + 1], gact[:, s + k:s + k + 1], ACT.Copy,
                                       scale=weight[:, tb, at:at + 1] if isinstance(h, int) else
                                       weight[:, tb, bass.ds(at, 1)]).then_inc(wact_ready, 1)
                    act.wait_ge(wact_ready, done + 2)
                    for k in range(2):
                        act.activation(diag[:, s + k, :], ident, ACT.Copy, scale=wact[:, s + k:s + k + 1])\
                           .then_inc(diag_ready, 1)

            top_exps(0, 0)
            for tb in range(TB):
                with act.Fori(0, PH - 1) as h:
                    top_exps(tb, h + 1)
                    weigh_rows(tb, h)
                if tb < TB - 1:
                    top_exps(tb + 1, 0)
                weigh_rows(tb, PH - 1)
            act.wait_ge(acc_used, 4)
            sum_squares("final", x)
            act.dma_start(gfin, bass.AP(final_g.tensor, 0, [[0, P], [1, D]])).then_inc(gfin_in, 16)
            act.dma_start(pool_w, pool_in.rearrange("p (a b) -> p a b", b=P)).then_inc(pool_in_s, 16)
            act.dma_start(cnt[:, :, :], cnt_in.rearrange("p (a b) -> p a b", a=SWA_TILES)).then_inc(pool_in_s, 16)
            point(act, "h")
            sum_squares("mixa", x)

            def head_roots(keys_):
                for j, key in enumerate(keys_):
                    wait_misc(act, key)
                    e = act.activation(sq2[:, 2 * j:2 * j + 2, :],
                                       misc_bank(key).rearrange("p (a b) -> p a b", a=2),
                                       ACT.Sqrt, bias=small[:, 9:10])
                    empty_misc(e, key)

            def mlp(l):
                wt = "up" + l
                for j in range(16):
                    product((wt, j))
                    h = hidden[:, 2 * j:2 * j + 2, :]
                    empty_lin(act.activation(h, lin_bank((wt, j)).rearrange("p (a b) -> p a b", a=2), ACT.Relu),
                              (wt, j))
                    lin_emptied(act, (wt, j))
                    act.activation(h, h, ACT.Square).then_inc(hidden_ready, 1)

            for j in range(3):
                copy_lin(("ina", j), u_pool[:, 2 * j:2 * j + 2, :])
            copy_lin(("ina", 3), raw2[:, 6:8, :])
            lin_emptied(act, ("ina", 3))
            act.activation(sq2[:, 6:8, :], raw2[:, 6:8, :], ACT.Square).then_inc(head_sq, 1)
            wait_misc(act, ("mqr", "a"))
            e = act.activation(sq2[:, 0:2, :], misc_bank(("mqr", "a")).rearrange("p (a b) -> p a b", a=2),
                               ACT.Sqrt, bias=small[:, 9:10])
            empty_misc(e, ("mqr", "a"))
            attention("mema", MEM_HEADS, 1, 2)
            x_updated("outa")
            xn_free("mixa")
            sum_squares("mlpa", x)
            mlp("a")
            x_updated("downa")
            xn_free("mlpa")
            sum_squares("mixb", x)
            act.dma_start(alibi[:, :, :], consts_in[:, 3 * P + TOPK:].rearrange("p (a b) -> p a b", a=TB))\
               .then_inc(alibi_in, 16)
            copy_lin(("kvb", 0), k_swa[:, :, :])
            copy_lin(("kvb", 1), v_swa[:, :, :])
            lin_emptied(act, ("kvb", 0))
            act.activation(sq2[:, 6:8, :], k_swa[:, :, :], ACT.Square).then_inc(head_sq, 1)
            wait_misc(act, ("kr",))
            e = act.activation(sq2[:, 0:2, :], misc_bank(("kr",)).rearrange("p (a b) -> p a b", a=2),
                               ACT.Sqrt, bias=small[:, 9:10])
            empty_misc(e, ("kr",))
            for j in range(4):
                copy_lin(("inb", j), raw2[:, 2 * j:2 * j + 2, :])
            lin_emptied(act, ("inb", 3))
            point(act, "k_swa")
            act.activation(sq2[:, :, :], raw2[:, :, :], ACT.Square).then_inc(head_sq, 1)
            head_roots([("qr", j) for j in range(4)])
            attention("swa", SWA_HEADS, 1, 2)
            attention("memb", MEM_HEADS, 1, 2)
            x_updated("outb")
            xn_free("mixb")
            sum_squares("mlpb", x)
            mlp("b")
            high_parts(NHALF)

        @block.tensor
        def _(pe):
            state = {"half": 0, "misc": 0}

            def fill_misc(key):
                assert MISC[key] == state["misc"], key
                state["misc"] += 1
                j = MISC[key]
                if j >= 4:
                    pe.wait_ge(misc_free[j % 4], j // 4)
                return misc_bank(key)

            def lin_bank_free(key):
                j = LIN[key]
                if j >= 4:
                    pe.wait_ge(lin_free[j % 4], j // 4)

            def half_chunk(by_feature, src, lo_made=None, first=True, last=True):
                n = state["half"]
                state["half"] += 1
                name = CHUNKS[n // 2]
                i = CHUNKS[:n // 2].count(name)
                key = (name, 2 * (i % 2 if name.startswith("down") else i) + n % 2)
                if first:
                    lin_bank_free(key)
                hi, lo = w_hi[:, n % HI, :, :], w_lo[:, n % LO, :, :]
                pe.wait_ge(hi_ready, n + 1)
                for r in range(2):
                    for turn, (w, a) in enumerate(((hi, op_hi), (lo, op_hi), (hi, op_lo))):
                        if r == 0 and turn == 1:
                            pe.wait_ge(lo_ready, n + 1)
                        if r == 0 and turn == 2 and lo_made:
                            lo_made()
                        for kc in range(KC):
                            part_, tokens_ = slice(r * P, (r + 1) * P), slice(r * HW, (r + 1) * HW)
                            start = turn == 0 and kc == 0 and first and (r == 0 or last)
                            stop = turn == 2 and kc == KC - 1 and last
                            l, m = (w[:, kc, part_], a[:, src, kc, :]) if by_feature \
                                else (a[:, src, kc, part_], w[:, kc, :])
                            mm = pe.matmul(lin_bank(key)[:, tokens_], l, m, start=start, stop=stop,
                                           skip_group_check=not (first and last))
                mm.then_inc(half_done, 1)

            def features(src, **k):
                for _ in range(2):
                    half_chunk(True, src, **k)

            def tokens(src, **k):
                for _ in range(2):
                    half_chunk(False, src, **k)

            def keys_values(src, **k):
                half_chunk(True, src, **k)
                half_chunk(False, src, **k)

            def split_made(name):
                pe.wait_ge(split_hi, SPLITS.index(name) + 1)
                return dict(lo_made=lambda: pe.wait_ge(split_lo, SPLITS.index(name) + 1))

            def norm(n):
                pe.wait_ge(xn_ready, 2 * [m for m in NORMS if m != "final"].index(n) + 1)
                for tb in range(TB):
                    if tb:
                        pe.wait_ge(xn_ready, 2 * [m for m in NORMS if m != "final"].index(n) + 2)
                    for h in range(2):
                        b = fill_misc(("xT", n, tb, h))
                        for f in range(4):
                            at = (4 * h + f) * P
                            mm = pe.transpose(b[:, f * P:(f + 1) * P], xn[:, tb, at:at + P], ident)
                        mm.then_inc(misc_full, 1)

            def normed(n):
                def lo_made():
                    for tb in range(TB):
                        for h in range(2):
                            misc_emptied(pe, ("xT", n, tb, h))

                pe.wait_ge(norm_hi, norm_tiles(n))
                return dict(lo_made=lo_made)

            def attention(kind, items, group, lag, scores, values, fill=()):
                def s(u):
                    b = fill_misc(("S", kind, u))
                    for qb in range(TB):
                        pairs = scores(u, qb)
                        for n, (l, r) in enumerate(pairs):
                            mm = pe.matmul(b[:, qb * S:(qb + 1) * S], l, r, start=(n == 0),
                                           stop=(n == len(pairs) - 1))
                    mm.then_inc(misc_full, 1)

                def o(i):
                    misc_emptied(pe, ("T", kind, i))
                    b = fill_misc(("O", kind, i))
                    for e, part_ in enumerate(values(i)):
                        for kb in range(2):
                            mm = pe.matmul(b[:, e * S:(e + 1) * S], part_(kb),
                                           prob_t[:, (ITEM0[kind] + i) % 2, kb, :], start=(kb == 0), stop=(kb == 1))
                    mm.then_inc(misc_full, 1)

                for i in range(min(lag, items)):
                    for g in range(group):
                        s(i * group + g)
                for i in range(items):
                    if i + lag < items:
                        for g in range(group):
                            s((i + lag) * group + g)
                    if i < len(fill) and fill[i]:
                        fill[i]()
                    if i:
                        o(i - 1)
                    r = (UNIT0[kind] + i * group) % 4
                    pe.wait_ge(p_ready, TB * (ITEM0[kind] + i + 1))
                    b = fill_misc(("T", kind, i))
                    for kb in range(2):
                        for qb in range(TB):
                            mm = pe.transpose(b[:, kb * S + qb * P:kb * S + (qb + 1) * P],
                                              prob[:, r, qb, kb * P:(kb + 1) * P], ident)
                    mm.then_inc(misc_full, 1)
                o(items - 1)

            pe.wait_ge(const_in, 48)
            pe.wait_ge(row_in, 32)
            b = fill_misc(("bias",))
            pe.matmul(b[0:8, :], rel_sb, onehot, start=True, stop=True).then_inc(misc_full, 1)
            norm("mix")
            wait_ = normed("mix")
            features(0, **wait_)
            for _ in range(3):
                features(0)
            for _ in range(2):
                tokens(0)
            for _ in range(2):
                features(0)
            for j in range(4):
                lin_emptied(pe, ("q", j))
                lin_emptied(pe, ("k", j))
                lin_emptied(pe, ("v", j))
            attention("diff", HEADS, 2, 1,
                      lambda u, qb: [(q_half[:, u % 2, u // 2, qb * P:(qb + 1) * P], k_diff[:, u // 2, :])],
                      lambda h: [lambda kb: v_diff[:, kb, h * P:(h + 1) * P]],
                      [lambda: features(0)] * 8)
            norm("mem")
            pe.wait_ge(sub_sq, 1)
            for j in range(4):
                b = fill_misc(("sub", j))
                pe.matmul(b, mean128, sq[:, 2 * j:2 * j + 2, :], start=True, stop=True).then_inc(misc_full, 1)
            features(1, **normed("mem"))
            features(1)
            for _ in range(2):
                tokens(1)
            norm("mem2")
            wait_ = normed("mem2")
            keys_values(0, **wait_)
            keys_values(1)
            for l in range(2):
                pe.wait_ge(head_sq, l + 1)
                b = fill_misc(("mkr", "ab"[l]))
                pe.matmul(b, mean64, junk[:, 2 * l:2 * l + 2, :], start=True, stop=True).then_inc(misc_full, 1)
            for name, buf in (("u", 0), ("o", 1)):
                features(buf, **split_made(name))
                features(buf)
            tokens(0, **split_made("merged"))
            tokens(0)
            norm("cross")
            features(1, **normed("cross"))
            features(1)
            for j in range(4):
                lin_emptied(pe, ("ck", j))
                lin_emptied(pe, ("cv", j))
                lin_emptied(pe, ("cq", j))
            attention("cross", CROSS_HEADS, 1, 2,
                      lambda h, qb: [(q_cross[:, 2 * h + e, qb * P:(qb + 1) * P], k_cross[:, 2 * h + e, :])
                                     for e in range(2)],
                      lambda h: [lambda kb, e=e: v_cross[:, kb, (2 * h + e) * P:(2 * h + e + 1) * P]
                                 for e in range(2)])
            for h in range(CROSS_HEADS):
                misc_emptied(pe, ("O", "cross", h))
            for _ in range(2):
                tokens(0)
            norm("ffn")
            features(1, **normed("ffn"))
            for _ in range(3):
                features(1)
            for j in range(8):
                lin_emptied(pe, ("pq", j))
            pe.wait_ge(keys_in_s, 16)
            for tb in range(TB):
                for j in range(4):
                    b = fill_misc(("sc", tb, j))
                    for n in range(4):
                        mm = pe.matmul(b[:, n * P:(n + 1) * P], q_peer[:, 4 * j + n, tb * P:(tb + 1) * P],
                                       keys[:, 4 * j + n, :], start=True, stop=True)
                    mm.then_inc(misc_full, 1)
            for j in range(4):
                misc_emptied(pe, ("sc", TB - 1, j))
            pe.wait_ge(peer_zero, 1)
            pe.sem_inc(row_free, GSLOTS)
            for tb in range(TB):
                for kc in range(KC):
                    for k, half in enumerate((op_hi, op_lo)):
                        mm = pe.matmul(token_rows[tb][:, kc // 4, kc % 4 * P:(kc % 4 + 1) * P],
                                       half[:, 1, kc, tb * P:(tb + 1) * P].bitcast(F32), ident,
                                       start=(k == 0), stop=(k == 1))
                mm.then_inc(hf_ready, 1)
            for tb in range(TB):
                sums = row_sums[tb]
                for n in range(2):
                    pe.matmul(sums[:, n, :], zeros, op_hi[:, 1, 0:2, :].bitcast(F32), start=True, stop=False,
                              skip_group_check=True)
                with pe.Fori(0, PAIRS // GSLOTS) as i:
                    for s in range(GSLOTS):
                        pe.wait_ge(diag_ready, i * GSLOTS + (tb * PAIRS + s + 1))
                        for n in range(2):
                            mm = pe.matmul(sums[:, n, :], diag[:, s, :], rows[:, s, D + n * CW:D + (n + 1) * CW],
                                           start=False, stop=False, skip_group_check=True)
                        mm.then_inc(row_free, 1)
                for n in range(2):
                    mm = pe.matmul(sums[:, n, :], zeros, op_hi[:, 1, 0:2, :].bitcast(F32), start=False, stop=True,
                                   skip_group_check=True)
                mm.then_inc(acc_ready, 1)

            def mlp(l):
                norm("mlp" + l)
                features(0, **normed("mlp" + l))
                for _ in range(7):
                    features(0)
                for g in range(4):
                    k = dict(first=(g == 0), last=(g == 3))
                    tokens((g + 1) % 2, **split_made(f"hidden{l}{g}"), **k)
                    tokens((g + 1) % 2, **k)

            norm("mixa")
            pe.wait_ge(acc_used, 4)
            features(0, **normed("mixa"))
            features(0)
            pe.wait_ge(head_sq, 3)
            b = fill_misc(("mqr", "a"))
            pe.matmul(b, mean64, sq2[:, 6:8, :], start=True, stop=True).then_inc(misc_full, 1)
            point(pe, "d_pool")
            pe.wait_ge(pool_in_s, 32)
            for g in range(2):
                for j in range(3):
                    b = fill_misc(("pool", g, j))
                    ins_ = [(n, a) for n, (a, o) in enumerate(POOL_BLOCKS) if o == j]
                    for n, (at, a) in enumerate(ins_):
                        mm = pe.matmul(b[:, 0:S], pool_w[:, 7 * g + at, :], win[:, 0, 3 * g + a, :],
                                       start=(n == 0), stop=(n == len(ins_) - 1))
                    mm.then_inc(misc_full, 1)
            point(pe, "mq")
            point(pe, "kmem_b")
            attention("mema", MEM_HEADS, 1, 2,
                      lambda h, qb: [(mq_half[:, h % 2, h // 2, qb * P:(qb + 1) * P], memk[:, 0, h // 2, :])],
                      lambda h: [lambda kb: memv[:, 0, kb, (h // 2) * P:(h // 2 + 1) * P]])
            for h in range(MEM_HEADS):
                misc_emptied(pe, ("O", "mema", h))
            for g in range(2):
                for j in range(3):
                    misc_emptied(pe, ("pool", g, j))
            for _ in range(2):
                tokens(1)
            mlp("a")
            norm("mixb")
            wait_ = normed("mixb")
            keys_values(1, **wait_)
            pe.wait_ge(head_sq, 4)
            b = fill_misc(("kr",))
            pe.matmul(b, mean64, sq2[:, 6:8, :], start=True, stop=True).then_inc(misc_full, 1)
            for _ in range(2):
                features(0)
            pe.wait_ge(head_sq, 5)
            for j in range(4):
                b = fill_misc(("qr", j))
                pe.matmul(b, mean64, sq2[:, 2 * j:2 * j + 2, :], start=True, stop=True).then_inc(misc_full, 1)
            point(pe, "q_swa")
            lin_emptied(pe, ("kvb", 1))
            attention("swa", SWA_HEADS, 1, 2,
                      lambda u, qb: [(q_swa[:, u % 2, u // 2, qb * P:(qb + 1) * P], k_swa[:, u // 6, :])],
                      lambda u: [lambda kb: v_swa[:, kb, (u // 6) * P:(u // 6 + 1) * P]])
            attention("memb", MEM_HEADS, 1, 2,
                      lambda h, qb: [(q_swa[:, h % 2, SWA_TILES + h // 2, qb * P:(qb + 1) * P],
                                      memk[:, 1, h // 2, :])],
                      lambda h: [lambda kb: memv[:, 1, kb, (h // 2) * P:(h // 2 + 1) * P]])
            for u in range(SWA_HEADS):
                misc_emptied(pe, ("O", "swa", u))
            for h in range(MEM_HEADS):
                misc_emptied(pe, ("O", "memb", h))
            for _ in range(2):
                tokens(1)
            mlp("b")
            assert state["misc"] == len(MISC) and state["half"] == NHALF

        @block.vector
        def _(dve):
            def do(ins):
                chain(dve, ins, dve_chain)

            def signal(ins):
                count[id(dve_chain)] += 1
                ins.then_inc(dve_chain, 1)

            def signalled():
                dve.wait_ge(dve_chain, count[id(dve_chain)])

            def rows2(ap):
                return ap.rearrange("p (a b) -> p a b", a=2)

            def scale_rows(n, src, dst):
                ss, ms, rs = stats(n)
                dve.wait_ge(squares, 2 * NORMS.index(n) + 2)
                dve.tensor_scalar(ms, ss, 1.0 / D, 1e-6, ALU.mult, ALU.add).then_inc(mean_sq, 1)
                dve.wait_ge(rstd_s, NORMS.index(n) + 1)
                for tb in range(TB):
                    ins = dve.tensor_scalar(dst[:, tb, :], src[:, tb, :], rs[:, tb:tb + 1], None, ALU.mult)
                    if n == "final":
                        do(ins)
                    else:
                        ins.then_inc(xn_ready, 1)

            def take_norm(n, dsts):
                made = norm_tiles(n) - 4 * len(dsts)
                for tb in range(TB):
                    for h in range(2):
                        key = ("xT", n, tb, h)
                        wait_misc(dve, key)
                        for g, buf in dsts:
                            dve.tensor_tensor(
                                op_hi[:, buf, 4 * h:4 * h + 4, tb * P:(tb + 1) * P],
                                misc_bank(key).rearrange("p (a b) -> p a b", a=4),
                                gain(g)[:, 4 * h:4 * h + 4].unsqueeze(2).broadcast_to([P, 4, P]), ALU.mult)\
                               .then_inc(norm_hi, 1)
                for tb in range(TB):
                    for h in range(2):
                        key = ("xT", n, tb, h)
                        made += len(dsts)
                        dve.wait_ge(norm_hi, made)
                        for k, (g, buf) in enumerate(dsts):
                            for f in range(4):
                                at = buf, 4 * h + f, slice(tb * P, (tb + 1) * P)
                                ins = dve.scalar_tensor_tensor(
                                    op_lo[:, at[0], at[1], at[2]], misc_bank(key)[:, f * P:(f + 1) * P],
                                    gain(g)[:, 4 * h + f:4 * h + f + 1],
                                    op_hi[:, at[0], at[1], at[2]].bitcast(F32), ALU.mult, ALU.subtract)
                        empty_misc(ins, key)

            def split(name, src, buf, tiles=slice(0, KC), last=True):
                hi, lo = op_hi[:, buf, tiles, :], op_lo[:, buf, tiles, :]
                a = dve.tensor_copy(hi, src)
                if last:
                    assert SPLITS[count.setdefault("split", 0)] == name, name
                    count["split"] += 1
                    a.then_inc(split_hi, 1)
                    dve.wait_ge(split_hi, count["split"])
                    dve.tensor_tensor(lo, src, hi.bitcast(F32), ALU.subtract).then_inc(split_lo, 1)
                else:
                    do(a)
                    do(dve.tensor_tensor(lo, src, hi.bitcast(F32), ALU.subtract))

            def add_x(weight):
                for j in range(4):
                    wait_lin(dve, (weight, j))
                    xs = x[:, :, j * HW:(j + 1) * HW]
                    empty_lin(dve.tensor_tensor(xs, rows2(lin_bank((weight, j))), xs, ALU.add), (weight, j))

            def maxima(kind, u, bias_ap=None, slope=None, sink=None):
                g = UNIT0[kind] + u
                r = g % 4
                key = ("S", kind, u)
                wait_misc(dve, key)
                b = rows2(misc_bank(key))
                src = b
                if bias_ap is not None:
                    if slope is None:
                        ins = dve.tensor_tensor(prob[:, r], b, bias_ap, ALU.add)
                    else:
                        ins = dve.scalar_tensor_tensor(prob[:, r], bias_ap, slope, b, ALU.mult, ALU.add)
                    empty_misc(ins, key)
                    misc_emptied(dve, key)
                    src = prob[:, r]
                if sink is None:
                    dve.tensor_reduce(nmax[:, r, :], src, AX.X, ALU.max, negate=True).then_inc(max_ready, 1)
                else:
                    do(dve.tensor_reduce(nmax[:, r, :], src, AX.X, ALU.max))
                    dve.tensor_scalar(nmax[:, r, :], nmax[:, r, :], sink, -1.0, ALU.max, ALU.mult)\
                       .then_inc(max_ready, 1)

            def exps_done(kind, u):
                in_psum = kind in ("cross", "mema", "memb")
                n = 0
                for k in ("diff", "cross", "mema", "swa", "memb"):
                    per = 1 if k in ("cross", "mema", "memb") else 2
                    if k == kind:
                        n += per * (u + 1)
                        break
                    n += per * {"diff": 2 * HEADS, "cross": CROSS_HEADS, "mema": MEM_HEADS, "swa": SWA_HEADS}[k]
                dve.wait_ge(exp_ready, n)
                if in_psum:
                    misc_emptied(dve, ("S", kind, u))

            def normalise(kind, i):
                if kind == "diff":
                    ra, rb = (UNIT0[kind] + 2 * i) % 4, (UNIT0[kind] + 2 * i + 1) % 4
                    exps_done(kind, 2 * i + 1)
                    do(dve.reciprocal(rsum[:, ra:rb + 1, :], ssum[:, ra:rb + 1, :]))
                    do(dve.tensor_scalar(rsum[:, rb, :], rsum[:, rb, :], small[:, 6:7], None, ALU.mult))
                    for qb in range(TB):
                        signal(dve.tensor_scalar(prob[:, rb, qb, :], prob[:, rb, qb, :], rsum[:, rb, qb:qb + 1],
                                                 None, ALU.mult))
                    signalled()
                    for qb in range(TB):
                        dve.scalar_tensor_tensor(prob[:, ra, qb, :], prob[:, ra, qb, :],
                                                 rsum[:, ra, qb:qb + 1], prob[:, rb, qb, :],
                                                 ALU.mult, ALU.add).then_inc(p_ready, 1)
                    return
                r = (UNIT0[kind] + i) % 4
                exps_done(kind, i)
                if kind == "swa":
                    do(dve.tensor_tensor(ssum[:, r, :], ssum[:, r, :], esink[:, r, :], ALU.add))
                do(dve.reciprocal(rsum[:, r, :], ssum[:, r, :]))
                for qb in range(TB):
                    dve.tensor_scalar(prob[:, r, qb, :], prob[:, r, qb, :], rsum[:, r, qb:qb + 1], None,
                                      ALU.mult).then_inc(p_ready, 1)

            def attention(kind, items, group, lag, extra, dst, fill=()):
                for i in range(min(lag, items)):
                    for g in range(group):
                        maxima(kind, i * group + g, **extra(i * group + g))
                def take(i):
                    key = ("O", kind, i)
                    wait_misc(dve, key)
                    lo, hi, buf, d, w = dst(i)
                    src = misc_bank(key)[lo:hi, 0:w]
                    if w == 2 * S:
                        src = rows2(src)
                    if buf is None:
                        empty_misc(dve.tensor_copy(o_diff[:, d, :], src), key)
                        return
                    do(dve.tensor_copy(op_hi[lo:hi, buf, d, :], src))
                    empty_misc(dve.tensor_tensor(op_lo[lo:hi, buf, d, :], src,
                                                 op_hi[lo:hi, buf, d, :].bitcast(F32), ALU.subtract), key)

                for i in range(items):
                    normalise(kind, i)
                    if i + lag < items:
                        for g in range(group):
                            u = (i + lag) * group + g
                            j = i + lag - 4 // group
                            if j >= 0:
                                wait_misc(dve, ("T", kind, j))
                            maxima(kind, u, **extra(u))
                    if i < len(fill) and fill[i]:
                        fill[i]()
                    if i:
                        take(i - 1)
                take(items - 1)

            do(dve.memset(q_half[HD:P, 0, :, :], 0.0))
            do(dve.memset(q_half[0:HD, 1, :, :], 0.0))
            do(dve.memset(small[:, 8:9], 1e-5))
            at_point(dve.memset(small[:, 9:10], 1e-6), "zeros")
            dve.wait_ge(const_in, 48)
            for j in range(2):
                at = 2 * j * HD
                do(dve.tensor_tensor(bc[:, at:at + HD], bc[:, at:at + HD], bc[:, at + HD:at + 2 * HD], ALU.mult))
                dve.tensor_reduce(small[:, j:j + 1], bc[:, at:at + HD], AX.X, ALU.add).then_inc(lam_sums, 1)
            dve.wait_ge(x_in_s, 16)
            scale_rows("mix", x, xn)
            wait_misc(dve, ("bias",))
            empty_misc(dve.tensor_copy(bias_row, misc_bank(("bias",))[0:8, :]), ("bias",))
            take_norm("mix", [("mix", 0)])
            dve.wait_ge(lam_exps, 1)
            do(dve.tensor_tensor(small[:, 5:6], small[:, 3:4], small[:, 2:3], ALU.subtract))
            do(dve.tensor_scalar(small[:, 6:7], small[:, 5:6], -LAM_INIT, None, ALU.add))
            dve.wait_ge(bias_in, 32)

            def take_cc(i):
                def f():
                    for j in (2 * i, 2 * i + 1):
                        key = ("cc", j)
                        wait_lin(dve, key)
                        us = u_conv[:, 2 * j:2 * j + 2, :]
                        lin_emptied(dve, ("cx", j))
                        empty_lin(dve.tensor_tensor(us, rows2(lin_bank(key)), us, ALU.mult), key)
                        lin_emptied(dve, key)
                        for t in (2 * j, 2 * j + 1):
                            a = VEC["conv"][0]
                            do(dve.tensor_scalar(conv[:, t, :], u_conv[:, t, :], vecs[:, a + 16 + t:a + 17 + t],
                                                 None, ALU.mult))
                            for back in (1, 2):
                                w = vecs[:, a + 8 * (2 - back) + t:a + 8 * (2 - back) + t + 1]
                                do(dve.scalar_tensor_tensor(conv[:, t, back:S], u_conv[:, t, 0:S - back], w,
                                                            conv[:, t, back:S], ALU.mult, ALU.add))
                return f

            def take_cb(i):
                def f():
                    for j in (2 * i, 2 * i + 1):
                        key = ("cb", j)
                        wait_lin(dve, key)
                        cs = conv[:, 2 * j:2 * j + 2, :]
                        empty_lin(dve.tensor_tensor(u_conv[:, 2 * j:2 * j + 2, :], rows2(lin_bank(key)), cs,
                                                    ALU.mult), key)
                return f

            def sigmoid(name, dst, i):
                def f():
                    for j in (2 * i, 2 * i + 1):
                        lin_emptied(dve, (name, j))
                    d = dst[:, 4 * i:4 * i + 4, :]
                    do(dve.tensor_scalar(d, d, 1.0, None, ALU.add))
                    do(dve.reciprocal(d, d))
                return f

            attention("diff", HEADS, 2, 1, lambda u: dict(bias_ap=bias[:, u // 2]),
                      lambda h: (0, P, None, h, S),
                      [take_cc(0), take_cc(1), take_cb(0), take_cb(1), sigmoid("gc", gate_c, 0),
                       sigmoid("gc", gate_c, 1), sigmoid("ga", gate_a, 0), sigmoid("ga", gate_a, 1)])
            for j in range(4):
                lin_emptied(dve, ("cb", j))
            do(dve.tensor_scalar(small[:, 7:8], gain("subln"), 1.0 - LAM_INIT, None, ALU.mult))
            dve.wait_ge(mem_in_s, 16)
            scale_rows("mem", xn, xn)
            take_norm("mem", [("mem", 1)])
            for j in range(4):
                misc_emptied(dve, ("sub", j))
            do(dve.reciprocal(sq[:, :, :], sq[:, :, :]))
            do(dve.scalar_tensor_tensor(o_diff[:, :, :], o_diff[:, :, :], small[:, 7:8], sq[:, :, :],
                                        ALU.mult, ALU.mult))
            dve.wait_ge(mem2_in_s, 16)
            scale_rows("mem2", xn, xn)
            take_norm("mem2", [("mem2a", 0), ("mem2b", 1)])
            for name, src, buf, key in (("u", u_conv, 0, ("mkva", 1)), ("o", o_diff, 1, ("mkvb", 1))):
                wait_lin(dve, key)
                split(name, src[:, :, :], buf)
            for l in range(2):
                misc_emptied(dve, ("mkr", "ab"[l]))
                r = junk[:, 4 + 2 * l:6 + 2 * l, :]
                do(dve.reciprocal(r, r))
                at_point(dve.scalar_tensor_tensor(memk[:, l, :, :], memk[:, l, :, :], gain("mkn" + "ab"[l]), r,
                                                  ALU.mult, ALU.mult), "kmem_" + "ab"[l])
            for j in range(4):
                key = ("cout", j)
                wait_lin(dve, key)
                g = gate_c[:, 2 * j:2 * j + 2, :]
                empty_lin(dve.tensor_tensor(g, rows2(lin_bank(key)), g, ALU.mult), key)
            for j in range(4):
                key = ("aout", j)
                wait_lin(dve, key)
                g = gate_a[:, 2 * j:2 * j + 2, :]
                empty_lin(dve.tensor_tensor(g, rows2(lin_bank(key)), g, ALU.mult), key)
                lin_emptied(dve, ("aout", j))
                lin_emptied(dve, ("cout", j))
                do(dve.tensor_tensor(g, g, gate_c[:, 2 * j:2 * j + 2, :], ALU.add))
                split("merged", g, 0, slice(2 * j, 2 * j + 2), last=(j == 3))
            add_x("mixo")
            scale_rows("cross", x, xn)
            take_norm("cross", [("cross", 1)])
            attention("cross", CROSS_HEADS, 1, 2, lambda u: {},
                      lambda h: (0, P, 0, slice(2 * h, 2 * h + 2), 2 * S))
            add_x("co")
            scale_rows("ffn", x, xn)
            take_norm("ffn", [("ffn", 1)])
            dve.memset(zeros, 0.0).then_inc(peer_zero, 1)
            STEPS = 22

            def top_experts(tb, h):
                turn = h + tb * PH
                steps = [0]

                def step(ins):
                    steps[0] += 1
                    ins.then_inc(top_chain, 1)
                    dve.wait_ge(top_chain, turn * STEPS + steps[0])
                    dve.sem_inc(top_passed, 1)

                def at(ap, size):
                    return ap[:, tb, h * size:(h + 1) * size] if isinstance(h, int) \
                        else ap[:, tb, bass.ds(h * size, size)]

                src = score[:, tb, 2 * h:2 * h + 2, :] if isinstance(h, int) \
                    else score[:, tb, bass.ds(h * 2, 2), :]
                step(dve.tensor_copy(half_score, src))
                for r in range(2):
                    k0 = 8 * r
                    dve.max(half_vals[:, 0, k0:k0 + 8], half_score[:, 0, :])
                    step(dve.max(half_vals[:, 1, k0:k0 + 8], half_score[:, 1, :]))
                    dve.max_index(half_idx[:, 0, k0:k0 + 8], half_vals[:, 0, k0:k0 + 8], half_score[:, 0, :])
                    step(dve.max_index(half_idx[:, 1, k0:k0 + 8], half_vals[:, 1, k0:k0 + 8], half_score[:, 1, :]))
                    if r == 0:
                        dve.match_replace(half_score[:, 0, :], half_vals[:, 0, 0:8], half_score[:, 0, :], -3e38)
                        step(dve.match_replace(half_score[:, 1, :], half_vals[:, 1, 0:8], half_score[:, 1, :],
                                               -3e38))
                dve.tensor_copy(half_idxf, half_idx)
                step(dve.tensor_tensor(cand, half_vals[:, 0, :].unsqueeze(2).broadcast_to([P, TOPK, TOPK]),
                                       half_vals[:, 1, :].unsqueeze(1).broadcast_to([P, TOPK, TOPK]), ALU.add))
                flat = cand.rearrange("p a b -> p (a b)")
                for r in range(2):
                    k0 = 8 * r
                    step(dve.max(top_vals[:, k0:k0 + 8], flat))
                    step(dve.max_index(top_pos[:, k0:k0 + 8], top_vals[:, k0:k0 + 8], flat))
                    if r == 0:
                        step(dve.match_replace(flat, top_vals[:, 0:8], flat, -3e38))
                dve.tensor_scalar(top_less, top_vals, top_vals[:, 0:1], None, ALU.subtract).then_inc(top_exp_in, 1)
                dve.tensor_scalar(top_half[:, 0, :], top_pos, 4, None, ALU.logical_shift_right)
                step(dve.tensor_scalar(top_half[:, 1, :], top_pos, TOPK - 1, None, ALU.bitwise_and))
                step(dve.tensor_copy(top_halff, top_half))
                for c in range(2):
                    step(dve.tensor_tensor(pick, iota16.unsqueeze(1).broadcast_to([P, TOPK, TOPK]),
                                           top_halff[:, c, :].unsqueeze(2).broadcast_to([P, TOPK, TOPK]),
                                           ALU.is_equal))
                    step(dve.tensor_tensor(pick, pick,
                                           half_idxf[:, c, :].unsqueeze(1).broadcast_to([P, TOPK, TOPK]),
                                           ALU.mult))
                    step(dve.tensor_reduce(found[:, c, :], pick, AX.X, ALU.add))
                dve.scalar_tensor_tensor(at(expert, TOPK), found[:, 0, :], float(NKEYS), found[:, 1, :],
                                         ALU.mult, ALU.add).then_inc(experts_ready, 1)
                dve.wait_ge(top_exp, turn + 1)
                step(dve.reciprocal(hinv, hsum))
                step(dve.tensor_scalar(at(weight, TOPK), top_e, hinv, None, ALU.mult))
                assert steps[0] == STEPS, steps

            def dot_rows(tb, h):
                for j in range(TOPK):
                    s = j % GSLOTS
                    if s == 0:
                        dve.wait_ge(gelu_ready, h * (TOPK // 2) + (tb * (PAIRS // 2) + j // 2 + 1))
                    dve.wait_ge(gathered[s], h * 32 + (tb * (PAIRS // GSLOTS) + j // GSLOTS + 1) * 16)
                    u = rows[:, s, 0:D].rearrange("p (a b) -> p a b", a=2)
                    dve.tensor_tensor_reduce(u, u, token_rows[tb][:, :, :], 1.0, 0.0,
                                             ALU.mult, ALU.add, dots[:, s:s + 1]).then_inc(dot_ready, 1)

            for j in range(4):
                misc_emptied(dve, ("sc", 0, j))
            top_experts(0, 0)
            for tb in range(TB):
                dve.wait_ge(hf_ready, tb + 1)
                with dve.Fori(0, PH - 1) as h:
                    top_experts(tb, h + 1)
                    dot_rows(tb, h)
                if tb < TB - 1:
                    for j in range(4):
                        misc_emptied(dve, ("sc", tb + 1, j))
                    top_experts(tb + 1, 0)
                dot_rows(tb, PH - 1)
                dve.wait_ge(acc_ready, tb + 1)
                for n in range(2):
                    xs = x[:, tb, n * CW:(n + 1) * CW]
                    dve.tensor_tensor(xs, row_sums[tb][:, n, :], xs, ALU.add).then_inc(acc_used, 1)
            dve.wait_ge(acc_used, 4)
            scale_rows("final", x, xn)
            dve.wait_ge(gfin_in, 16)
            for tb in range(TB):
                ins = dve.tensor_tensor(x[:, tb, :], xn[:, tb, :], gfin, ALU.mult)
                do(ins) if tb == 0 else at_point(ins, "h")
            point(dve, "h")
            scale_rows("mixa", x, xn)
            take_norm("mixa", [("mixa", 0)])

            do(dve.memset(mq_half[HD:P, 0, :, :], 0.0))
            do(dve.memset(mq_half[0:HD, 1, :, :], 0.0))
            for j in range(3):
                lin_emptied(dve, ("ina", j))

            def window(dst, src, t0, back):
                n = SWA_TILES
                do(dve.tensor_copy(dst[:, t0:n, 0:back], src[:, t0:n, 0:back]))
                do(dve.tensor_tensor(dst[:, t0:n, back:S], src[:, t0:n, back:S], src[:, t0:n, 0:S - back],
                                     ALU.add))

            w0, w1 = win[:, 0], win[:, 1]
            window(w0, u_pool, 0, 1)
            window(w1, w0, 1, 2)
            window(w0, w1, 3, 4)
            window(w1, w0, 4, 8)
            dve.wait_ge(pool_in_s, 32)
            for src, lo, hi, t in ((w0, 0, P, 0), (w0, 0, HD, 1), (w1, HD, P, 1), (w1, 0, P, 2), (w0, 0, P, 3),
                                   (w0, 0, HD, 4), (w1, HD, P, 4), (w1, 0, P, 5)):
                do(dve.tensor_tensor(w0[lo:hi, t, :], src[lo:hi, t, :], cnt[lo:hi, t, :], ALU.mult))
            at_point(dve.tensor_tensor(w0, w0, u_pool[:, :, :], ALU.subtract), "d_pool")
            misc_emptied(dve, ("mqr", "a"))
            r = sq2[:, 0:2, :]
            do(dve.reciprocal(r, r))
            do(dve.tensor_scalar(small[:, 10:11], gain("mqna"), HD ** -0.5, None, ALU.mult))
            do(dve.scalar_tensor_tensor(mq_half[0:HD, 0, :, :], raw2[0:HD, 6:8, :], small[0:HD, 10:11], r[0:HD],
                                        ALU.mult, ALU.mult))
            at_point(dve.scalar_tensor_tensor(mq_half[HD:P, 1, :, :], raw2[HD:P, 6:8, :], small[HD:P, 10:11],
                                              r[HD:P], ALU.mult, ALU.mult), "mq")
            for g in range(2):
                for j in range(3):
                    key = ("pool", g, j)
                    wait_misc(dve, key)
                    t = 3 * g + j
                    do(dve.tensor_scalar(op_hi[:, 1, t, :], misc_bank(key)[:, 0:S], gain("pool")[:, t:t + 1], None,
                                         ALU.mult))
                    empty_misc(dve.scalar_tensor_tensor(op_lo[:, 1, t, :], misc_bank(key)[:, 0:S],
                                                        gain("pool")[:, t:t + 1],
                                                        op_hi[:, 1, t, :].bitcast(F32), ALU.mult, ALU.subtract),
                               key)

            def half_tile(t0):
                def f(h):
                    lo = HD * (h % 2)
                    return lo, lo + HD, 1, t0 + h // 2, S
                return f

            attention("mema", MEM_HEADS, 1, 2, lambda u: {}, half_tile(SWA_TILES))
            add_x("outa")

            def mlp(l):
                scale_rows("mlp" + l, x, xn)
                take_norm("mlp" + l, [("mlp" + l, 0)])
                up_done = LAST[("up" + l, 15)]
                for g in range(4):
                    dve.wait_ge(hidden_ready, 16 * "ab".index(l) + 4 * (g + 1))
                    if g:
                        dve.wait_ge(half_done, up_done + (4 * (g - 1) if g > 1 else 0))
                    split(f"hidden{l}{g}", hidden[:, KC * g:KC * (g + 1), :], (g + 1) % 2)
                add_x("down" + l)

            mlp("a")
            scale_rows("mixb", x, xn)
            take_norm("mixb", [("kv", 1), ("mixb", 0)])
            do(dve.memset(q_swa[HD:P, 0, :, :], 0.0))
            do(dve.memset(q_swa[0:HD, 1, :, :], 0.0))
            misc_emptied(dve, ("kr",))
            do(dve.reciprocal(r, r))
            at_point(dve.scalar_tensor_tensor(k_swa[:, :, :], k_swa[:, :, :], gain("kn"), r, ALU.mult, ALU.mult),
                     "k_swa")
            do(dve.tensor_scalar(small[:, 10:11], gain("qn"), HD ** -0.5, None, ALU.mult))
            do(dve.tensor_scalar(small[:, 11:12], gain("mqnb"), HD ** -0.5, None, ALU.mult))
            for j in range(4):
                misc_emptied(dve, ("qr", j))
            do(dve.reciprocal(sq2[:, :, :], sq2[:, :, :]))
            for a, b, g in ((0, SWA_TILES, 10), (SWA_TILES, KC, 11)):
                for c in range(2):
                    lo, hi = c * HD, (c + 1) * HD
                    ins = dve.scalar_tensor_tensor(q_swa[lo:hi, c, a:b, :], raw2[lo:hi, a:b, :],
                                                   small[lo:hi, g:g + 1], sq2[lo:hi, a:b, :], ALU.mult, ALU.mult)
                    at_point(ins, "q_swa") if (a and c) else do(ins)
            dve.wait_ge(alibi_in, 16)

            def swa_extra(u):
                h = SWA_ORDER[u]
                slope = float(np.float32(2.0) ** np.float32(-8.0 * (h + 1) / SWA_HEADS))
                return dict(bias_ap=alibi[:, :, :], slope=slope, sink=bc[:, 4 * HD + h:4 * HD + h + 1])

            attention("swa", SWA_HEADS, 1, 2, swa_extra, half_tile(0))
            attention("memb", MEM_HEADS, 1, 2, lambda u: {}, half_tile(SWA_TILES))
            add_x("outb")
            mlp("b")


def chunked(w):
    k, n = w.shape
    c = w.reshape(k // D, KC, P, n // HW, HW).transpose(3, 0, 2, 1, 4)
    order = [(j, g) for g in range(k // D) for j in range(n // HW)]
    return [c[j, g].reshape(P, KC * HW) for j, g in order]


def tiles(v):
    return v.reshape(-1, P).T


def layout(i):
    w_in = np.split(i["w_in"][0], 8, axis=1)
    cb, cc, cx, q, k, v, gc, ga = w_in
    ckv = i["w_ckv"][0]
    heads = np.concatenate([np.arange(h * HD, (h + 1) * HD) for h in SWA_ORDER])
    order = np.concatenate([heads, np.arange(SWA_HEADS * HD, D)])
    parts = {"q": q, "k": k, "v": v, "cx": cx, "cc": cc, "cb": cb, "gc": gc, "ga": ga,
             "ck": ckv[:, :D], "cv": ckv[:, D:], "cout": i["w_conv_out"][0], "aout": i["w_attn_out"][0],
             "mixo": i["w_mix_out"][0], "cq": i["w_cq"][0], "co": i["w_co"][0], "pq": i["w_pq"][0],
             "mkva": i["w_mem_kv_2"][0], "mkvb": i["w_mem_kv_2"][1], "kvb": i["w_kv_2"],
             "ina": i["w_in_2"][0], "inb": i["w_in_2"][1][:, order],
             "outa": i["w_out_2"][0], "outb": i["w_out_2"][1][order],
             "upa": i["w_up_2"][0], "upb": i["w_up_2"][1], "downa": i["w_down_2"][0], "downb": i["w_down_2"][1]}
    made = {name: chunked(w) for name, w in parts.items()}
    taken = {}
    stream = np.empty((NHALF, P, KC * HW), np.float32)
    for n in range(NHALF):
        c = CHUNKS[n // 2]
        stream[n] = made[c][taken.get(c, 0)]
        taken[c] = taken.get(c, 0) + 1

    def twice(g):
        return np.concatenate([g, g]).reshape(P, 1)

    columns = {"mix": tiles(i["norm_mix_g"][0]), "cross": tiles(i["norm_cross_g"][0]),
               "mem": tiles(i["norm_mem_g"][0]), "ffn": tiles(i["norm_ffn_g"][0]),
               "mixa": tiles(i["norm_mix_2"][0]), "mixb": tiles(i["norm_mix_2"][1]),
               "mlpa": tiles(i["norm_mlp_2"][0]), "mlpb": tiles(i["norm_mlp_2"][1]), "kv": tiles(i["kv_norm_2"]),
               "mem2a": tiles(i["mem_norm_2"][0]), "mem2b": tiles(i["mem_norm_2"][1]),
               "conv": tiles(i["conv_w"][0]), "subln": i["subln_g"][0].reshape(P, 1),
               "pool": tiles(i["pool_scale_2"][0]), "kn": twice(i["k_norm_2"]), "qn": twice(i["q_norm_2"][0]),
               "mqna": twice(i["mem_q_norm_2"][0]), "mqnb": twice(i["mem_q_norm_2"][1]),
               "mkna": twice(i["mem_k_norm_2"][0]), "mknb": twice(i["mem_k_norm_2"][1])}
    vecs = np.concatenate([columns[n] for n in VEC], axis=1)
    bc = np.concatenate([i["lambda_q1"][0], i["lambda_k1"][0], i["lambda_q2"][0], i["lambda_k2"][0],
                         i["sinks_2"][0]]).reshape(1, NBC)
    n = np.arange(S)
    big = np.maximum(n, 1).astype(np.float32)
    exact = BUCKETS // 2
    large = exact + (np.log(big / exact) / math.log(MAX_DISTANCE / exact) * (BUCKETS - exact)).astype(np.int32)
    bucket = np.where(n < exact, n, np.minimum(large, BUCKETS - 1))
    onehot = np.zeros((BUCKETS + 1, 2 * S), np.float32)
    onehot[bucket[::-1], n] = 1.0
    onehot[BUCKETS, S:] = 1.0
    rel = np.concatenate([i["rel_bias"], np.full((1, HEADS), MASKED, np.float32)])
    pos = np.arange(P)
    dist = P * np.arange(TB)[None, :, None] + pos[:, None, None] - n[None, None, :]
    alibi = np.where((dist >= 0) & (dist < P), -dist, -1e36).astype(np.float32)
    same = (pos[:, None] // HD == pos[None, :] // HD)
    consts = np.concatenate([np.eye(P), np.full((P, P), 1.0 / P), same / HD,
                             np.tile(np.arange(TOPK), (P, 1)), alibi.reshape(P, -1)], axis=1).astype(np.float32)
    window = np.repeat(np.array(POOL_WINDOWS), POOL_GROUP)
    cnt = 1.0 / np.minimum(n[None, :] + 1, window[:, None])
    cnt = cnt.reshape(SWA_TILES, P, S).transpose(1, 0, 2).reshape(P, -1).astype(np.float32)
    pool_w = np.zeros((2, 2 * POOL_GROUP, 2 * POOL_GROUP), np.float32)
    for g in range(len(POOL_WINDOWS)):
        a = g % 2 * POOL_GROUP
        pool_w[g // 2, a:a + POOL_GROUP, a:a + POOL_GROUP] = i["pool_w_2"][0, g]
    pool_w = np.concatenate([pool_w[g, a * P:(a + 1) * P, o * P:(o + 1) * P]
                             for g in range(2) for a, o in POOL_BLOCKS], axis=1)
    keys = i["sub_keys"][0].transpose(3, 1, 0, 2).reshape(P, -1)
    return dict(x_in=i["x"][0], mem_in=i["mem"][0], mem2_in=i["mem_2"][0], wstream=stream,
                experts=np.concatenate([i["peer_u"][0], i["peer_v"][0]], axis=1), vecs_in=vecs, bc_in=bc,
                final_g=i["final_g"].reshape(1, D), rel_in=rel, keys_in=keys, pool_in=pool_w,
                consts_in=consts, onehot_in=onehot, cnt_in=cnt)


def kernel(**inputs):
    import concourse.bacc as bacc
    from concourse.bass_utils import run_bass_kernel_spmd

    nc = bacc.Bacc("TRN2", target_bir_lowering=False, num_devices=1)
    arrays, args = {}, {}
    for name, a in layout({k: np.asarray(v) for k, v in inputs.items()}).items():
        arrays[name] = np.ascontiguousarray(a)
        args[name] = nc.dram_tensor(name, a.shape, F32, kind="ExternalInput").ap()
    args["scratch"] = nc.dram_tensor("scratch", (HEADS, P * (2 * S + 1)), F32, kind="Internal").ap()
    args["out"] = nc.dram_tensor("out_dram", (S, D), F32, kind="ExternalOutput").ap()
    build(nc, **args)
    r = run_bass_kernel_spmd(nc, [arrays], core_ids=[0])
    return r.results[0]["out_dram"].reshape(1, S, D)
```

```python
import math
from contextlib import ExitStack

import numpy as np

import concourse.bass as bass
from concourse import mybir

F32 = mybir.dt.float32
F32R = mybir.dt.float32r
I32 = mybir.dt.int32
U32 = mybir.dt.uint32
ALU = mybir.AluOpType
ACT = mybir.ActivationFunctionType
AX = mybir.AxisListType

P = 128
D = 1024
S = 256
KC = D // P
TB = S // P
CW = 512
HEADS = 8
HD = 64
CROSS_HEADS = 4
BUCKETS = 32
MAX_DISTANCE = 128
PH = 8
TOPK = 16
NKEYS = 128
PAIRS = PH * TOPK
SWA_HEADS = 12
SWA_TILES = SWA_HEADS * HD // P
MEM_HEADS = 4
POOL_WINDOWS = (2, 4, 8, 16)
POOL_GROUP = SWA_HEADS * HD // len(POOL_WINDOWS)
FF_TILES = 4 * D // P
LAM_INIT = 0.8 - 0.6 * math.exp(0.0)
MASKED = -1e30
HW = CW // 2
RAW = 3
HI = 3
LO = 2
GSLOTS = 8
AHEAD = 2
EARLY_SLOTS = 5
SWA_ORDER = [h for j in range(SWA_TILES) for h in (6 * (j // 3) + j % 3, 6 * (j // 3) + 3 + j % 3)]
POOL_BLOCKS = [(0, 0), (1, 0), (0, 1), (1, 1), (2, 1), (1, 2), (2, 2)]

VEC = {}
for _name, _n in [("mix", 8), ("cross", 8), ("mem", 8), ("ffn", 8), ("mixa", 8), ("mixb", 8), ("mlpa", 8),
                  ("mlpb", 8), ("kv", 8), ("mem2a", 8), ("mem2b", 8), ("conv", 24), ("subln", 1),
                  ("pool", 6), ("kn", 1), ("qn", 1), ("mqna", 1), ("mqnb", 1), ("mkna", 1), ("mknb", 1)]:
    VEC[_name] = (sum(n for _, n in VEC.values()), _n)
NVEC = sum(n for _, n in VEC.values())
NBC = 4 * HD + SWA_HEADS

CHUNKS = (["q", "q", "k", "k", "v", "v", "cx", "cx", "cc", "cc", "cb", "cb", "gc", "gc", "ga", "ga"]
          + ["ck", "ck", "cv", "cv", "mkva", "mkvb", "cout", "cout", "aout", "aout", "mixo", "mixo"]
          + ["cq", "cq", "co", "co", "pq", "pq", "pq", "pq"]
          + ["ina", "ina", "outa", "outa"] + ["upa"] * 8 + ["downa"] * 8
          + ["kvb", "inb", "inb", "outb", "outb"] + ["upb"] * 8 + ["downb"] * 8)
NCHUNK = len(CHUNKS)
NHALF = 2 * NCHUNK
FIRST_CHUNK = {"mix": CHUNKS.index("q"), "mem": CHUNKS.index("ck"), "mem2": CHUNKS.index("mkva"),
               "cross": CHUNKS.index("cq"), "ffn": CHUNKS.index("pq"), "mixa": CHUNKS.index("ina"),
               "mlpa": CHUNKS.index("upa"), "mixb": CHUNKS.index("kvb"), "mlpb": CHUNKS.index("upb")}
ROOT_LATER = ("cross", "ffn", "mlpa", "mlpb")
ROOTED = [n for n in FIRST_CHUNK if n not in ROOT_LATER]
OPERANDS = [(n, k) for n in FIRST_CHUNK for k in range(2 if n in ("mem2", "mixb") else 1)]
SPLITS = ["u", "o", "merged"] + [f"hidden{l}{g}" for l in "ab" for g in range(4)]


def plan():
    lin, last, misc = {}, {}, {}
    half = 0
    seen = {}
    for n, c in enumerate(CHUNKS):
        for norm_ in ROOTED:
            if FIRST_CHUNK[norm_] == n:
                lin["roots", norm_] = len(lin)
        i = seen.get(c, 0)
        seen[c] = i + 1
        for j in range(2):
            half += 1
            key = (c, 2 * (i % 2) + j) if c.startswith("down") else (c, 2 * i + j)
            lin.setdefault(key, len(lin))
            last[key] = half

    def m(*name):
        misc[name] = len(misc)

    def norm(n):
        for j in range(4):
            m("xT", n, j)

    def attention(kind, items, group, lag):
        for i in range(min(lag, items)):
            for g in range(group):
                m("S", kind, i * group + g)
        for i in range(items):
            if i + lag < items:
                for g in range(group):
                    m("S", kind, (i + lag) * group + g)
            if i:
                m("O", kind, i - 1)
            m("T", kind, i)
        m("O", kind, items - 1)

    norm("mix")
    m("bias")
    attention("diff", HEADS, 2, 1)
    norm("mem")
    for j in range(4):
        m("sub", j)
    norm("mem2")
    for l in "ab":
        m("mkr", l)
    norm("cross")
    attention("cross", CROSS_HEADS, 1, 2)
    norm("ffn")
    for tb in range(TB):
        for j in range(4):
            m("sc", tb, j)
    norm("mixa")
    for g in range(2):
        for j in range(3):
            m("pool", g, j)
        if g == 0:
            m("mqr", "a")
    attention("mema", MEM_HEADS, 1, 2)
    norm("mlpa")
    norm("mixb")
    m("kr")
    for j in range(4):
        m("qr", j)
    attention("swa", SWA_HEADS, 1, 2)
    attention("memb", MEM_HEADS, 1, 2)
    norm("mlpb")
    return lin, last, misc


def build(nc, x_in, mem_in, mem2_in, wstream, experts, vecs_in, bc_in, final_g, rel_in, keys_in, pool_in,
          consts_in, onehot_in, cnt_in, scratch, out):
    LIN, LAST, MISC = plan()
    ctx = ExitStack()
    with ctx:
        def sb(name, shape, dt=F32):
            return ctx.enter_context(nc.sbuf_tensor(name, shape, dt))

        sems = {}

        def sem(name):
            sems[name] = ctx.enter_context(nc.semaphore(name))
            return sems[name]

        raw = sb("raw", [P, RAW, KC, HW])
        w_hi = sb("w_hi", [P, HI, KC, HW], F32R)
        w_lo = sb("w_lo", [P, LO, KC, HW], F32R)
        x = sb("x", [P, TB, D])
        xn = sb("xn", [P, TB, D])
        op_hi = sb("op_hi", [P, 2, KC, S], F32R)
        op_lo = sb("op_lo", [P, 2, KC, S], F32R)
        memk = sb("memk", [P, 2, 2, S])
        memv = sb("memv", [P, 2, TB, S])
        vecs = sb("vecs", [P, NVEC])
        bc = sb("bc", [P, NBC])
        consts = sb("consts", [P, 3 * P + TOPK])
        stat = sb("stat", [P, 2, 14])
        arena = sb("arena", [P, 21508])

        ident = consts[:, 0:P]
        mean128 = consts[:, P:2 * P]
        mean64 = consts[:, 2 * P:3 * P]
        iota16 = consts[:, 3 * P:3 * P + TOPK]

        def part(at, *shape):
            n = int(np.prod(shape))
            v = arena[:, at:at + n]
            if len(shape) == 2:
                v = v.rearrange("p (a b) -> p a b", a=shape[0])
            if len(shape) == 3:
                v = v.rearrange("p (a b c) -> p a b c", a=shape[0], b=shape[1])
            if len(shape) == 4:
                v = v.rearrange("p (a b c d) -> p a b c d", a=shape[0], b=shape[1], c=shape[2])
            return v

        prob = part(18432, 4, TB, S)
        prob_t = part(20480, 2, 2 * S)
        norm_t = xn[:, :, :].rearrange("p t (a b) -> p (t a) b", b=S)
        root_diag = part(18432, TB, P)
        root_rows = part(18432 + S, S)
        q_half = part(0, 2, HEADS, S)
        k_diff = part(4096, HEADS, S)
        v_diff = part(6144, TB, D)
        u_conv = part(8192, KC, S)
        conv = part(10240, KC, S)
        gate_c = part(12288, KC, S)
        gate_a = part(10240, KC, S)
        bias = part(14336, HEADS, TB, S)
        o_diff = part(0, KC, S)
        rel_sb = part(12288, 512)[0:BUCKETS + 1, 0:8]
        onehot = part(12800, 512)[0:BUCKETS + 1, :]
        bias_row = part(13312, 512)[0:8, :]
        k_cross = part(2048, KC, S)
        v_cross = part(4096, TB, D)
        q_cross = part(6144, KC, S)
        sq = part(14336, KC, S)
        junk = part(16384, KC, S)
        means = part(6144, KC, S)
        scratch1 = part(18432, KC, S)
        q_peer = part(12288, 2 * PH, S)
        keys = part(10240, 2 * PH, NKEYS)
        rows = part(0, GSLOTS, 2 * D)
        score = part(16384, TB, 2 * PH, NKEYS)
        u_pool = part(0, SWA_TILES, S)
        win = part(2048, 2, SWA_TILES, S)
        cnt = part(5120, SWA_TILES, S)
        pool_w = part(6656, 2 * len(POOL_BLOCKS), P)
        mq_half = part(8448, 2, 2, S)
        sq2 = part(11520, KC, S)
        raw2 = part(13568, KC, S)
        q_swa = part(0, 2, KC, S)
        k_swa = part(4096, 2, S)
        sqk = part(15616, 4, S)
        v_swa = part(4608, TB, S)
        alibi = part(5120, TB, S)
        slopes = part(16640, SWA_HEADS, P)
        hidden = part(0, FF_TILES, S)
        gfin = part(16384, D)

        half_score = part(20480, 2, NKEYS)
        half_vals = part(20736, 2, TOPK)
        half_idx = part(20768, 2, TOPK).bitcast(U32)
        half_idxf = part(20800, 2, TOPK)
        cand = part(20832, TOPK, TOPK)
        top_vals = part(21088, TOPK)
        top_pos = part(21104, TOPK).bitcast(U32)
        top_half = part(21120, 2, TOPK).bitcast(U32)
        top_halff = part(21152, 2, TOPK)
        pick = part(21184, TOPK, TOPK)
        found = part(21440, 2, TOPK)
        top_less = part(21472, TOPK)
        top_e = part(21488, TOPK)
        hsum = part(21504, 1)
        hinv = part(21505, 1)
        diag = xn[:, 0, :].rearrange("p (s n) -> p s n", s=GSLOTS)
        expert = xn[:, 1, 0:256].rearrange("p (t n) -> p t n", t=TB).bitcast(I32)
        weight = xn[:, 1, 256:512].rearrange("p (t n) -> p t n", t=TB)
        zeros = xn[:, 1, 640:768]
        stage = xn[:, 1, 768:784].rearrange("p (t n) -> p t n", t=2).bitcast(I32)
        dots = xn[:, 1, 784:792]
        gact = xn[:, 1, 792:800]
        wact = xn[:, 1, 800:808]
        nmax = sb("nmax", [P, 4, 2])
        ssum = sb("ssum", [P, 4, 2])
        rsum = sb("rsum", [P, 4, 2])
        esink = sb("esink", [P, 4, 2])
        small = sb("small", [P, 16])

        bank_pairs = [ctx.enter_context(nc.psum_tensor(f"banks{i}", [P, 2, 512], F32)) for i in range(4)]
        banks = [bank_pairs[i // 2][:, i % 2, :] for i in range(8)]

        raw_in = [sem(f"raw_in{i}") for i in range(RAW)]
        hi_ready = sem("hi_ready")
        lo_ready = sem("lo_ready")
        norm_rows = sem("norm_rows")
        norm_hi = sem("norm_hi")
        norm_lo = sem("norm_lo")
        roots_full = sem("roots_full")
        split_hi = sem("split_hi")
        split_lo = sem("split_lo")
        half_done = sem("half_done")
        lin_free = [sem(f"lin_free{i}") for i in range(4)]
        misc_full = sem("misc_full")
        misc_free = [sem(f"misc_free{i}") for i in range(4)]
        x_in_s = sem("x_in_s")
        mem_in_s = sem("mem_in_s")
        mem2_in_s = sem("mem2_in_s")
        const_in = sem("const_in")
        row_in = sem("row_in")
        bias_out = sem("bias_out")
        bias_in = sem("bias_in")
        keys_in_s = sem("keys_in_s")
        gfin_in = sem("gfin_in")
        pool_in_s = sem("pool_in_s")
        alibi_in = sem("alibi_in")
        out_s = sem("out_s")
        dve_chain = sem("dve_chain")
        act_chain = sem("act_chain")
        pool_chain = sem("pool_chain")
        squares = sem("squares")
        mean_sq = sem("mean_sq")
        rstd_s = sem("rstd_s")
        root_ready = sem("root_ready")
        max_ready = sem("max_ready")
        exp_ready = sem("exp_ready")
        p_ready = sem("p_ready")
        lam_sums = sem("lam_sums")
        lam_exps = sem("lam_exps")
        sub_sq = sem("sub_sq")
        head_sq = sem("head_sq")
        ready = sem("ready")
        sub_roots = sem("sub_roots")
        top_chain = sem("top_chain")
        top_passed = sem("top_passed")
        top_exp_in = sem("top_exp_in")
        top_exp = sem("top_exp")
        experts_ready = sem("experts_ready")
        gathered = [sem(f"gathered{i}") for i in range(GSLOTS)]
        staged = sem("staged")
        issued = sem("issued")
        hidden_ready = sem("hidden_ready")
        peer_zero = sem("peer_zero")
        hf_ready = sem("hf_ready")
        dot_ready = sem("dot_ready")
        gelu_ready = sem("gelu_ready")
        wact_ready = sem("wact_ready")
        diag_ready = sem("diag_ready")
        row_free = sem("row_free")
        acc_ready = sem("acc_ready")
        acc_used = sem("acc_used")

        count = {}

        def chain(eng, ins, s):
            count[id(s)] = count.get(id(s), 0) + 1
            ins.then_inc(s, 1)
            eng.wait_ge(s, count[id(s)])

        token_rows = bank_pairs[1], bank_pairs[2]
        row_sums = bank_pairs[0], bank_pairs[3]

        def lin_bank(key):
            return banks[LIN[key] % 4]

        def misc_bank(key):
            return banks[4 + MISC[key] % 4]

        def wait_lin(eng, key):
            eng.wait_ge(half_done, LAST[key])

        def wait_misc(eng, key):
            eng.wait_ge(misc_full, MISC[key] + 1)

        def empty_lin(ins, key):
            ins.then_inc(lin_free[LIN[key] % 4], 1)

        def empty_misc(ins, key):
            ins.then_inc(misc_free[MISC[key] % 4], 1)

        def lin_emptied(eng, key):
            eng.wait_ge(lin_free[LIN[key] % 4], LIN[key] // 4 + 1)

        def misc_emptied(eng, key):
            eng.wait_ge(misc_free[MISC[key] % 4], MISC[key] // 4 + 1)

        def gain(name):
            a, n = VEC[name]
            return vecs[:, a:a + n]

        NORMS = ["mix", "mem", "mem2", "cross", "ffn", "final", "mixa", "mlpa", "mixb", "mlpb"]

        def stats(n):
            st = stat[:, NORMS.index(n) % 2, :]
            return st[:, 0:8].rearrange("p (t j) -> p t j", t=TB), st[:, 8:10], st[:, 10:12], st[:, 12:14]

        BY_BLOCK = ("cross", "ffn", "mlpa", "mixb", "mlpb")

        def squares_of(n):
            return sum(TB * (4 if m in BY_BLOCK else 1) for m in NORMS[:NORMS.index(n) + 1])

        def norm_pairs(n, k=0):
            return 4 * OPERANDS.index((n, k))

        IN_PSUM = ("cross", "mema", "swa", "memb")

        def seen_keys(kind, qb):
            return P * (qb + 1) if kind in ("diff", "swa") else S

        UNIT0, ITEM0 = {}, {}
        n_units = n_items = 0
        for kind, items, group in (("diff", HEADS, 2), ("cross", CROSS_HEADS, 1), ("mema", MEM_HEADS, 1),
                                   ("swa", SWA_HEADS, 1), ("memb", MEM_HEADS, 1)):
            UNIT0[kind], ITEM0[kind] = n_units, n_items
            n_units += items * group
            n_items += items

        POINTS = ["zeros", "kmem_a", "kmem_b", "h0", "h1", "d_pool", "mq", "slopes", "q0", "q1", "q2", "q3"]

        def at_point(ins, name):
            assert POINTS[count.setdefault("point", 0)] == name, name
            count["point"] += 1
            ins.then_inc(ready, 1)

        def point(eng, name):
            eng.wait_ge(ready, POINTS.index(name) + 1)

        block = ctx.enter_context(nc.Block())

        @block.sync
        def _(sp):
            def load(n, slot):
                sp.dma_start(raw[:, slot, :, :], wstream[n].rearrange("p (a b) -> p a b", a=KC))\
                  .then_inc(raw_in[slot], 16)

            sp.dma_start(x[:, :, :], x_in.rearrange("(t p) d -> p t d", p=P)).then_inc(x_in_s, 16)
            load(0, 0)
            sp.wait_ge(const_in, 48)
            for n in range(1, RAW):
                load(n, n)
            with sp.Fori(1, NHALF // RAW) as i:
                for slot in range(RAW):
                    sp.wait_ge(lo_ready, i * RAW + (slot + 1 - RAW))
                    sp.dma_start(raw[:, slot, :, :],
                                 wstream[bass.ds(i * RAW + slot, 1)].rearrange("o p (a b) -> p (o a) b", a=KC))\
                      .then_inc(raw_in[slot], 16)
            for n in range(NHALF - NHALF % RAW, NHALF):
                sp.wait_ge(lo_ready, n + 1 - RAW)
                load(n, n % RAW)
            for j in range(4):
                lin_emptied(sp, ("downb", j))
            sp.dma_start(out.rearrange("(t p) d -> p t d", p=P), x[:, :, :]).then_inc(out_s, 16)
            sp.wait_ge(out_s, 16)

        @block.gpsimd
        def _(pool):
            pool.memset(small[:, 14:16], -0.5).then_inc(pool_chain, 1)
            pool.wait_ge(pool_chain, 1)

            def rstd(n):
                _, _, ms, rs = stats(n)
                pool.wait_ge(mean_sq, NORMS.index(n) + 1)
                pool.tensor_tensor(rs, ms, small[:, 14:16], ALU.pow).then_inc(rstd_s, 1)

            halves = [0]

            def low_parts(upto):
                for n in range(halves[0], upto):
                    pool.wait_ge(hi_ready, n + 1)
                    if n >= LO:
                        pool.wait_ge(half_done, n - LO + 1)
                    pool.tensor_tensor(w_lo[:, n % LO, :, :], raw[:, n % RAW, :, :],
                                       w_hi[:, n % HI, :, :].bitcast(F32), ALU.subtract).then_inc(lo_ready, 1)
                halves[0] = upto

            for n, upto in (("mix", 0), ("mem", 33), ("mem2", 37), ("cross", 57), ("ffn", 65)):
                low_parts(upto)
                rstd(n)
            low_parts(72)
            for tb in range(TB):
                with pool.Fori(0, PH) as h:
                    pool.wait_ge(experts_ready, h + (tb * PH + 1))
                    for half in range(2):
                        turn = h * 2 + (half + tb * (PAIRS // GSLOTS))
                        pool.tensor_copy(stage[:, half, :],
                                         expert[:, tb, bass.ds(h * TOPK + half * GSLOTS, GSLOTS)])\
                            .then_inc(staged, 1)
                        pool.wait_ge(staged, turn + 1)
                        pool.sem_inc(issued, 1)
                        for s in range(GSLOTS):
                            pool.wait_ge(row_free, turn * GSLOTS + (s + 1))
                            pool.sem_inc(issued, 1)
                            pool.indirect_dma_start(
                                rows[:, s, :], None, experts,
                                bass.IndirectOffsetOnAxis(ap=stage[:, half, s:s + 1], axis=0))\
                                .then_inc(gathered[s], 16)
            for n, upto in (("final", 73), ("mixa", 73), ("mlpa", 81), ("mixb", 113), ("mlpb", 123)):
                low_parts(upto)
                rstd(n)
            low_parts(NHALF)

        @block.scalar
        def _(act):
            act.dma_start(consts[:, :], consts_in[:, 0:3 * P + TOPK]).then_inc(const_in, 16)
            act.dma_start(vecs[:, :], vecs_in).then_inc(const_in, 16)
            act.dma_start(bc[:, :], bass.AP(bc_in.tensor, 0, [[0, P], [1, NBC]])).then_inc(const_in, 16)
            act.dma_start(rel_sb, rel_in).then_inc(row_in, 16)
            act.dma_start(onehot, onehot_in).then_inc(row_in, 16)

            halves = [0]

            def high_parts(upto):
                for n in range(halves[0], min(upto, NHALF)):
                    act.wait_ge(raw_in[n % RAW], 16 * (n // RAW + 1))
                    if n >= HI:
                        act.wait_ge(half_done, n - HI + 1)
                    act.activation(w_hi[:, n % HI, :, :], raw[:, n % RAW, :, :], ACT.Copy).then_inc(hi_ready, 1)
                halves[0] = max(halves[0], upto)

            def product(key):
                high_parts(LAST[key] + 2)
                wait_lin(act, key)

            def sum_squares(n, src, row_ready=None):
                for tb in range(TB):
                    if row_ready:
                        row_ready(tb)
                    act.activation(xn[:, tb, :] if src is x else junk[:, 4 * tb:4 * tb + 4, :],
                                   src[:, tb, :] if src is x else src[:, tb, :].rearrange("p (a b) -> p a b", a=4),
                                   ACT.Square, accum_out=stats(n)[1][:, tb:tb + 1]).then_inc(squares, 1)

            def squares_and_rows(n, weight, buf):
                def high(j):
                    act.wait_ge(norm_rows, 2 * (norm_pairs(n) + j + 1))
                    act.activation(op_hi[:, buf, 2 * j:2 * j + 2, :], norm_t[:, 2 * j:2 * j + 2, :], ACT.Copy)\
                       .then_inc(norm_hi, 1)

                for j in range(4):
                    high_parts(LAST[(weight, j)] + 2)
                    lin_emptied(act, (weight, j))
                    if j == 3:
                        high(2)
                        high(3)
                    for tb in range(TB):
                        act.activation(junk[:, 4 * tb + j, :], x[:, tb, j * HW:(j + 1) * HW], ACT.Square,
                                       accum_out=stats(n)[0][:, tb, j:j + 1]).then_inc(squares, 1)
                    if j in (1, 2):
                        high(j - 1)
                high_parts(LAST[(weight, 3)] + HI)

            def roots_of(n):
                act.wait_ge(rstd_s, NORMS.index(n) + 1)
                return stats(n)[3]

            def sum_squares_of_sum(n, weight):
                for j in range(4):
                    high_parts(LAST[(weight, j)] + 2)
                    lin_emptied(act, (weight, j))
                    for tb in range(TB):
                        c = slice(j * HW, (j + 1) * HW)
                        act.activation(xn[:, tb, c], x[:, tb, c], ACT.Square,
                                       accum_out=stats(n)[0][:, tb, j:j + 1]).then_inc(squares, 1)
                high_parts(LAST[(weight, 3)] + HI)

            def xn_free(n):
                act.wait_ge(norm_lo, norm_pairs(n) + 4)

            def high_rows(n, buf, k=0):
                for j in range(4):
                    act.wait_ge(norm_rows, 2 * (norm_pairs(n, k) + j + 1))
                    act.activation(op_hi[:, buf, 2 * j:2 * j + 2, :], norm_t[:, 2 * j:2 * j + 2, :], ACT.Copy)\
                       .then_inc(norm_hi, 1)

            def exps(kind, u):
                g = UNIT0[kind] + u
                r = g % 4
                act.wait_ge(max_ready, g + 1)
                in_psum = kind in IN_PSUM
                src = misc_bank(("S", kind, u)).rearrange("p (a b) -> p a b", a=TB) if in_psum \
                    else prob[:, r]
                if kind == "swa":
                    h = SWA_ORDER[u]
                    sink = bc[:, 4 * HD + h:4 * HD + h + 1]
                    chain(act, act.activation(esink[:, r, :], nmax[:, r, :], ACT.Exp, bias=sink), act_chain)
                for qb in range(TB):
                    n = seen_keys(kind, qb)
                    scale = dict(scale=roots_of("cross")[:, qb:qb + 1]) if kind == "cross" else {}
                    e = act.activation(prob[:, r, qb, 0:n], src[:, qb, 0:n], ACT.Exp, **scale,
                                       bias=nmax[:, r, qb:qb + 1], accum_out=ssum[:, r, qb:qb + 1])
                    if in_psum and qb == TB - 1:
                        empty_misc(e, ("S", kind, u))
                    else:
                        e.then_inc(exp_ready, 1)

            def turned(kind, i):
                wait_misc(act, ("T", kind, i))
                if i >= 2:
                    wait_misc(act, ("O", kind, i - 2))
                n = S + seen_keys(kind, 0)
                e = act.activation(prob_t[:, (ITEM0[kind] + i) % 2, 0:n], misc_bank(("T", kind, i))[:, 0:n], ACT.Copy)
                empty_misc(e, ("T", kind, i))

            def free_prob(kind, i, group):
                j = i - 4 // group
                if j >= 0:
                    wait_misc(act, ("T", kind, j))

            def attention(kind, items, group, lag, fill=()):
                start = halves[0]
                for i in range(min(lag, items)):
                    for g in range(group):
                        exps(kind, i * group + g)
                for i in range(items):
                    if i + lag < items:
                        for g in range(group):
                            free_prob(kind, i + lag, group)
                            exps(kind, (i + lag) * group + g)
                    if i < len(fill):
                        high_parts(start + 2 * (i + 1))
                        if fill[i]:
                            fill[i]()
                    turned(kind, i)

            def copy_lin(key, dst, scale=None):
                product(key)
                src = lin_bank(key)
                if len(dst.shape) == 3:
                    src = src.rearrange("p (a b) -> p a b", a=2)
                e = act.activation(dst, src, ACT.Copy, scale=scale) if scale is not None \
                    else act.activation(dst, src, ACT.Copy)
                empty_lin(e, key)

            act.wait_ge(x_in_s, 16)
            sum_squares("mix", x)
            high_parts(1)
            high_rows("mix", 0)
            point(act, "zeros")
            for j in range(4):
                product(("q", j))
                src = lin_bank(("q", j)).rearrange("p (a b) -> p a b", a=2)
                chain(act, act.activation(q_half[0:HD, 0, 2 * j:2 * j + 2, :], src[0:HD], ACT.Copy,
                                          scale=HD ** -0.5), act_chain)
                e = act.activation(q_half[HD:P, 1, 2 * j:2 * j + 2, :], src[HD:P], ACT.Copy, scale=HD ** -0.5)
                empty_lin(e, ("q", j))
            misc_emptied(act, ("bias",))
            head = P * (2 * S + 1)
            act.dma_start(bass.AP(scratch.tensor, 0, [[head, HEADS], [2 * S + 1, P], [1, 2 * S]]),
                          bias_row.unsqueeze(1).broadcast_to([HEADS, P, 2 * S])).then_inc(bias_out, 16)
            for j in range(4):
                copy_lin(("k", j), k_diff[:, 2 * j:2 * j + 2, :])
            act.wait_ge(bias_out, 16)
            for qb in range(TB):
                act.dma_start(bias[:, :, qb, :], bass.AP(scratch.tensor, S - 1 - P * qb,
                                                         [[2 * S, P], [head, HEADS], [1, S]])).then_inc(bias_in, 16)
            for j in range(4):
                copy_lin(("v", j), v_diff[:, :, j * HW:(j + 1) * HW])
            for j in range(4):
                copy_lin(("cx", j), u_conv[:, 2 * j:2 * j + 2, :])
            xn_free("mix")
            act.dma_start(xn[:, :, :], mem_in.rearrange("(t p) d -> p t d", p=P)).then_inc(mem_in_s, 16)
            act.wait_ge(lam_sums, 2)
            act.activation(small[:, 2:4], small[:, 0:2], ACT.Exp).then_inc(lam_exps, 1)

            def gate(name, dst, i):
                def f():
                    for j in (2 * i, 2 * i + 1):
                        product((name, j))
                        e = act.activation(dst[:, 2 * j:2 * j + 2, :],
                                           lin_bank((name, j)).rearrange("p (a b) -> p a b", a=2),
                                           ACT.Exp, scale=-1.0)
                        empty_lin(e, (name, j))
                return f

            attention("diff", HEADS, 2, 1, [None] * 4 + [gate("gc", gate_c, 0), gate("gc", gate_c, 1),
                                                         gate("ga", gate_a, 0), gate("ga", gate_a, 1)])
            act.wait_ge(mem_in_s, 16)
            sum_squares("mem", xn)
            misc_emptied(act, ("O", "diff", HEADS - 1))
            act.activation(sq[:, :, :], o_diff[:, :, :], ACT.Square).then_inc(sub_sq, 1)
            high_rows("mem", 1)
            for j in range(4):
                wait_misc(act, ("sub", j))
                src = misc_bank(("sub", j)).rearrange("p (a b) -> p a b", a=2)
                t = slice(2 * j, 2 * j + 2)
                chain(act, act.activation(sq[:, t, :], src, ACT.Ln, bias=small[:, 8:9]), act_chain)
                empty_misc(act.activation(means[:, t, :], src, ACT.Identity, bias=small[:, 8:9]), ("sub", j))
            act.activation(sq[:, :, :], sq[:, :, :], ACT.Exp, scale=-0.5).then_inc(sub_roots, 1)
            xn_free("mem")
            act.dma_start(xn[:, :, :], mem2_in.rearrange("(t p) d -> p t d", p=P)).then_inc(mem2_in_s, 16)
            for j in range(4):
                copy_lin(("ck", j), k_cross[:, 2 * j:2 * j + 2, :])
            act.wait_ge(mem2_in_s, 16)
            act.wait_ge(squares, squares_of("mem"))
            sum_squares("mem2", xn)
            for j in range(4):
                copy_lin(("cv", j), v_cross[:, :, j * HW:(j + 1) * HW])
            high_rows("mem2", 0, 0)
            high_rows("mem2", 1, 1)
            for l in range(2):
                copy_lin(("mkv" + "ab"[l], 0), memk[:, l, :, :])
                copy_lin(("mkv" + "ab"[l], 1), memv[:, l, :, :])
            act.wait_ge(squares, squares_of("mem2"))
            for l in range(2):
                key = ("mkr", "ab"[l])
                lin_emptied(act, ("mkv" + "ab"[l], 0))
                act.activation(junk[:, 2 * l:2 * l + 2, :], memk[:, l, :, :], ACT.Square).then_inc(head_sq, 1)
                wait_misc(act, key)
                e = act.activation(junk[:, 4 + 2 * l:6 + 2 * l, :],
                                   misc_bank(key).rearrange("p (a b) -> p a b", a=2), ACT.Sqrt, bias=small[:, 9:10])
                empty_misc(e, key)
            xn_free("mem2")
            squares_and_rows("cross", "mixo", 1)
            for j in range(4):
                copy_lin(("cq", j), q_cross[:, 2 * j:2 * j + 2, :], scale=(D // CROSS_HEADS) ** -0.5)
            attention("cross", CROSS_HEADS, 1, 2)
            squares_and_rows("ffn", "co", 1)
            wait_misc(act, ("O", "cross", CROSS_HEADS - 1))
            act.dma_start(keys[:, :, :], keys_in.rearrange("p (a b) -> p a b", a=2 * PH)).then_inc(keys_in_s, 16)
            def top_exps(tb, h):
                act.wait_ge(top_exp_in, h + (tb * PH + 1))
                act.activation(top_e, top_less, ACT.Exp, accum_out=hsum).then_inc(top_exp, 1)

            def copy_scores(tb, j):
                wait_misc(act, ("sc", tb, j))
                e = act.activation(score[:, tb, 4 * j:4 * j + 4, :],
                                   misc_bank(("sc", tb, j)).rearrange("p (a b) -> p a b", a=4), ACT.Copy,
                                   scale=roots_of("ffn")[:, tb:tb + 1])
                empty_misc(e, ("sc", tb, j))

            for j in range(8):
                copy_lin(("pq", j), q_peer[:, 2 * j:2 * j + 2, :])
                if j == 1:
                    copy_scores(0, 0)
                if j in (3, 5):
                    top_exps(0, (j - 3) // 2)
            for tb in range(TB):
                for j in range(4):
                    if tb or j:
                        copy_scores(tb, j)
            act.sem_inc(gelu_ready, 1)

            def weigh_rows(tb, h):
                for j in range(0, TOPK, 2):
                    s = j % GSLOTS
                    done = h * TOPK + (tb * PAIRS + j)
                    act.wait_ge(dot_ready, done + 2)
                    act.activation(gact[:, s:s + 2], dots[:, s:s + 2], ACT.Gelu,
                                   scale=stats("ffn")[3][:, tb:tb + 1]).then_inc(gelu_ready, 1)
                    act.wait_ge(gelu_ready, h * (TOPK // 2) + (tb * (PAIRS // 2) + j // 2 + 2))
                    act.wait_ge(row_free, done + 2)
                    for k in range(2):
                        at = h * TOPK + (j + k)
                        act.activation(wact[:, s + k:s + k + 1], gact[:, s + k:s + k + 1], ACT.Copy,
                                       scale=weight[:, tb, at:at + 1] if isinstance(h, int) else
                                       weight[:, tb, bass.ds(at, 1)]).then_inc(wact_ready, 1)
                    act.wait_ge(wact_ready, done + 2)
                    for k in range(2):
                        act.activation(diag[:, s + k, :], ident, ACT.Copy, scale=wact[:, s + k:s + k + 1])\
                           .then_inc(diag_ready, 1)

            for tb in range(TB):
                with act.Fori(0, PH - AHEAD) as h:
                    weigh_rows(tb, h)
                    top_exps(tb, h + AHEAD)
                for h in range(AHEAD):
                    weigh_rows(tb, h + PH - AHEAD)
                    if tb < TB - 1:
                        top_exps(tb + 1, h)
                if tb == 0:
                    act.dma_start(gfin, bass.AP(final_g.tensor, 0, [[0, P], [1, D]])).then_inc(gfin_in, 16)
            act.wait_ge(acc_used, 4)
            sum_squares("final", x)
            act.dma_start(pool_w, pool_in.rearrange("p (a b) -> p a b", b=P)).then_inc(pool_in_s, 16)
            act.dma_start(cnt[:, :, :], cnt_in.rearrange("p (a b) -> p a b", a=SWA_TILES)).then_inc(pool_in_s, 16)
            act.wait_ge(squares, squares_of("final"))
            sum_squares("mixa", x, lambda tb: point(act, f"h{tb}"))
            high_rows("mixa", 0)

            def roots(key, dst):
                wait_misc(act, key)
                empty_misc(act.activation(dst, misc_bank(key).rearrange("p (a b) -> p a b", a=2), ACT.Sqrt,
                                          bias=small[:, 9:10]), key)

            def mlp(l):
                wt = "up" + l
                for j in range(16):
                    product((wt, j))
                    h = hidden[:, 2 * j:2 * j + 2, :]
                    empty_lin(act.activation(h, lin_bank((wt, j)).rearrange("p (a b) -> p a b", a=2), ACT.Relu),
                              (wt, j))
                    lin_emptied(act, (wt, j))
                    act.activation(h, h, ACT.Square).then_inc(hidden_ready, 1)

            for j in range(3):
                copy_lin(("ina", j), u_pool[:, 2 * j:2 * j + 2, :])
            copy_lin(("ina", 3), raw2[:, 6:8, :])
            lin_emptied(act, ("ina", 3))
            act.activation(sq2[:, 6:8, :], raw2[:, 6:8, :], ACT.Square).then_inc(head_sq, 1)
            wait_misc(act, ("mqr", "a"))
            e = act.activation(sq2[:, 0:2, :], misc_bank(("mqr", "a")).rearrange("p (a b) -> p a b", a=2),
                               ACT.Sqrt, bias=small[:, 9:10])
            empty_misc(e, ("mqr", "a"))
            attention("mema", MEM_HEADS, 1, 2)
            squares_and_rows("mlpa", "outa", 0)
            mlp("a")
            sum_squares_of_sum("mixb", "downa")
            high_rows("mixb", 1, 0)
            high_rows("mixb", 0, 1)
            act.dma_start(alibi[:, :, :], consts_in[:, 3 * P + TOPK:].rearrange("p (a b) -> p a b", a=TB))\
               .then_inc(alibi_in, 16)
            copy_lin(("kvb", 0), k_swa[:, :, :])
            copy_lin(("kvb", 1), v_swa[:, :, :])
            lin_emptied(act, ("kvb", 0))
            act.activation(sqk[:, 0:2, :], k_swa[:, :, :], ACT.Square).then_inc(head_sq, 1)
            roots(("kr",), sqk[:, 2:4, :])
            for j in range(4):
                d = raw2[:, 2 * j:2 * j + 2, :]
                copy_lin(("inb", j), d)
                lin_emptied(act, ("inb", j))
                act.activation(sq2[:, 2 * j:2 * j + 2, :], d, ACT.Square).then_inc(head_sq, 1)
                if j:
                    roots(("qr", j - 1), sq2[:, 2 * j - 2:2 * j, :])
            roots(("qr", 3), sq2[:, 6:8, :])
            attention("swa", SWA_HEADS, 1, 2)
            attention("memb", MEM_HEADS, 1, 2)
            squares_and_rows("mlpb", "outb", 0)
            mlp("b")
            high_parts(NHALF)

        @block.tensor
        def _(pe):
            state = {"half": 0, "misc": 0}

            def fill_misc(key):
                assert MISC[key] == state["misc"], key
                state["misc"] += 1
                j = MISC[key]
                if j >= 4:
                    pe.wait_ge(misc_free[j % 4], j // 4)
                return misc_bank(key)

            def lin_bank_free(key):
                j = LIN[key]
                if j >= 4:
                    pe.wait_ge(lin_free[j % 4], j // 4)

            def half_chunk(by_feature, src, hi_made=None, lo_made=None, first=True, last=True):
                n = state["half"]
                state["half"] += 1
                name = CHUNKS[n // 2]
                i = CHUNKS[:n // 2].count(name)
                key = (name, 2 * (i % 2 if name.startswith("down") else i) + n % 2)
                if first:
                    lin_bank_free(key)
                hi, lo = w_hi[:, n % HI, :, :], w_lo[:, n % LO, :, :]
                pe.wait_ge(hi_ready, n + 1)
                for r in range(2):
                    for turn, (w, a) in enumerate(((hi, op_hi), (lo, op_hi), (hi, op_lo))):
                        if r == 0 and turn == 1:
                            pe.wait_ge(lo_ready, n + 1)
                        for kc in range(KC):
                            if r == 0 and turn == 0 and hi_made:
                                hi_made(kc)
                            if r == 0 and turn == 2 and lo_made:
                                lo_made(kc)
                            part_, tokens_ = slice(r * P, (r + 1) * P), slice(r * HW, (r + 1) * HW)
                            start = turn == 0 and kc == 0 and first and (r == 0 or last)
                            stop = turn == 2 and kc == KC - 1 and last
                            l, m = (w[:, kc, part_], a[:, src, kc, :]) if by_feature \
                                else (a[:, src, kc, part_], w[:, kc, :])
                            mm = pe.matmul(lin_bank(key)[:, tokens_], l, m, start=start, stop=stop,
                                           skip_group_check=not (first and last))
                mm.then_inc(half_done, 1)

            def features(src, **k):
                for _ in range(2):
                    half_chunk(True, src, **k)

            def tokens(src, **k):
                for _ in range(2):
                    half_chunk(False, src, **k)

            def keys_values(src, **k):
                half_chunk(True, src, **k)
                half_chunk(False, src, **k)

            def split_made(name):
                def made(s):
                    return lambda kc: kc or pe.wait_ge(s, SPLITS.index(name) + 1)

                return dict(hi_made=made(split_hi), lo_made=made(split_lo))

            def turn_rows(n, j, src=x):
                b = fill_misc(("xT", n, j))
                for f in range(2):
                    for tb in range(TB):
                        at = (2 * j + f) * P
                        mm = pe.transpose(b[:, f * S + tb * P:f * S + (tb + 1) * P], src[:, tb, at:at + P], ident)
                mm.then_inc(misc_full, 1)

            def spread_roots(n):
                key = ("roots", n)
                lin_bank_free(key)
                for tb in range(TB):
                    pe.wait_ge(root_ready, TB * ROOTED.index(n) + tb + 1)
                    mm = pe.matmul(lin_bank(key)[:, tb * P:(tb + 1) * P], mean128, root_diag[:, tb, :],
                                   start=True, stop=True)
                mm.then_inc(roots_full, 1)

            def norm(n, src=x):
                for j in range(4):
                    turn_rows(n, j, src)
                spread_roots(n)

            def product_and_norm(src, weight, n, **k):
                for j in range(4):
                    half_chunk(False, src, **k)
                    k = {m: v for m, v in k.items() if m in ("first", "last")}
                    if j:
                        lin_emptied(pe, (weight, j - 1))
                        turn_rows(n, j - 1)
                lin_emptied(pe, (weight, 3))
                turn_rows(n, 3)
                if n in ROOTED:
                    spread_roots(n)

            def normed(n, k=0):
                def made(s):
                    return lambda kc: kc % 2 or pe.wait_ge(s, norm_pairs(n, k) + kc // 2 + 1)

                return dict(hi_made=made(norm_hi), lo_made=made(norm_lo))

            def attention(kind, items, group, lag, scores, values, fill=()):
                def s(u):
                    b = fill_misc(("S", kind, u))
                    for qb in range(TB):
                        pairs = scores(u, qb)
                        for n, (l, r) in enumerate(pairs):
                            seen = seen_keys(kind, qb)
                            mm = pe.matmul(b[:, qb * S:qb * S + seen], l, r[:, 0:seen], start=(n == 0),
                                           stop=(n == len(pairs) - 1))
                    mm.then_inc(misc_full, 1)

                def first_query(kb):
                    return kb if seen_keys(kind, 0) == P else 0

                def o(i):
                    misc_emptied(pe, ("T", kind, i))
                    b = fill_misc(("O", kind, i))
                    for e, part_ in enumerate(values(i)):
                        for kb in range(2):
                            q0 = first_query(kb) * P
                            mm = pe.matmul(b[:, e * S + q0:(e + 1) * S], part_(kb),
                                           prob_t[:, (ITEM0[kind] + i) % 2, kb * S:(kb + 1) * S - q0],
                                           start=(kb == 0), stop=(kb == 1))
                    mm.then_inc(misc_full, 1)

                for i in range(min(lag, items)):
                    for g in range(group):
                        s(i * group + g)
                for i in range(items):
                    if i + lag < items:
                        for g in range(group):
                            s((i + lag) * group + g)
                    if i < len(fill) and fill[i]:
                        fill[i]()
                    if i:
                        o(i - 1)
                    r = (UNIT0[kind] + i * group) % 4
                    pe.wait_ge(p_ready, TB * (ITEM0[kind] + i + 1))
                    b = fill_misc(("T", kind, i))
                    for kb in range(2):
                        for qb in range(first_query(kb), TB):
                            at = kb * S + (qb - first_query(kb)) * P
                            mm = pe.transpose(b[:, at:at + P], prob[:, r, qb, kb * P:(kb + 1) * P], ident)
                    mm.then_inc(misc_full, 1)
                o(items - 1)

            pe.wait_ge(const_in, 48)
            pe.wait_ge(x_in_s, 16)
            norm("mix")
            features(0, **normed("mix"))
            pe.wait_ge(row_in, 32)
            b = fill_misc(("bias",))
            pe.matmul(b[0:8, :], rel_sb, onehot, start=True, stop=True).then_inc(misc_full, 1)
            for _ in range(3):
                features(0)
            for _ in range(2):
                tokens(0)
            for _ in range(2):
                features(0)
            for j in range(4):
                lin_emptied(pe, ("q", j))
                lin_emptied(pe, ("k", j))
                lin_emptied(pe, ("v", j))
            attention("diff", HEADS, 2, 1,
                      lambda u, qb: [(q_half[:, u % 2, u // 2, qb * P:(qb + 1) * P], k_diff[:, u // 2, :])],
                      lambda h: [lambda kb: v_diff[:, kb, h * P:(h + 1) * P]],
                      [lambda: features(0)] * 8)
            pe.wait_ge(mem_in_s, 16)
            norm("mem", xn)
            pe.wait_ge(sub_sq, 1)
            for j in range(4):
                b = fill_misc(("sub", j))
                pe.matmul(b, mean128, sq[:, 2 * j:2 * j + 2, :], start=True, stop=True).then_inc(misc_full, 1)
            features(1, **normed("mem"))
            features(1)
            for _ in range(2):
                tokens(1)
            pe.wait_ge(mem2_in_s, 16)
            norm("mem2", xn)
            keys_values(0, **normed("mem2", 0))
            keys_values(1, **normed("mem2", 1))
            for l in range(2):
                pe.wait_ge(head_sq, l + 1)
                b = fill_misc(("mkr", "ab"[l]))
                pe.matmul(b, mean64, junk[:, 2 * l:2 * l + 2, :], start=True, stop=True).then_inc(misc_full, 1)
            for name, buf in (("u", 0), ("o", 1)):
                features(buf, **split_made(name))
                features(buf)
            product_and_norm(0, "mixo", "cross", **split_made("merged"))
            features(1, **normed("cross"))
            features(1)
            for j in range(4):
                lin_emptied(pe, ("ck", j))
                lin_emptied(pe, ("cv", j))
                lin_emptied(pe, ("cq", j))
            attention("cross", CROSS_HEADS, 1, 2,
                      lambda h, qb: [(q_cross[:, 2 * h + e, qb * P:(qb + 1) * P], k_cross[:, 2 * h + e, :])
                                     for e in range(2)],
                      lambda h: [lambda kb, e=e: v_cross[:, kb, (2 * h + e) * P:(2 * h + e + 1) * P]
                                 for e in range(2)])
            for h in range(CROSS_HEADS):
                misc_emptied(pe, ("O", "cross", h))
            product_and_norm(0, "co", "ffn")
            def scores_of_keys(tb, j):
                b = fill_misc(("sc", tb, j))
                for n in range(4):
                    mm = pe.matmul(b[:, n * P:(n + 1) * P], q_peer[:, 4 * j + n, tb * P:(tb + 1) * P],
                                   keys[:, 4 * j + n, :], start=True, stop=True)
                mm.then_inc(misc_full, 1)

            features(1, **normed("ffn"))
            features(1)
            for j in range(2):
                lin_emptied(pe, ("pq", j))
            pe.wait_ge(keys_in_s, 16)
            pe.sem_inc(row_free, EARLY_SLOTS)
            scores_of_keys(0, 0)
            for _ in range(2):
                features(1)
            for j in range(2, 8):
                lin_emptied(pe, ("pq", j))

            def token_rows_of(tb):
                for kc in range(KC):
                    for k, half in enumerate((op_hi, op_lo)):
                        mm = pe.matmul(token_rows[tb][:, kc // 4, kc % 4 * P:(kc % 4 + 1) * P],
                                       half[:, 1, kc, tb * P:(tb + 1) * P].bitcast(F32), ident,
                                       start=(k == 0), stop=(k == 1))
                mm.then_inc(hf_ready, 1)

            token_rows_of(0)
            for tb in range(TB):
                for j in range(4):
                    if tb or j:
                        scores_of_keys(tb, j)
            for j in range(4):
                misc_emptied(pe, ("sc", TB - 1, j))
            pe.wait_ge(peer_zero, 1)
            pe.sem_inc(row_free, GSLOTS - EARLY_SLOTS)
            token_rows_of(1)
            for tb in range(TB):
                sums = row_sums[tb]
                for n in range(2):
                    pe.matmul(sums[:, n, :], zeros, op_hi[:, 1, 0:2, :].bitcast(F32), start=True, stop=False,
                              skip_group_check=True)
                with pe.Fori(0, PAIRS // GSLOTS) as i:
                    for s in range(GSLOTS):
                        pe.wait_ge(diag_ready, i * GSLOTS + (tb * PAIRS + s + 1))
                        for n in range(2):
                            mm = pe.matmul(sums[:, n, :], diag[:, s, :], rows[:, s, D + n * CW:D + (n + 1) * CW],
                                           start=False, stop=False, skip_group_check=True)
                        mm.then_inc(row_free, 1)
                for n in range(2):
                    mm = pe.matmul(sums[:, n, :], zeros, op_hi[:, 1, 0:2, :].bitcast(F32), start=False, stop=True,
                                   skip_group_check=True)
                mm.then_inc(acc_ready, 1)

            def mlp(l, next_norm=None):
                features(0, **normed("mlp" + l))
                for _ in range(7):
                    features(0)
                for g in range(4):
                    k = dict(first=(g == 0), last=(g == 3))
                    if g == 3 and next_norm:
                        product_and_norm((g + 1) % 2, "down" + l, next_norm, **split_made(f"hidden{l}{g}"), **k)
                        continue
                    tokens((g + 1) % 2, **split_made(f"hidden{l}{g}"), **k)
                    tokens((g + 1) % 2, **k)

            point(pe, "h1")
            pe.wait_ge(acc_used, 4)
            norm("mixa")
            features(0, **normed("mixa"))
            features(0)
            def query_means_a():
                pe.wait_ge(head_sq, 3)
                b = fill_misc(("mqr", "a"))
                pe.matmul(b, mean64, sq2[:, 6:8, :], start=True, stop=True).then_inc(misc_full, 1)

            point(pe, "d_pool")
            pe.wait_ge(pool_in_s, 32)
            for g in range(2):
                for j in range(3):
                    b = fill_misc(("pool", g, j))
                    ins_ = [(n, a) for n, (a, o) in enumerate(POOL_BLOCKS) if o == j]
                    for n, (at, a) in enumerate(ins_):
                        mm = pe.matmul(b[:, 0:S], pool_w[:, 7 * g + at, :], win[:, 0, 3 * g + a, :],
                                       start=(n == 0), stop=(n == len(ins_) - 1))
                    mm.then_inc(misc_full, 1)
                if g == 0:
                    query_means_a()
            point(pe, "mq")
            point(pe, "kmem_b")
            attention("mema", MEM_HEADS, 1, 2,
                      lambda h, qb: [(mq_half[:, h % 2, h // 2, qb * P:(qb + 1) * P], memk[:, 0, h // 2, :])],
                      lambda h: [lambda kb: memv[:, 0, kb, (h // 2) * P:(h // 2 + 1) * P]])
            for h in range(MEM_HEADS):
                misc_emptied(pe, ("O", "mema", h))
            for g in range(2):
                for j in range(3):
                    misc_emptied(pe, ("pool", g, j))
            product_and_norm(1, "outa", "mlpa")
            mlp("a", "mixb")
            keys_values(1, **normed("mixb", 0))
            pe.wait_ge(head_sq, 4)
            b = fill_misc(("kr",))
            pe.matmul(b, mean64, sqk[:, 0:2, :], start=True, stop=True).then_inc(misc_full, 1)

            def query_means(j):
                pe.wait_ge(head_sq, 5 + j)
                b = fill_misc(("qr", j))
                pe.matmul(b, mean64, sq2[:, 2 * j:2 * j + 2, :], start=True, stop=True).then_inc(misc_full, 1)

            features(0, **normed("mixb", 1))
            query_means(0)
            half_chunk(True, 0)
            query_means(1)
            half_chunk(True, 0)
            query_means(2)
            query_means(3)
            lin_emptied(pe, ("kvb", 1))
            pe.wait_ge(alibi_in, 16)
            point(pe, "slopes")

            def swa_scores(u, qb):
                if qb == 0 and u % 4 == 0:
                    point(pe, f"q{u // 4}")
                return [(q_swa[:, u % 2, u // 2, qb * P:(qb + 1) * P], k_swa[:, u // 6, :]),
                        (slopes[:, u, :], alibi[:, qb, :])]

            attention("swa", SWA_HEADS, 1, 2,
                      swa_scores,
                      lambda u: [lambda kb: v_swa[:, kb, (u // 6) * P:(u // 6 + 1) * P]])
            point(pe, "q3")
            attention("memb", MEM_HEADS, 1, 2,
                      lambda h, qb: [(q_swa[:, h % 2, SWA_TILES + h // 2, qb * P:(qb + 1) * P],
                                      memk[:, 1, h // 2, :])],
                      lambda h: [lambda kb: memv[:, 1, kb, (h // 2) * P:(h // 2 + 1) * P]])
            for u in range(SWA_HEADS):
                misc_emptied(pe, ("O", "swa", u))
            for h in range(MEM_HEADS):
                misc_emptied(pe, ("O", "memb", h))
            product_and_norm(1, "outb", "mlpb")
            mlp("b")
            assert state["misc"] == len(MISC) and state["half"] == NHALF

        @block.vector
        def _(dve):
            def do(ins):
                chain(dve, ins, dve_chain)

            def signal(ins):
                count[id(dve_chain)] += 1
                ins.then_inc(dve_chain, 1)

            def signalled():
                dve.wait_ge(dve_chain, count[id(dve_chain)])

            def rows2(ap):
                return ap.rearrange("p (a b) -> p a b", a=2)

            def inverse_roots(n):
                parts, ss, ms, rs = stats(n)
                dve.wait_ge(squares, squares_of(n))
                if n in BY_BLOCK:
                    do(dve.tensor_reduce(ss, parts, AX.X, ALU.add))
                dve.tensor_scalar(ms, ss, 1.0 / D, 1e-6, ALU.mult, ALU.add).then_inc(mean_sq, 1)
                dve.wait_ge(rstd_s, NORMS.index(n) + 1)
                return rs

            def take_norm(n, dsts):
                rs = inverse_roots(n)
                for tb in range(TB):
                    dve.tensor_scalar(root_diag[:, tb, :], ident, rs[:, tb:tb + 1], float(P), ALU.mult, ALU.mult)\
                       .then_inc(root_ready, 1)
                for j in range(4):
                    wait_misc(dve, ("xT", n, j))
                dve.wait_ge(roots_full, ROOTED.index(n) + 1)
                empty_lin(dve.tensor_copy(root_rows, lin_bank(("roots", n))[:, 0:S]), ("roots", n))
                lin_emptied(dve, ("roots", n))
                for k, (g, buf) in enumerate(dsts):
                    made = norm_pairs(n, k)
                    if k:
                        dve.wait_ge(norm_lo, made)
                    for t in range(KC):
                        dve.scalar_tensor_tensor(norm_t[:, t, :],
                                                 misc_bank(("xT", n, t // 2))[:, t % 2 * S:(t % 2 + 1) * S],
                                                 gain(g)[:, t:t + 1], root_rows, ALU.mult, ALU.mult)\
                           .then_inc(norm_rows, 1)
                    for j in range(4):
                        t = slice(2 * j, 2 * j + 2)
                        dve.wait_ge(norm_hi, made + j + 1)
                        dve.tensor_tensor(op_lo[:, buf, t, :], norm_t[:, t, :], op_hi[:, buf, t, :].bitcast(F32),
                                          ALU.subtract).then_inc(norm_lo, 1)
                for j in range(4):
                    dve.sem_inc(misc_free[MISC["xT", n, j] % 4], 1)

            def split(name, src, buf, tiles=slice(0, KC), last=True):
                hi, lo = op_hi[:, buf, tiles, :], op_lo[:, buf, tiles, :]
                a = dve.tensor_copy(hi, src)
                if last:
                    assert SPLITS[count.setdefault("split", 0)] == name, name
                    count["split"] += 1
                    a.then_inc(split_hi, 1)
                    dve.wait_ge(split_hi, count["split"])
                    dve.tensor_tensor(lo, src, hi.bitcast(F32), ALU.subtract).then_inc(split_lo, 1)
                else:
                    do(a)
                    do(dve.tensor_tensor(lo, src, hi.bitcast(F32), ALU.subtract))

            def add_piece(weight, j, times=None):
                key = (weight, j)
                wait_lin(dve, key)
                c = slice(j * HW, (j + 1) * HW)
                if times is None:
                    empty_lin(dve.tensor_tensor(x[:, :, c], rows2(lin_bank(key)), x[:, :, c], ALU.add), key)
                    return
                for tb in range(TB):
                    ins = dve.scalar_tensor_tensor(x[:, tb, c], lin_bank(key)[:, tb * HW:(tb + 1) * HW],
                                                   times[:, tb:tb + 1], x[:, tb, c], ALU.mult, ALU.add)
                empty_lin(ins, key)

            def add_x(weight, times=None):
                for j in range(4):
                    add_piece(weight, j, times)

            def add_and_take(weight, n, g, buf):
                def rows_(j):
                    wait_misc(dve, ("xT", n, j))
                    for f in range(2):
                        t = 2 * j + f
                        dve.tensor_scalar(norm_t[:, t, :], misc_bank(("xT", n, j))[:, f * S:(f + 1) * S],
                                          gain(g)[:, t:t + 1], None, ALU.mult).then_inc(norm_rows, 1)

                def low(j):
                    t = slice(2 * j, 2 * j + 2)
                    dve.wait_ge(norm_hi, norm_pairs(n) + j + 1)
                    dve.tensor_tensor(op_lo[:, buf, t, :], norm_t[:, t, :], op_hi[:, buf, t, :].bitcast(F32),
                                      ALU.subtract).then_inc(norm_lo, 1)
                    dve.sem_inc(misc_free[MISC["xT", n, j] % 4], 1)

                add_piece(weight, 0)
                add_piece(weight, 1)
                rows_(0)
                add_piece(weight, 2)
                rows_(1)
                low(0)
                add_piece(weight, 3)
                rows_(2)
                rows_(3)
                for j in (1, 2, 3):
                    low(j)
                return inverse_roots(n)

            def maxima(kind, u, bias_ap=None, sink=None):
                g = UNIT0[kind] + u
                r = g % 4
                key = ("S", kind, u)
                wait_misc(dve, key)
                b = rows2(misc_bank(key))
                if bias_ap is not None:
                    for qb in range(TB):
                        n = seen_keys(kind, qb)
                        ins = dve.tensor_tensor(prob[:, r, qb, 0:n], b[:, qb, 0:n], bias_ap[:, qb, 0:n], ALU.add)
                    empty_misc(ins, key)
                    misc_emptied(dve, key)
                    b = prob[:, r]
                if seen_keys(kind, 0) == P:
                    for qb in range(TB):
                        ins = dve.tensor_reduce(nmax[:, r, qb:qb + 1], b[:, qb, 0:seen_keys(kind, qb)], AX.X,
                                                ALU.max, negate=(sink is None))
                else:
                    ins = dve.tensor_reduce(nmax[:, r, :], b, AX.X, ALU.max, negate=True)
                if kind == "cross":
                    do(ins)
                    ins = dve.tensor_tensor(nmax[:, r, :], nmax[:, r, :], stats("cross")[3], ALU.mult)
                if sink is None:
                    ins.then_inc(max_ready, 1)
                else:
                    do(ins)
                    dve.tensor_scalar(nmax[:, r, :], nmax[:, r, :], sink, -1.0, ALU.max, ALU.mult)\
                       .then_inc(max_ready, 1)

            def exps_done(kind, u):
                in_psum = kind in IN_PSUM
                n = 0
                for k in ("diff", "cross", "mema", "swa", "memb"):
                    per = 1 if k in IN_PSUM else 2
                    if k == kind:
                        n += per * (u + 1)
                        break
                    n += per * {"diff": 2 * HEADS, "cross": CROSS_HEADS, "mema": MEM_HEADS, "swa": SWA_HEADS}[k]
                dve.wait_ge(exp_ready, n)
                if in_psum:
                    misc_emptied(dve, ("S", kind, u))

            def normalise(kind, i):
                if kind == "diff":
                    ra, rb = (UNIT0[kind] + 2 * i) % 4, (UNIT0[kind] + 2 * i + 1) % 4
                    exps_done(kind, 2 * i + 1)
                    do(dve.reciprocal(rsum[:, ra:rb + 1, :], ssum[:, ra:rb + 1, :]))
                    do(dve.tensor_scalar(rsum[:, rb, :], rsum[:, rb, :], small[:, 6:7], None, ALU.mult))
                    for qb in range(TB):
                        n = seen_keys(kind, qb)
                        signal(dve.tensor_scalar(prob[:, rb, qb, 0:n], prob[:, rb, qb, 0:n],
                                                 rsum[:, rb, qb:qb + 1], None, ALU.mult))
                    signalled()
                    for qb in range(TB):
                        n = seen_keys(kind, qb)
                        dve.scalar_tensor_tensor(prob[:, ra, qb, 0:n], prob[:, ra, qb, 0:n],
                                                 rsum[:, ra, qb:qb + 1], prob[:, rb, qb, 0:n],
                                                 ALU.mult, ALU.add).then_inc(p_ready, 1)
                    return
                r = (UNIT0[kind] + i) % 4
                exps_done(kind, i)
                if kind == "swa":
                    do(dve.tensor_tensor(ssum[:, r, :], ssum[:, r, :], esink[:, r, :], ALU.add))
                do(dve.reciprocal(rsum[:, r, :], ssum[:, r, :]))
                for qb in range(TB):
                    n = seen_keys(kind, qb)
                    dve.tensor_scalar(prob[:, r, qb, 0:n], prob[:, r, qb, 0:n], rsum[:, r, qb:qb + 1], None,
                                      ALU.mult).then_inc(p_ready, 1)

            def attention(kind, items, group, lag, extra, dst, fill=()):
                for i in range(min(lag, items)):
                    for g in range(group):
                        maxima(kind, i * group + g, **extra(i * group + g))
                def take(i):
                    key = ("O", kind, i)
                    wait_misc(dve, key)
                    lo, hi, buf, d, w = dst(i)
                    src = misc_bank(key)[lo:hi, 0:w]
                    if w == 2 * S:
                        src = rows2(src)
                    if buf is None:
                        empty_misc(dve.tensor_copy(o_diff[:, d, :], src), key)
                        return
                    do(dve.tensor_copy(op_hi[lo:hi, buf, d, :], src))
                    empty_misc(dve.tensor_tensor(op_lo[lo:hi, buf, d, :], src,
                                                 op_hi[lo:hi, buf, d, :].bitcast(F32), ALU.subtract), key)

                for i in range(items):
                    normalise(kind, i)
                    if i + lag < items:
                        for g in range(group):
                            u = (i + lag) * group + g
                            j = i + lag - 4 // group
                            if j >= 0:
                                wait_misc(dve, ("T", kind, j))
                            maxima(kind, u, **extra(u))
                    if i < len(fill) and fill[i]:
                        fill[i]()
                    if i:
                        take(i - 1)
                take(items - 1)

            do(dve.memset(q_half[HD:P, 0, :, :], 0.0))
            do(dve.memset(q_half[0:HD, 1, :, :], 0.0))
            do(dve.memset(small[:, 8:9], 1e-5))
            at_point(dve.memset(small[:, 9:10], 1e-6), "zeros")
            dve.wait_ge(const_in, 48)
            for j in range(2):
                at = 2 * j * HD
                do(dve.tensor_tensor(bc[:, at:at + HD], bc[:, at:at + HD], bc[:, at + HD:at + 2 * HD], ALU.mult))
                dve.tensor_reduce(small[:, j:j + 1], bc[:, at:at + HD], AX.X, ALU.add).then_inc(lam_sums, 1)
            dve.wait_ge(x_in_s, 16)
            take_norm("mix", [("mix", 0)])
            wait_misc(dve, ("bias",))
            empty_misc(dve.tensor_copy(bias_row, misc_bank(("bias",))[0:8, :]), ("bias",))
            dve.wait_ge(lam_exps, 1)
            do(dve.tensor_tensor(small[:, 5:6], small[:, 3:4], small[:, 2:3], ALU.subtract))
            do(dve.tensor_scalar(small[:, 6:7], small[:, 5:6], -LAM_INIT, None, ALU.add))
            dve.wait_ge(bias_in, 32)

            def take_cc(i):
                def f():
                    for j in (2 * i, 2 * i + 1):
                        key = ("cc", j)
                        wait_lin(dve, key)
                        us = u_conv[:, 2 * j:2 * j + 2, :]
                        lin_emptied(dve, ("cx", j))
                        empty_lin(dve.tensor_tensor(us, rows2(lin_bank(key)), us, ALU.mult), key)
                        lin_emptied(dve, key)
                        for t in (2 * j, 2 * j + 1):
                            a = VEC["conv"][0]
                            do(dve.tensor_scalar(conv[:, t, :], u_conv[:, t, :], vecs[:, a + 16 + t:a + 17 + t],
                                                 None, ALU.mult))
                            for back in (1, 2):
                                w = vecs[:, a + 8 * (2 - back) + t:a + 8 * (2 - back) + t + 1]
                                do(dve.scalar_tensor_tensor(conv[:, t, back:S], u_conv[:, t, 0:S - back], w,
                                                            conv[:, t, back:S], ALU.mult, ALU.add))
                return f

            def take_cb(i):
                def f():
                    for j in (2 * i, 2 * i + 1):
                        key = ("cb", j)
                        wait_lin(dve, key)
                        cs = conv[:, 2 * j:2 * j + 2, :]
                        empty_lin(dve.tensor_tensor(u_conv[:, 2 * j:2 * j + 2, :], rows2(lin_bank(key)), cs,
                                                    ALU.mult), key)
                return f

            def sigmoid(name, dst, i):
                for j in (2 * i, 2 * i + 1):
                    lin_emptied(dve, (name, j))
                d = dst[:, 4 * i:4 * i + 4, :]
                do(dve.tensor_scalar(d, d, 1.0, None, ALU.add))
                do(dve.reciprocal(d, d))

            attention("diff", HEADS, 2, 1, lambda u: dict(bias_ap=bias[:, u // 2]),
                      lambda h: (0, P, None, h, S),
                      [take_cc(0), take_cc(1), take_cb(0), take_cb(1), None, None,
                       lambda: sigmoid("gc", gate_c, 0), lambda: sigmoid("gc", gate_c, 1)])
            for j in range(4):
                lin_emptied(dve, ("cb", j))
            do(dve.tensor_scalar(small[:, 7:8], gain("subln"), 1.0 - LAM_INIT, None, ALU.mult))
            dve.wait_ge(mem_in_s, 16)
            take_norm("mem", [("mem", 1)])
            for j in range(4):
                misc_emptied(dve, ("sub", j))
            dve.wait_ge(sub_roots, 1)
            t = scratch1[:, :, :]
            do(dve.tensor_tensor(t, sq[:, :, :], sq[:, :, :], ALU.mult))
            do(dve.tensor_tensor(t, t, means[:, :, :], ALU.mult))
            do(dve.tensor_scalar(t, t, -0.5, 1.5, ALU.mult, ALU.add))
            do(dve.tensor_tensor(sq[:, :, :], sq[:, :, :], t, ALU.mult))
            do(dve.scalar_tensor_tensor(o_diff[:, :, :], o_diff[:, :, :], small[:, 7:8], sq[:, :, :],
                                        ALU.mult, ALU.mult))
            dve.wait_ge(mem2_in_s, 16)
            sigmoid("ga", gate_a, 0)
            take_norm("mem2", [("mem2a", 0), ("mem2b", 1)])
            for name, src, buf, key in (("u", u_conv, 0, ("mkva", 1)), ("o", o_diff, 1, ("mkvb", 1))):
                wait_lin(dve, key)
                split(name, src[:, :, :], buf)
            for l in range(2):
                misc_emptied(dve, ("mkr", "ab"[l]))
                r = junk[:, 4 + 2 * l:6 + 2 * l, :]
                do(dve.reciprocal(r, r))
                at_point(dve.scalar_tensor_tensor(memk[:, l, :, :], memk[:, l, :, :], gain("mkn" + "ab"[l]), r,
                                                  ALU.mult, ALU.mult), "kmem_" + "ab"[l])
            sigmoid("ga", gate_a, 1)
            for j in range(4):
                key = ("cout", j)
                wait_lin(dve, key)
                g = gate_c[:, 2 * j:2 * j + 2, :]
                empty_lin(dve.tensor_tensor(g, rows2(lin_bank(key)), g, ALU.mult), key)
            for j in range(4):
                key = ("aout", j)
                wait_lin(dve, key)
                g = gate_a[:, 2 * j:2 * j + 2, :]
                empty_lin(dve.tensor_tensor(g, rows2(lin_bank(key)), g, ALU.mult), key)
                lin_emptied(dve, ("aout", j))
                lin_emptied(dve, ("cout", j))
                do(dve.tensor_tensor(g, g, gate_c[:, 2 * j:2 * j + 2, :], ALU.add))
                split("merged", g, 0, slice(2 * j, 2 * j + 2), last=(j == 3))
            add_and_take("mixo", "cross", "cross", 1)
            attention("cross", CROSS_HEADS, 1, 2, lambda u: {},
                      lambda h: (0, P, 0, slice(2 * h, 2 * h + 2), 2 * S))
            add_and_take("co", "ffn", "ffn", 1)
            dve.wait_ge(norm_lo, norm_pairs("ffn") + 4)
            dve.memset(zeros, 0.0).then_inc(peer_zero, 1)
            STEPS = 22

            def top_experts(tb, h):
                turn = h + tb * PH
                steps = [0]

                def step(ins):
                    steps[0] += 1
                    ins.then_inc(top_chain, 1)
                    dve.wait_ge(top_chain, turn * STEPS + steps[0])
                    dve.sem_inc(top_passed, 1)

                def at(ap, size):
                    return ap[:, tb, h * size:(h + 1) * size] if isinstance(h, int) \
                        else ap[:, tb, bass.ds(h * size, size)]

                src = score[:, tb, 2 * h:2 * h + 2, :] if isinstance(h, int) \
                    else score[:, tb, bass.ds(h * 2, 2), :]
                step(dve.tensor_copy(half_score, src))
                for r in range(2):
                    k0 = 8 * r
                    dve.max(half_vals[:, 0, k0:k0 + 8], half_score[:, 0, :])
                    step(dve.max(half_vals[:, 1, k0:k0 + 8], half_score[:, 1, :]))
                    dve.max_index(half_idx[:, 0, k0:k0 + 8], half_vals[:, 0, k0:k0 + 8], half_score[:, 0, :])
                    step(dve.max_index(half_idx[:, 1, k0:k0 + 8], half_vals[:, 1, k0:k0 + 8], half_score[:, 1, :]))
                    if r == 0:
                        dve.match_replace(half_score[:, 0, :], half_vals[:, 0, 0:8], half_score[:, 0, :], -3e38)
                        step(dve.match_replace(half_score[:, 1, :], half_vals[:, 1, 0:8], half_score[:, 1, :],
                                               -3e38))
                dve.tensor_copy(half_idxf, half_idx)
                step(dve.tensor_tensor(cand, half_vals[:, 0, :].unsqueeze(2).broadcast_to([P, TOPK, TOPK]),
                                       half_vals[:, 1, :].unsqueeze(1).broadcast_to([P, TOPK, TOPK]), ALU.add))
                flat = cand.rearrange("p a b -> p (a b)")
                for r in range(2):
                    k0 = 8 * r
                    step(dve.max(top_vals[:, k0:k0 + 8], flat))
                    step(dve.max_index(top_pos[:, k0:k0 + 8], top_vals[:, k0:k0 + 8], flat))
                    if r == 0:
                        step(dve.match_replace(flat, top_vals[:, 0:8], flat, -3e38))
                dve.tensor_scalar(top_less, top_vals, top_vals[:, 0:1], None, ALU.subtract).then_inc(top_exp_in, 1)
                dve.tensor_scalar(top_half[:, 0, :], top_pos, 4, None, ALU.logical_shift_right)
                step(dve.tensor_scalar(top_half[:, 1, :], top_pos, TOPK - 1, None, ALU.bitwise_and))
                step(dve.tensor_copy(top_halff, top_half))
                for c in range(2):
                    step(dve.tensor_tensor(pick, iota16.unsqueeze(1).broadcast_to([P, TOPK, TOPK]),
                                           top_halff[:, c, :].unsqueeze(2).broadcast_to([P, TOPK, TOPK]),
                                           ALU.is_equal))
                    step(dve.tensor_tensor(pick, pick,
                                           half_idxf[:, c, :].unsqueeze(1).broadcast_to([P, TOPK, TOPK]),
                                           ALU.mult))
                    step(dve.tensor_reduce(found[:, c, :], pick, AX.X, ALU.add))
                dve.scalar_tensor_tensor(at(expert, TOPK), found[:, 0, :], float(NKEYS), found[:, 1, :],
                                         ALU.mult, ALU.add).then_inc(experts_ready, 1)
                dve.wait_ge(top_exp, turn + 1)
                step(dve.reciprocal(hinv, hsum))
                step(dve.tensor_scalar(at(weight, TOPK), top_e, hinv, None, ALU.mult))
                assert steps[0] == STEPS, steps

            def dot_rows(tb, h):
                for j in range(TOPK):
                    s = j % GSLOTS
                    if s == 0:
                        dve.wait_ge(gelu_ready, h * (TOPK // 2) + (tb * (PAIRS // 2) + j // 2 + 1))
                    dve.wait_ge(gathered[s], h * 32 + (tb * (PAIRS // GSLOTS) + j // GSLOTS + 1) * 16)
                    u = rows[:, s, 0:D].rearrange("p (a b) -> p a b", a=2)
                    dve.tensor_tensor_reduce(u, u, token_rows[tb][:, :, :], 1.0, 0.0,
                                             ALU.mult, ALU.add, dots[:, s:s + 1]).then_inc(dot_ready, 1)

            misc_emptied(dve, ("sc", 0, 0))
            for h in range(AHEAD):
                top_experts(0, h)
            for j in range(1, 4):
                misc_emptied(dve, ("sc", 0, j))
            for tb in range(TB):
                dve.wait_ge(hf_ready, tb + 1)
                with dve.Fori(0, PH - AHEAD) as h:
                    dot_rows(tb, h)
                    top_experts(tb, h + AHEAD)
                if tb < TB - 1:
                    for j in range(4):
                        misc_emptied(dve, ("sc", tb + 1, j))
                for h in range(AHEAD):
                    dot_rows(tb, h + PH - AHEAD)
                    if tb < TB - 1:
                        top_experts(tb + 1, h)
                dve.wait_ge(acc_ready, tb + 1)
                for n in range(2):
                    xs = x[:, tb, n * CW:(n + 1) * CW]
                    dve.tensor_tensor(xs, row_sums[tb][:, n, :], xs, ALU.add).then_inc(acc_used, 1)
            dve.wait_ge(acc_used, 4)
            rs = inverse_roots("final")
            dve.wait_ge(gfin_in, 16)
            for tb in range(TB):
                at_point(dve.scalar_tensor_tensor(x[:, tb, :], x[:, tb, :], rs[:, tb:tb + 1], gfin,
                                                  ALU.mult, ALU.mult), f"h{tb}")
            take_norm("mixa", [("mixa", 0)])

            do(dve.memset(mq_half[HD:P, 0, :, :], 0.0))
            do(dve.memset(mq_half[0:HD, 1, :, :], 0.0))
            dve.wait_ge(pool_in_s, 32)
            w0, w1 = win[:, 0], win[:, 1]

            def window(dst, src, t, back):
                do(dve.tensor_copy(dst[:, t:t + 1, 0:back], src[:, t:t + 1, 0:back]))
                do(dve.tensor_tensor(dst[:, t:t + 1, back:S], src[:, t:t + 1, back:S], src[:, t:t + 1, 0:S - back],
                                     ALU.add))

            for t in range(SWA_TILES):
                if t % 2 == 0:
                    lin_emptied(dve, ("ina", t // 2))
                last = (t * P + P - 1) // POOL_GROUP
                sums = u_pool, w0, w1, w0, w1
                for level in range(last + 1):
                    window(sums[level + 1], sums[level], t, POOL_WINDOWS[level] // 2)
                for lo in (0, HD):
                    group = (t * P + lo) // POOL_GROUP
                    do(dve.tensor_tensor(w0[lo:lo + HD, t, :], sums[group + 1][lo:lo + HD, t, :],
                                         cnt[lo:lo + HD, t, :], ALU.mult))
                ins = dve.tensor_tensor(w0[:, t, :], w0[:, t, :], u_pool[:, t, :], ALU.subtract)
                at_point(ins, "d_pool") if t == SWA_TILES - 1 else do(ins)
            for g in range(2):
                if g:
                    misc_emptied(dve, ("mqr", "a"))
                    r = sq2[:, 0:2, :]
                    do(dve.reciprocal(r, r))
                    do(dve.tensor_scalar(small[:, 10:11], gain("mqna"), HD ** -0.5, None, ALU.mult))
                    do(dve.scalar_tensor_tensor(mq_half[0:HD, 0, :, :], raw2[0:HD, 6:8, :], small[0:HD, 10:11], r[0:HD],
                                                ALU.mult, ALU.mult))
                    at_point(dve.scalar_tensor_tensor(mq_half[HD:P, 1, :, :], raw2[HD:P, 6:8, :], small[HD:P, 10:11],
                                                      r[HD:P], ALU.mult, ALU.mult), "mq")
                for j in range(3):
                    key = ("pool", g, j)
                    wait_misc(dve, key)
                    t = 3 * g + j
                    do(dve.tensor_scalar(op_hi[:, 1, t, :], misc_bank(key)[:, 0:S], gain("pool")[:, t:t + 1], None,
                                         ALU.mult))
                    empty_misc(dve.scalar_tensor_tensor(op_lo[:, 1, t, :], misc_bank(key)[:, 0:S],
                                                        gain("pool")[:, t:t + 1],
                                                        op_hi[:, 1, t, :].bitcast(F32), ALU.mult, ALU.subtract),
                               key)

            def half_tile(t0):
                def f(h):
                    lo = HD * (h % 2)
                    return lo, lo + HD, 1, t0 + h // 2, S
                return f

            attention("mema", MEM_HEADS, 1, 2, lambda u: {}, half_tile(SWA_TILES))

            def slope_diagonals():
                for u, h in enumerate(SWA_ORDER):
                    slope = float(np.float32(2.0) ** np.float32(-8.0 * (h + 1) / SWA_HEADS))
                    ins = dve.tensor_scalar(slopes[:, u, :], ident, slope, None, ALU.mult)
                at_point(ins, "slopes")

            def mlp(l, beside=None):
                rs = add_and_take("out" + l, "mlp" + l, "mlp" + l, 0)
                do(dve.tensor_tensor(stats("mlp" + l)[1], rs, rs, ALU.mult))
                if beside:
                    beside()
                up_done = LAST[("up" + l, 15)]
                for g in range(4):
                    dve.wait_ge(hidden_ready, 16 * "ab".index(l) + 4 * (g + 1))
                    if g:
                        dve.wait_ge(half_done, up_done + (4 * (g - 1) if g > 1 else 0))
                    split(f"hidden{l}{g}", hidden[:, KC * g:KC * (g + 1), :], (g + 1) % 2)
                add_x("down" + l, stats("mlp" + l)[1])

            mlp("a", slope_diagonals)
            take_norm("mixb", [("kv", 1), ("mixb", 0)])
            do(dve.memset(q_swa[HD:P, 0, :, :], 0.0))
            do(dve.memset(q_swa[0:HD, 1, :, :], 0.0))
            misc_emptied(dve, ("kr",))
            do(dve.reciprocal(sqk[:, 2:4, :], sqk[:, 2:4, :]))
            do(dve.scalar_tensor_tensor(k_swa[:, :, :], k_swa[:, :, :], gain("kn"), sqk[:, 2:4, :], ALU.mult,
                                        ALU.mult))
            do(dve.tensor_scalar(small[:, 10:11], gain("qn"), HD ** -0.5, None, ALU.mult))
            do(dve.tensor_scalar(small[:, 11:12], gain("mqnb"), HD ** -0.5, None, ALU.mult))

            def take_queries(j):
                misc_emptied(dve, ("qr", j))
                t = slice(2 * j, 2 * j + 2)
                do(dve.reciprocal(sq2[:, t, :], sq2[:, t, :]))
                g = 10 if 2 * j < SWA_TILES else 11
                for c in range(2):
                    lo, hi = c * HD, (c + 1) * HD
                    ins = dve.scalar_tensor_tensor(q_swa[lo:hi, c, t, :], raw2[lo:hi, t, :], small[lo:hi, g:g + 1],
                                                   sq2[lo:hi, t, :], ALU.mult, ALU.mult)
                    at_point(ins, f"q{j}") if c else do(ins)

            take_queries(0)
            take_queries(1)

            def swa_extra(u):
                h = SWA_ORDER[u]
                return dict(sink=bc[:, 4 * HD + h:4 * HD + h + 1])

            attention("swa", SWA_HEADS, 1, 2, swa_extra, half_tile(0),
                      [lambda: take_queries(2), None, lambda: take_queries(3)])
            attention("memb", MEM_HEADS, 1, 2, lambda u: {}, half_tile(SWA_TILES))
            mlp("b")


def chunked(w):
    k, n = w.shape
    c = w.reshape(k // D, KC, P, n // HW, HW).transpose(3, 0, 2, 1, 4)
    order = [(j, g) for g in range(k // D) for j in range(n // HW)]
    return [c[j, g].reshape(P, KC * HW) for j, g in order]


def tiles(v):
    return v.reshape(-1, P).T


def layout(i):
    w_in = np.split(i["w_in"][0], 8, axis=1)
    cb, cc, cx, q, k, v, gc, ga = w_in
    ckv = i["w_ckv"][0]
    heads = np.concatenate([np.arange(h * HD, (h + 1) * HD) for h in SWA_ORDER])
    order = np.concatenate([heads, np.arange(SWA_HEADS * HD, D)])
    parts = {"q": q, "k": k, "v": v, "cx": cx, "cc": cc, "cb": cb, "gc": gc, "ga": ga,
             "ck": ckv[:, :D], "cv": ckv[:, D:], "cout": i["w_conv_out"][0], "aout": i["w_attn_out"][0],
             "mixo": i["w_mix_out"][0], "cq": i["w_cq"][0], "co": i["w_co"][0], "pq": i["w_pq"][0],
             "mkva": i["w_mem_kv_2"][0], "mkvb": i["w_mem_kv_2"][1], "kvb": i["w_kv_2"],
             "ina": i["w_in_2"][0], "inb": i["w_in_2"][1][:, order],
             "outa": i["w_out_2"][0], "outb": i["w_out_2"][1][order],
             "upa": i["w_up_2"][0], "upb": i["w_up_2"][1], "downa": i["w_down_2"][0], "downb": i["w_down_2"][1]}
    made = {name: chunked(w) for name, w in parts.items()}
    taken = {}
    stream = np.empty((NHALF, P, KC * HW), np.float32)
    for n in range(NHALF):
        c = CHUNKS[n // 2]
        stream[n] = made[c][taken.get(c, 0)]
        taken[c] = taken.get(c, 0) + 1

    def twice(g):
        return np.concatenate([g, g]).reshape(P, 1)

    columns = {"mix": tiles(i["norm_mix_g"][0]), "cross": tiles(i["norm_cross_g"][0]),
               "mem": tiles(i["norm_mem_g"][0]), "ffn": tiles(i["norm_ffn_g"][0]),
               "mixa": tiles(i["norm_mix_2"][0]), "mixb": tiles(i["norm_mix_2"][1]),
               "mlpa": tiles(i["norm_mlp_2"][0]), "mlpb": tiles(i["norm_mlp_2"][1]), "kv": tiles(i["kv_norm_2"]),
               "mem2a": tiles(i["mem_norm_2"][0]), "mem2b": tiles(i["mem_norm_2"][1]),
               "conv": tiles(i["conv_w"][0]), "subln": i["subln_g"][0].reshape(P, 1),
               "pool": tiles(i["pool_scale_2"][0]), "kn": twice(i["k_norm_2"]), "qn": twice(i["q_norm_2"][0]),
               "mqna": twice(i["mem_q_norm_2"][0]), "mqnb": twice(i["mem_q_norm_2"][1]),
               "mkna": twice(i["mem_k_norm_2"][0]), "mknb": twice(i["mem_k_norm_2"][1])}
    vecs = np.concatenate([columns[n] for n in VEC], axis=1)
    bc = np.concatenate([i["lambda_q1"][0], i["lambda_k1"][0], i["lambda_q2"][0], i["lambda_k2"][0],
                         i["sinks_2"][0]]).reshape(1, NBC)
    n = np.arange(S)
    big = np.maximum(n, 1).astype(np.float32)
    exact = BUCKETS // 2
    large = exact + (np.log(big / exact) / math.log(MAX_DISTANCE / exact) * (BUCKETS - exact)).astype(np.int32)
    bucket = np.where(n < exact, n, np.minimum(large, BUCKETS - 1))
    onehot = np.zeros((BUCKETS + 1, 2 * S), np.float32)
    onehot[bucket[::-1], n] = 1.0
    onehot[BUCKETS, S:] = 1.0
    rel = np.concatenate([i["rel_bias"], np.full((1, HEADS), MASKED, np.float32)])
    pos = np.arange(P)
    dist = P * np.arange(TB)[None, :, None] + pos[:, None, None] - n[None, None, :]
    alibi = np.where((dist >= 0) & (dist < P), -dist, -1e36).astype(np.float32)
    same = (pos[:, None] // HD == pos[None, :] // HD)
    consts = np.concatenate([np.eye(P), np.full((P, P), 1.0 / P), same / HD,
                             np.tile(np.arange(TOPK), (P, 1)), alibi.reshape(P, -1)], axis=1).astype(np.float32)
    window = np.repeat(np.array(POOL_WINDOWS), POOL_GROUP)
    cnt = 1.0 / np.minimum(n[None, :] + 1, window[:, None])
    cnt = cnt.reshape(SWA_TILES, P, S).transpose(1, 0, 2).reshape(P, -1).astype(np.float32)
    pool_w = np.zeros((2, 2 * POOL_GROUP, 2 * POOL_GROUP), np.float32)
    for g in range(len(POOL_WINDOWS)):
        a = g % 2 * POOL_GROUP
        pool_w[g // 2, a:a + POOL_GROUP, a:a + POOL_GROUP] = i["pool_w_2"][0, g]
    pool_w = np.concatenate([pool_w[g, a * P:(a + 1) * P, o * P:(o + 1) * P]
                             for g in range(2) for a, o in POOL_BLOCKS], axis=1)
    keys = i["sub_keys"][0].transpose(3, 1, 0, 2).reshape(P, -1)
    return dict(x_in=i["x"][0], mem_in=i["mem"][0], mem2_in=i["mem_2"][0], wstream=stream,
                experts=np.concatenate([i["peer_u"][0], i["peer_v"][0]], axis=1), vecs_in=vecs, bc_in=bc,
                final_g=i["final_g"].reshape(1, D), rel_in=rel, keys_in=keys, pool_in=pool_w,
                consts_in=consts, onehot_in=onehot, cnt_in=cnt)


def kernel(**inputs):
    import concourse.bacc as bacc
    from concourse.bass_utils import run_bass_kernel_spmd

    nc = bacc.Bacc("TRN2", target_bir_lowering=False, num_devices=1)
    arrays, args = {}, {}
    for name, a in layout({k: np.asarray(v) for k, v in inputs.items()}).items():
        arrays[name] = np.ascontiguousarray(a)
        args[name] = nc.dram_tensor(name, a.shape, F32, kind="ExternalInput").ap()
    args["scratch"] = nc.dram_tensor("scratch", (HEADS, P * (2 * S + 1)), F32, kind="Internal").ap()
    args["out"] = nc.dram_tensor("out_dram", (S, D), F32, kind="ExternalOutput").ap()
    build(nc, **args)
    r = run_bass_kernel_spmd(nc, [arrays], core_ids=[0])
    return r.results[0]["out_dram"].reshape(1, S, D)
```
